# Optimizing a Trainium2 kernel written in Bass

```python
import math
import jax
import jax.numpy as jnp
from jax import lax
import numpy as np

D_MODEL = 2048
BATCH = 1
SEQ = 256
DEPTH = 2
DEC_BATCH = 8
DEC_SEQ = 8
PAST_LEN = 2048
PAGE_SIZE = 128

HEAD_DIM = 64
A_DIM = D_MODEL // 4
B_DIM = D_MODEL // 4
C_DIM = D_MODEL // 2
A_HEADS = A_DIM // HEAD_DIM
B_HEADS = B_DIM // HEAD_DIM
C_Q_HEADS = C_DIM // HEAD_DIM
C_KV_HEADS = 2
C_GROUP = C_Q_HEADS // C_KV_HEADS
MIX_DIM = A_DIM + B_DIM + C_DIM
C_KV_DIM = C_KV_HEADS * HEAD_DIM
A_BRANCHES = ((128, 1), (512, 4), (2048, 16))
A_MAX_WINDOW = 2048
C_WINDOW = 128
BLOCK = 128
ROPE_THETA = 500000.0
ROPE_DIM = HEAD_DIM // 4
B_DECAY_LORA = 96
B_AAA_LORA = 96
B_GATE_LORA = 64
B_COLS = 3 * B_DIM + B_DECAY_LORA + B_AAA_LORA + B_GATE_LORA
IN_COLS = 3 * A_DIM + B_COLS + C_DIM + 2 * C_KV_DIM
IN_SPLITS = (A_DIM, 2 * A_DIM, 3 * A_DIM, 3 * A_DIM + B_COLS, 3 * A_DIM + B_COLS + C_DIM, 3 * A_DIM + B_COLS + C_DIM + C_KV_DIM)
B_SPLITS = (B_DIM, 2 * B_DIM, 3 * B_DIM, 3 * B_DIM + B_DECAY_LORA, 3 * B_DIM + B_DECAY_LORA + B_AAA_LORA)
D_FF = -(-8 * D_MODEL // (3 * 256)) * 256
RMS_EPS = 1e-6
GN_EPS = 64e-5
ATTN_SCALE = HEAD_DIM ** -0.5

kernel_name = 'hybrid_dilated_rwkv7_swa_decoder_step'

def rms_norm(x, g):
    xf = x.astype(jnp.float32)
    y = xf * lax.rsqrt(jnp.mean(xf * xf, axis=-1, keepdims=True) + RMS_EPS)
    return (y * g.astype(jnp.float32)).astype(x.dtype)

def rope_partial(x, pos):
    half = ROPE_DIM // 2
    inv = jnp.exp(-math.log(ROPE_THETA) * jnp.arange(half, dtype=jnp.float32) * 2.0 / ROPE_DIM)
    ang = pos.astype(jnp.float32)[:, None] * inv[None, :]
    shp = (ang.shape[0],) + (1,) * (x.ndim - 3) + (half,)
    cos = jnp.cos(ang).reshape(shp).astype(x.dtype)
    sin = jnp.sin(ang).reshape(shp).astype(x.dtype)
    x1 = x[..., :half]
    x2 = x[..., half:ROPE_DIM]
    return jnp.concatenate([x1 * cos - x2 * sin, x2 * cos + x1 * sin, x[..., ROPE_DIM:]], axis=-1)

def band_attention(q, k, v, window):
    B, L, Hk, G, hd = q.shape
    Lp = -(-L // BLOCK) * BLOCK
    pad = Lp - L
    if pad:
        q = jnp.pad(q, [(0, 0), (0, pad), (0, 0), (0, 0), (0, 0)])
        k = jnp.pad(k, [(0, 0), (0, pad), (0, 0), (0, 0)])
        v = jnp.pad(v, [(0, 0), (0, pad), (0, 0), (0, 0)])
    nb = Lp // BLOCK
    qb = q.reshape(B, nb, BLOCK, Hk, G, hd)
    kb = k.reshape(B, nb, BLOCK, Hk, hd)
    vb = v.reshape(B, nb, BLOCK, Hk, hd)
    k2 = jnp.concatenate([jnp.concatenate([jnp.zeros_like(kb[:, :1]), kb[:, :-1]], axis=1), kb], axis=2)
    v2 = jnp.concatenate([jnp.concatenate([jnp.zeros_like(vb[:, :1]), vb[:, :-1]], axis=1), vb], axis=2)
    s = jnp.einsum('bnqhgd,bnkhd->bnhgqk', qb, k2, preferred_element_type=jnp.float32) * ATTN_SCALE
    kpos = jnp.arange(2 * BLOCK)
    dist = (jnp.arange(BLOCK) + BLOCK)[:, None] - kpos[None, :]
    band = (dist >= 0) & (dist <= window)
    has_prev = (jnp.arange(nb)[:, None, None] > 0) | (kpos[None, None, :] >= BLOCK)
    mask = band[None] & has_prev
    s = jnp.where(mask[None, :, None, None], s, -jnp.inf)
    lse = jax.nn.logsumexp(s, axis=-1)
    p = jnp.exp(s - lse[..., None]).astype(v.dtype)
    o = jnp.einsum('bnhgqk,bnkhd->bnqhgd', p, v2).reshape(B, Lp, Hk, G, hd)[:, :L]
    lse = lse.transpose(0, 1, 4, 2, 3).reshape(B, Lp, Hk, G)[:, :L]
    return o, lse

def combine_branches(outs, lses):
    wts = jax.nn.softmax(jnp.stack(lses, axis=0), axis=0)
    o = jnp.stack(outs, axis=0).astype(jnp.float32)
    return jnp.sum(wts[..., None] * o, axis=0).astype(outs[0].dtype)

def dilated_attention_prompt(q, k, v):
    B, L, H, hd = q.shape
    outs, lses = [], []
    for window, dil in A_BRANCHES:
        Ls = L // dil

        def to_sub(t):
            return t.reshape(B, Ls, dil, H, hd).transpose(0, 2, 1, 3, 4).reshape(B * dil, Ls, H, hd)

        o, lse = band_attention(to_sub(q)[:, :, :, None, :], to_sub(k), to_sub(v), window // dil)
        outs.append(o[:, :, :, 0].reshape(B, dil, Ls, H, hd).transpose(0, 2, 1, 3, 4).reshape(B, L, H, hd))
        lses.append(lse[..., 0].reshape(B, dil, Ls, H).transpose(0, 2, 1, 3).reshape(B, L, H))
    return combine_branches(outs, lses)

def dilated_attention_sample(q, k_all, v_all, n_buf):
    T = q.shape[1]
    qi = n_buf + jnp.arange(T)
    outs, lses = [], []
    for window, dil in A_BRANCHES:
        n_keys = window // dil + 1
        idx = qi[:, None] - dil * jnp.arange(n_keys)[None, :]
        valid = idx >= 0
        idx = jnp.maximum(idx, 0)
        kg = k_all[:, idx]
        vg = v_all[:, idx]
        s = jnp.einsum('bthd,btjhd->bthj', q, kg, preferred_element_type=jnp.float32) * ATTN_SCALE
        s = jnp.where(valid[None, :, None, :], s, -jnp.inf)
        lse = jax.nn.logsumexp(s, axis=-1)
        p = jnp.exp(s - lse[..., None]).astype(vg.dtype)
        outs.append(jnp.einsum('bthj,btjhd->bthd', p, vg))
        lses.append(lse)
    return combine_branches(outs, lses)

def apply_sink(o, lse, sink):
    scale = jax.nn.sigmoid(lse - sink.astype(jnp.float32))
    return (o.astype(jnp.float32) * scale[..., None]).astype(o.dtype)

def window_attention_prompt(q, k, v, sink):
    o, lse = band_attention(q, k, v, C_WINDOW)
    return apply_sink(o, lse, sink)

def window_attention_sample(q, k_all, v_all, n_buf, sink):
    T = q.shape[1]
    M = k_all.shape[1]
    dist = (n_buf + jnp.arange(T))[:, None] - jnp.arange(M)[None, :]
    mask = (dist >= 0) & (dist <= C_WINDOW)
    s = jnp.einsum('bthgd,bmhd->bhgtm', q, k_all, preferred_element_type=jnp.float32) * ATTN_SCALE
    s = jnp.where(mask, s, -jnp.inf)
    lse = jax.nn.logsumexp(s, axis=-1)
    p = jnp.exp(s - lse[..., None]).astype(v_all.dtype)
    o = jnp.einsum('bhgtm,bmhd->bthgd', p, v_all)
    return apply_sink(o, lse.transpose(0, 3, 1, 2), sink)

def rwkv7_time_mix(pb, pb_prev, s0, mu, w0, w2, a0, a2, g2, k_k, k_a, r_k, lnx_w, lnx_b):
    f32 = jnp.float32
    B, L, _ = pb.shape
    p = pb.astype(f32)
    shifted = jnp.concatenate([pb_prev.astype(f32)[:, None], p[:, :-1]], axis=1)
    p = p + (shifted - p) * mu.astype(f32)
    r, k, v, wl, al, gl = jnp.split(p, B_SPLITS, axis=-1)
    w = -jax.nn.softplus(-(w0.astype(f32) + jnp.tanh(wl) @ w2.astype(f32))) - 0.5
    decay = jnp.exp(-jnp.exp(w))
    a = jax.nn.sigmoid(a0.astype(f32) + al @ a2.astype(f32))
    g = jax.nn.sigmoid(gl) @ g2.astype(f32)

    def heads(t):
        return t.reshape(B, L, B_HEADS, HEAD_DIM)

    kk = heads(k * k_k.astype(f32))
    kk = kk / jnp.maximum(jnp.sqrt(jnp.sum(kk * kk, axis=-1, keepdims=True)), 1e-12)
    k = k * (1.0 + (a - 1.0) * k_a.astype(f32))
    r_h, k_h, v_h, d_h, a_h = heads(r), heads(k), heads(v), heads(decay), heads(a)
    b_h = kk * a_h

    def step(S, inp):
        r_t, d_t, k_t, v_t, kk_t, b_t = inp
        sa = jnp.einsum('bhij,bhj->bhi', S, -kk_t)
        S = S * d_t[:, :, None, :] + sa[..., None] * b_t[:, :, None, :] + v_t[..., None] * k_t[:, :, None, :]
        return S, jnp.einsum('bhij,bhj->bhi', S, r_t)

    xs = tuple(jnp.moveaxis(t, 1, 0) for t in (r_h, d_h, k_h, v_h, kk, b_h))
    S, y = lax.scan(step, s0.astype(f32), xs)
    y = jnp.moveaxis(y, 0, 1)
    mean = jnp.mean(y, axis=-1, keepdims=True)
    var = jnp.mean(jnp.square(y - mean), axis=-1, keepdims=True)
    y = ((y - mean) * lax.rsqrt(var + GN_EPS)).reshape(B, L, B_DIM) * lnx_w.astype(f32) + lnx_b.astype(f32)
    bonus = jnp.sum(r_h * k_h * r_k.astype(f32).reshape(B_HEADS, HEAD_DIM), axis=-1, keepdims=True) * v_h
    y = (y + bonus.reshape(B, L, B_DIM)) * g
    return y.astype(pb.dtype), S.astype(pb.dtype), pb[:, -1]

def trunk_layer(x, pos, lw, past):
    (g_mix, w_in, w_out, mu, w0, w2, a0, a2, g2, k_k, k_a, r_k, lnx_w, lnx_b,
     sink, g_ffn, w_gate, w_up, w_down) = lw
    nb, L, _ = x.shape
    h = rms_norm(x, g_mix)
    p = h @ w_in
    qa, ka, va, pb, qc, kc, vc = jnp.split(p, IN_SPLITS, axis=-1)
    qa = rope_partial(qa.reshape(nb, L, A_HEADS, HEAD_DIM), pos)
    ka = rope_partial(ka.reshape(nb, L, A_HEADS, HEAD_DIM), pos)
    va = va.reshape(nb, L, A_HEADS, HEAD_DIM)
    qc = rope_partial(qc.reshape(nb, L, C_KV_HEADS, C_GROUP, HEAD_DIM), pos)
    kc = rope_partial(kc.reshape(nb, L, C_KV_HEADS, HEAD_DIM), pos)
    vc = vc.reshape(nb, L, C_KV_HEADS, HEAD_DIM)
    rwkv_w = (mu, w0, w2, a0, a2, g2, k_k, k_a, r_k, lnx_w, lnx_b)
    if past is None:
        oa = dilated_attention_prompt(qa, ka, va)
        oc = window_attention_prompt(qc, kc, vc, sink)
        ob, wkv, shift = rwkv7_time_mix(pb, jnp.zeros((nb, B_COLS), p.dtype),
                                        jnp.zeros((nb, B_HEADS, HEAD_DIM, HEAD_DIM), jnp.float32), *rwkv_w)
        a_keep = min(A_MAX_WINDOW, L)
        c_keep = min(C_WINDOW, L)
        new = (ka[:, L - a_keep:], va[:, L - a_keep:], kc[:, L - c_keep:], vc[:, L - c_keep:], wkv, shift)
    else:
        a_k_buf, a_v_buf, c_k_buf, c_v_buf, wkv0, shift0 = past
        oa = dilated_attention_sample(qa, jnp.concatenate([a_k_buf.astype(ka.dtype), ka], axis=1),
                                      jnp.concatenate([a_v_buf.astype(va.dtype), va], axis=1), a_k_buf.shape[1])
        oc = window_attention_sample(qc, jnp.concatenate([c_k_buf.astype(kc.dtype), kc], axis=1),
                                     jnp.concatenate([c_v_buf.astype(vc.dtype), vc], axis=1), c_k_buf.shape[1], sink)
        ob, wkv, shift = rwkv7_time_mix(pb, shift0, wkv0, *rwkv_w)
        new = (ka, va, kc, vc, wkv, shift)
    mixed = jnp.concatenate([oa.reshape(nb, L, A_DIM), ob, oc.reshape(nb, L, C_DIM)], axis=-1)
    x = x + mixed @ w_out
    h = rms_norm(x, g_ffn)
    x = x + (jax.nn.silu(h @ w_gate) * (h @ w_up)) @ w_down
    return x, new

def setup_inputs(seed: int = 0) -> dict:
    key = jax.random.key(seed)
    ks = jax.random.split(key, 32)
    f32 = jnp.float32
    a_win = min(A_MAX_WINDOW, PAST_LEN)
    c_win = min(C_WINDOW, PAST_LEN)

    def nrm(k, shape, scale):
        return jax.random.normal(k, shape, f32) * scale

    return {
        'x_prompt': nrm(ks[0], (BATCH, SEQ, D_MODEL), 1.0),
        'x_sample': nrm(ks[1], (DEC_BATCH, DEC_SEQ, D_MODEL), 1.0),
        'cache_a_k': nrm(ks[2], (DEPTH, DEC_BATCH, a_win, A_HEADS, HEAD_DIM), 1.0),
        'cache_a_v': nrm(ks[3], (DEPTH, DEC_BATCH, a_win, A_HEADS, HEAD_DIM), 1.0),
        'cache_c_k': nrm(ks[4], (DEPTH, DEC_BATCH, c_win, C_KV_HEADS, HEAD_DIM), 1.0),
        'cache_c_v': nrm(ks[5], (DEPTH, DEC_BATCH, c_win, C_KV_HEADS, HEAD_DIM), 1.0),
        'state_b_wkv': nrm(ks[6], (DEPTH, DEC_BATCH, B_HEADS, HEAD_DIM, HEAD_DIM), 0.3),
        'state_b_shift': nrm(ks[7], (DEPTH, DEC_BATCH, B_COLS), 1.0),
        'g_mix': 1.0 + nrm(ks[8], (DEPTH, D_MODEL), 0.02),
        'w_in': nrm(ks[9], (DEPTH, D_MODEL, IN_COLS), D_MODEL ** -0.5),
        'w_out': nrm(ks[10], (DEPTH, MIX_DIM, D_MODEL), 0.5 * MIX_DIM ** -0.5),
        'b_mu': jax.random.uniform(ks[11], (DEPTH, B_COLS), f32, 0.0, 1.0),
        'b_w0': jax.random.uniform(ks[12], (DEPTH, B_DIM), f32, -6.0, -1.0),
        'b_w2': nrm(ks[13], (DEPTH, B_DECAY_LORA, B_DIM), 0.1),
        'b_a0': nrm(ks[14], (DEPTH, B_DIM), 0.1),
        'b_a2': nrm(ks[15], (DEPTH, B_AAA_LORA, B_DIM), 0.1),
        'b_g2': nrm(ks[16], (DEPTH, B_GATE_LORA, B_DIM), B_GATE_LORA ** -0.5),
        'b_k_k': 0.85 + nrm(ks[17], (DEPTH, B_DIM), 0.05),
        'b_k_a': 1.0 + nrm(ks[18], (DEPTH, B_DIM), 0.05),
        'b_r_k': nrm(ks[19], (DEPTH, B_DIM), 0.1),
        'b_lnx_w': 1.0 + nrm(ks[20], (DEPTH, B_DIM), 0.02),
        'b_lnx_b': nrm(ks[21], (DEPTH, B_DIM), 0.02),
        'c_sink': nrm(ks[22], (DEPTH, C_KV_HEADS, C_GROUP), 1.0),
        'g_ffn': 1.0 + nrm(ks[23], (DEPTH, D_MODEL), 0.02),
        'w_gate': nrm(ks[24], (DEPTH, D_MODEL, D_FF), D_MODEL ** -0.5),
        'w_up': nrm(ks[25], (DEPTH, D_MODEL, D_FF), D_MODEL ** -0.5),
        'w_down': nrm(ks[26], (DEPTH, D_FF, D_MODEL), 0.5 * D_FF ** -0.5),
        'g_final': 1.0 + nrm(ks[27], (D_MODEL,), 0.02),
    }

def reference(x_prompt, x_sample, cache_a_k, cache_a_v, cache_c_k, cache_c_v, state_b_wkv, state_b_shift,
              g_mix, w_in, w_out, b_mu, b_w0, b_w2, b_a0, b_a2, b_g2, b_k_k, b_k_a, b_r_k, b_lnx_w, b_lnx_b,
              c_sink, g_ffn, w_gate, w_up, w_down, g_final):
    pos_p = jnp.arange(x_prompt.shape[1], dtype=jnp.int32)
    pos_s = PAST_LEN + jnp.arange(x_sample.shape[1], dtype=jnp.int32)
    hp, hs = x_prompt, x_sample
    new_p = [[] for _ in range(6)]
    new_s = [[] for _ in range(6)]
    for l in range(DEPTH):
        lw = (g_mix[l], w_in[l], w_out[l], b_mu[l], b_w0[l], b_w2[l], b_a0[l], b_a2[l], b_g2[l],
              b_k_k[l], b_k_a[l], b_r_k[l], b_lnx_w[l], b_lnx_b[l], c_sink[l], g_ffn[l],
              w_gate[l], w_up[l], w_down[l])
        hp, st_p = trunk_layer(hp, pos_p, lw, None)
        hs, st_s = trunk_layer(hs, pos_s, lw, (cache_a_k[l], cache_a_v[l], cache_c_k[l], cache_c_v[l],
                                               state_b_wkv[l], state_b_shift[l]))
        for i in range(6):
            new_p[i].append(st_p[i])
            new_s[i].append(st_s[i])
    y_prompt = rms_norm(hp, g_final)
    y_sample = rms_norm(hs, g_final)
    a_k_p, a_v_p, c_k_p, c_v_p, wkv_p, shift_p = [jnp.stack(t, axis=0) for t in new_p]
    a_k_s, a_v_s, c_k_s, c_v_s, wkv_s, shift_s = [jnp.stack(t, axis=0) for t in new_s]
    return (y_prompt, y_sample, a_k_p, a_v_p, c_k_p, c_v_p, wkv_p, shift_p,
            a_k_s, a_v_s, c_k_s, c_v_s, wkv_s, shift_s)


_drawn_inputs = setup_inputs


def setup_inputs(seed=0):
    import zlib

    import numpy as np

    out = dict(_drawn_inputs(seed))
    spreads = {}
    factors = {'b_lnx_w': 8.0, 'b_lnx_b': 8.0, 'c_sink': 6.808, 'g_ffn': 4.829, 'g_final': 2.826}
    for name, (base, spread) in spreads.items():
        noise = np.random.default_rng([zlib.crc32(name.encode()), seed]).standard_normal(out[name].shape)
        drawn = base * np.exp(spread * noise) if base else spread * noise
        out[name] = jnp.asarray(drawn.astype(out[name].dtype))
    for name, factor in factors.items():
        out[name] = (out[name] * factor).astype(out[name].dtype)
    return out
```

```python
import math
from contextlib import ExitStack

import numpy as np

import concourse.bass as bass
from concourse import mybir

ALU = mybir.AluOpType
ACT = mybir.ActivationFunctionType
AX_X = mybir.AxisListType.X
F32 = mybir.dt.float32
F32R = mybir.dt.float32r

P = 128
D = 2048
DEPTH = 2
SEQ = 256
NB = 8
TS = 8
NS = NB * TS
TOK = SEQ + NS
KT = D // P
HD = 64
DFF = 5632
FC = 11
NCH = DFF // P // FC
PAST = 2048
B_COLS = 1792
LORA_W, LORA_A, LORA_G = 96, 96, 64
SCALE = HD ** -0.5
NEG = -1.0e30
DECAY = -math.exp(-0.5)
QA, KA, VA, BR, QC, KC, VC = 0, 4, 8, 12, 26, 34, 35
NP_TILES = 36
G_MIX, G_FFN, MU, W0, A0, KK, KA_, RK_, LNW, LNB, G_FIN, N_PAR = 0, 16, 32, 46, 50, 54, 58, 62, 66, 70, 74, 90
LEVELS = (2, 4, 8, 16, 32)


def constants():
    parts, at = [], {}

    def put(name, a):
        a = np.asarray(a, np.float64).reshape(a.shape[0], -1)
        full = np.zeros((P, a.shape[1]))
        full[:a.shape[0]] = a
        at[name] = (sum(x.shape[1] for x in parts), a.shape[1])
        parts.append(full)

    p = np.arange(P)
    put("ident", np.eye(P))
    put("ones", np.ones((P, P)))
    put("headones", (p[:, None] // HD == p[None, :] // HD) * 1.0)
    rot = np.zeros((P, P))
    for m in range(P):
        d = m % HD
        if d < 8:
            rot[m + 8, m] = -1.0
        elif d < 16:
            rot[m - 8, m] = 1.0
    put("rot", rot)
    pos = np.concatenate([np.arange(SEQ), np.tile(PAST + np.arange(TS), NB)]).astype(np.float32)
    inv = np.exp(np.float32(-math.log(500000.0)) * np.arange(8, dtype=np.float32) * np.float32(2.0) / np.float32(16)).astype(np.float32)
    ang = (pos[None, :] * inv[:, None]).astype(np.float32).astype(np.float64)
    cos, sin = np.ones((P, TOK)), np.zeros((P, TOK))
    for m in range(P):
        if m % HD < 16:
            cos[m], sin[m] = np.cos(ang[m % 8]), np.sin(ang[m % 8])
    put("cos", cos)
    put("sin", sin)

    def branches(dist):
        n = ((dist >= 0) & (dist <= 128)) * 1 + ((dist >= 0) & (dist <= 512) & (dist % 4 == 0)) * 1
        n = n + ((dist >= 0) & (dist <= 2048) & (dist % 16 == 0)) * 1
        return np.where(n > 0, np.log(np.maximum(n, 1)), NEG)

    def window(dist):
        return np.where((dist >= 0) & (dist <= 128), 0.0, NEG)

    k = np.arange(SEQ)
    for name, f in (("maskA", branches), ("maskC", window)):
        put(name, np.concatenate([f(p[:, None] - k[None, :P]), f(P + p[:, None] - k[None, :])], 1))
    t = np.arange(TS)
    fixed = []
    for kt in range(6):
        row = (kt * 16 + p // 8) * 16 + p % 8
        fixed.append(np.tile(branches(PAST + t[None, :] - row[:, None]), (1, 8)))
    for kt in range(4):
        row = PAST - 512 + 4 * p + kt
        fixed.append(np.tile(branches(PAST + t[None, :] - row[:, None]), (1, 8)))
    fixed.append(np.tile(window(P + t[None, :] - p[:, None]), (1, 16)))
    put("maskF", np.concatenate(fixed, 1))
    bt = p - 64
    new = []
    for b in range(NB):
        own = (bt[:, None] >= 0) & (bt[:, None] // TS == b)
        dist = t[None, :] - bt[:, None] % TS
        new.append(np.tile(np.where(own, branches(dist), NEG), (1, 8)))
        new.append(np.tile(np.where(own, window(dist), NEG), (1, 16)))
    put("maskN", np.concatenate(new, 1))
    s, c = p[:, None], p[None, :]

    def pair(size):
        return ((s // (2 * size) == c // (2 * size)) & (s // size % 2 == 0) & (c // size % 2 == 1)) * 1.0

    put("negE1T", -pair(1))
    put("negE1", -pair(1).T)
    for size in LEVELS:
        put(f"lev{size}", pair(size))
    for name, size in (("P", 64), ("S", TS)):
        put("strict" + name, ((s // size == c // size) & (s < c)) * 1.0)
        put("incl" + name, ((s // size == c // size) & (s <= c)) * 1.0)
    put("own", (np.arange(NS)[:, None] // TS == np.arange(NB)[None, :]) * 1.0)
    return np.concatenate(parts, 1).astype(np.float32), at


class Tally:

    def __init__(self):
        self.n = {}

    def __call__(self, sem, by=1):
        self.n[id(sem)] = self.n.get(id(sem), 0) + by
        return self.n[id(sem)]


def segments():
    out, n = [], 0
    for l in range(DEPTH):
        for kind, c, blocks, kt, nd in (
            [("in", 0, 26, KT, 1), ("inq", 0, 8, KT, 2), ("inkv", 0, 2, KT, 1), ("out", 0, 16, KT, 3)]
            + [x for c in range(NCH) for x in (("gu", c, 2 * FC, KT, 1), ("down", c, 16, FC, 1))]
        ):
            out.append((l, kind, c, n, blocks, kt, nd))
            n += blocks
    return out


def build(nc, I, O, at):
    ctx = ExitStack()
    with ctx:
        base = [16512]

        def region(size):
            o = base[0]
            base[0] += size
            return o

        def place(name, shape, offset, dt=F32):
            return nc.alloc_sbuf_tensor_at(name, shape, dt, offset=offset)

        ncon = max(o + n for o, n in at.values())
        RX, RC, RP, RH, RW = region(20480), region(ncon * 4), region(46080), region(40960), region(49152)
        RS, RM = region(31744), region(1440)

        xT = place("xT", [P, KT, TOK], RX)
        con = place("con", [P, ncon], RC)
        par = place("par", [P, N_PAR], RM)
        npar = place("npar", [P, 8], RM + 384)
        shf = place("shf", [P, NB, 14], RM + 416)
        shc = place("shc", [P, 9, 14], RM + 864)
        sink = place("sink", [P, 16], RM + 1376)
        pT = place("pT", [P, NP_TILES, TOK], RP)
        hh = place("hh", [P, KT, TOK], RH, F32R)
        hl = place("hl", [P, KT, TOK], RH + 20480, F32R)
        sq = place("sq", [P, KT, TOK], RH + 20480)
        raw = [place(f"raw{i}", [P, KT, P], RW + 8192 * i) for i in range(2)]
        wh = [place(f"wh{i}", [P, KT, P], RW + 16384 + 8192 * i, F32R) for i in range(2)]
        wl = [place(f"wl{i}", [P, KT, P], RW + 32768 + 8192 * i, F32R) for i in range(2)]
        ah = place("ah", [P, FC, TOK], RP, F32R)
        al = place("al", [P, FC, TOK], RP + 14080, F32R)
        ge = place("ge", [P, TOK], RP + 28160)
        gt = place("gt", [P, TOK], RP + 29440)
        ga = place("ga", [P, TOK], RP + 30720)
        ht = [place(f"ht{i}", [P, 4, TOK], RP + 32000 + 5120 * i) for i in range(2)]
        ssum = place("ssum", [P, TOK], RP + 42240)
        rsb = place("rsb", [P, TOK], RP + 43520)
        prow = place("prow", [N_PAR, P], RP)
        srow = place("srow", [NB * 14, P], RP + 512)
        xin = place("xin", [P, 3, D], RH)
        yout = [place(f"yout{i}", [P, D], RW + 8192 * i) for i in range(3)]
        xm = place("xm", [P, 14, TOK], RH)
        lw = place("lw", [P, 4, TOK], RH + 17920)
        cl = place("cl", [P, 4, TOK], RH + 23040)
        aa = place("aa", [P, 4, TOK], RH + 28160)
        kk = place("kk", [P, 4, TOK], RH + 33280)
        th12 = place("th12", [P, TOK], RH + 38400)
        sg13 = place("sg13", [P, TOK], RH + 39680)
        S0T = place("S0T", [P, NB, 4, P], RH + 17920)
        RKm = place("RKm", [P, 1024], RH + 34304)
        dA, dB, dK, dR, gg, e1, e2, yy = (place(n, [P, 4, TOK], RW + 5120 * i) for i, n in enumerate(
            ("dA", "dB", "dK", "dR", "gg", "e1", "e2", "yy")))
        vt, at_, bt, kt_ = (place(n, [P, 512], RW + 25600 + 2048 * i) for i, n in enumerate(("vt", "at_", "bt", "kt_")))
        S0P = place("S0P", [P, 4, P], RW + 40960)
        uu, tnv, nvs = (place(n, [P, 512], RW + 43008 + 2048 * i) for i, n in enumerate(("uu", "tnv", "nvs")))
        eA, eB, eR = (place(n, [P, 4, 2, P], RP + 20480 + 4096 * i) for i, n in enumerate(("eA", "eB", "eR")))
        pc = place("pc", [P, 4, 12], RP + 20480 + 12288)
        MT, WT, TT, ET, ZZ, NTm, RBm = (place(n, [P, 1024], RS + 4096 * i) for i, n in enumerate(
            ("MT", "WT", "TT", "ET", "ZZ", "NTm", "RBm")))
        tat = place("tat", [P, 512], RS + 28672)
        u1s = place("u1s", [P, 4, NS], RS + 30720)
        lora = [place(f"lora{i}", [P, 512], RS + 2048 * i) for i in range(4)]
        S0in = place("S0in", [P, NB, 4, P], RS + 8192)
        ux, vx = (place(n, [NS, 2, NB, HD], RS + 12288 + 4096 * i) for i, n in enumerate(("ux", "vx")))
        Sout = place("Sout", [P, NB, 4, HD], RS)
        SoutP = place("SoutP", [P, 4, HD], RS + 8192)
        stmp = place("stmp", [P, 512], RS + 20480)
        shr = place("shr", [126, P], RW + 35840)
        cK = [place(f"cK{i}", [P, 10, 512], RH if i == 0 else RW) for i in range(2)]
        cV = [place(f"cV{i}", [P, 10, 512], (RH if i == 0 else RW) + 20480) for i in range(2)]
        ktr = [place(f"ktr{i}", [P, 4, P], RW + 40960 + 2048 * i) for i in range(3)]
        kct = place("kct", [P, P], RW + 47104)
        rm = place("rm", [P, 2], RW + 47616)
        q0 = RP + 20480
        qdA = place("qdA", [P, NB, 4, 2, TS], q0)
        qdC = place("qdC", [P, NB, 2, 8, TS], q0 + 2048)
        ckc = [place(f"ckc{i}", [P, P], q0 + 6144 + 512 * i) for i in range(2)]
        cvc = [place(f"cvc{i}", [P, P], q0 + 7168 + 512 * i) for i in range(2)]
        dg = place("dg", [P, 192], q0 + 8192)
        dn = place("dn", [P, 192], q0 + 8960)
        mx = place("mx", [P, 192], q0 + 9728)
        es = place("es", [P, 16, TS], q0 + 10496)
        rden = place("rden", [P, 192], q0 + 11008)
        mb = place("mb", [P, 192], q0 + 11776)
        tk = [place(f"tk{i}", [P, 3, n], RS + o) for i, (n, o) in enumerate(((512, 0), (512, 6144), (256, 12288)))]
        sms = [place(f"sms{i}", [P, 960], RS + 15360 + 3840 * i) for i in range(2)]
        psm = [place(f"psm{i}", [P, 384], RS + 23040 + 1536 * i) for i in range(2)]
        ppt = [place(f"ppt{i}", [P, 384], RS + 26112 + 1536 * i) for i in range(2)]
        nm = [place(f"nm{i}", [P, 2], RS + 29184 + 64 * i) for i in range(2)]
        sums = [place(f"sums{i}", [P, 2], RS + 29312 + 64 * i) for i in range(2)]
        psk = [place(f"psk{i}", [P, 2], RS + 29440 + 64 * i) for i in range(2)]

        PS = ctx.enter_context(nc.psum_tensor("PS", [P, 8, 512], F32))

        def C(name, rows=P, cols=None):
            o, n = at[name]
            return con[0:rows, o:o + (cols or n)]

        ident = C("ident")
        names = """con x par lora s0 cache0 cache1 w0 w1 wh wl mm ev gexp al
            xtr xtc sq ssum nmm ht hh hl part parc
            zero xm shc sht shrc th sg z aa zexp aexp g gc ksq kss rkp rks clr expd abkr bon st stc
            tok tokc exd G Gc et Z Zc TZ TW TA TAc NV NVc TNV U Y0 Uc Sm SP Y Yc U1 U1c ux Se SF So Soc
            gn ysq gv vr sd rw rot rotc kv kvc qz qbd
            S sm nmx pex pn PT ptc O oc
            ktp ktc sc bS smb mxt dgm bc bsub bex dnm bsum bpv bo mix dve act fin fint finc out souts pool""".split()
        sem = {n: ctx.enter_context(nc.semaphore("s_" + n)) for n in names}
        segs = segments()
        block = ctx.enter_context(nc.Block())

        landed, count = {}, 0
        for (l, kind, c, n0, blocks, kts, nd) in segs:
            landed[n0] = count
            count += 16 * nd * (blocks // 2)

        def start_of(l, kind, c=0):
            return next(x[3] for x in segs if x[:3] == (l, kind, c))

        def seg(l, kind, c=0):
            return next(x for x in segs if x[:3] == (l, kind, c))

        layer_first = [start_of(l, "in") for l in range(DEPTH)]
        CACHE_DMAS = 16
        N_OUTS = 6 + 6 + 3 + 3 + 2

        @block.sync
        def _(sp):
            want = Tally()
            outs = Tally()

            def load(j, l, kind, c, b):
                r = raw[j]
                inc = sem[f"w{j}"]
                if kind in ("in", "inkv"):
                    w = I["w_in"][l].rearrange("(k p) n -> p k n", p=P)
                    c0 = 0 if kind == "in" else KC * P
                    sp.dma_start(r[:], w[:, :, bass.ds(b * P + c0, P)]).then_inc(inc, 16)
                elif kind == "inq":
                    w = I["w_in"][l].rearrange("(k p) n -> p k n", p=P)
                    for half in range(2):
                        sp.dma_start(r[:, :, half * HD:(half + 1) * HD],
                                     w[:, :, bass.ds(b * HD + (QC * P + half * 512), HD)]).then_inc(inc, 16)
                elif kind == "out":
                    w = I["w_out"][l]
                    sp.dma_start(r[:, 0:8], w[0:1024].rearrange("(k p) n -> p k n", p=P)[:, :, bass.ds(b * P, P)]).then_inc(inc, 16)
                    for half in range(2):
                        rows = w[1024 + 512 * half:1536 + 512 * half].rearrange("(k p) n -> p k n", p=HD)
                        sp.dma_start(r[half * HD:(half + 1) * HD, 8:16], rows[:, :, bass.ds(b * P, P)]).then_inc(inc, 16)
                elif kind == "down":
                    w = I["w_down"][l][c * FC * P:(c + 1) * FC * P].rearrange("(k p) n -> p k n", p=P)
                    sp.dma_start(r[:, 0:FC], w[:, :, bass.ds(b * P, P)]).then_inc(inc, 16)

            def load_gu(j, l, c, i):
                w = I["w_gate" if j == 0 else "w_up"][l].rearrange("(k p) n -> p k n", p=P)
                sp.dma_start(raw[j][:], w[:, :, bass.ds(i * P + c * FC * P, P)]).then_inc(sem[f"w{j}"], 16)

            def stream(l, kind, c=0):
                _, _, _, n0, blocks, kts, nd = seg(l, kind, c)

                def pair(i, first):
                    for j in range(2):
                        if not (first and n0 == 0):
                            sp.wait_ge(sem["wl"], 2 * i + (n0 + j - 1))
                        load_gu(j, l, c, i) if kind == "gu" else load(j, l, kind, c, 2 * i + j)
                pair(0, True)
                if blocks > 2:
                    with sp.Fori(1, blocks // 2) as i:
                        pair(i, False)

            sp.dma_start(con[:], I["con"]).then_inc(sem["con"], 16)
            for q in range(2):
                sp.dma_start(xin[:, q, :], I["x_prompt"][0, q * P:(q + 1) * P, :]).then_inc(sem["x"], 16)
            sp.dma_start(xin[0:NS, 2, :], I["x_sample"].rearrange("b t d -> (b t) d")).then_inc(sem["x"], 16)
            for l in range(DEPTH):
                if l:
                    sp.wait_ge(sem["ev"], layer_first[l])
                for name, r0, n in (("g_mix", G_MIX, 16), ("g_ffn", G_FFN, 16), ("b_mu", MU, 14), ("b_w0", W0, 4),
                                    ("b_a0", A0, 4), ("b_k_k", KK, 4), ("b_k_a", KA_, 4), ("b_r_k", RK_, 4),
                                    ("b_lnx_w", LNW, 4), ("b_lnx_b", LNB, 4)):
                    sp.dma_start(prow[r0:r0 + n, :], I[name][l].rearrange("(r c) -> r c", c=P)).then_inc(sem["par"], 16)
                sp.dma_start(prow[G_FIN:G_FIN + 16, :], I["g_final"].rearrange("(r c) -> r c", c=P)).then_inc(sem["par"], 16)
                sp.dma_start(srow[:], I["state_b_shift"][l].rearrange("b (r c) -> (b r) c", c=P)).then_inc(sem["par"], 16)
                sp.dma_start(sink[:], I["c_sink"][l].rearrange("k g -> (k g)").rearrange("(o n) -> o n", o=1).broadcast_to([P, 16])).then_inc(sem["par"], 16)
                sp.wait_ge(sem["zero"], 2 * l + 1)
                sp.dma_start(lora[0][0:LORA_W, :], I["b_w2"][l]).then_inc(sem["lora"], 16)
                sp.dma_start(lora[1][96:128, :], I["b_a2"][l][0:32]).then_inc(sem["lora"], 16)
                sp.dma_start(lora[2][0:64, :], I["b_a2"][l][32:96]).then_inc(sem["lora"], 16)
                sp.dma_start(lora[3][64:128, :], I["b_g2"][l]).then_inc(sem["lora"], 16)
                for b in range(NB):
                    for h2 in range(2):
                        sp.dma_start(S0in[h2 * HD:(h2 + 1) * HD, b, :, h2 * HD:(h2 + 1) * HD],
                                     I["state_b_wkv"][l, b].rearrange("(f h) i j -> h i f j", h=2)[h2]).then_inc(sem["s0"], 16)
                stream(l, "in")
                stream(l, "inq")
                stream(l, "inkv")
                sp.wait_ge(sem["shrc"], l + 1)
                sp.dma_start(O["new_shift_prompt"][l, 0].rearrange("(r c) -> r c", c=P), shr[0:14, :]).then_inc(sem["out"], 16)
                sp.dma_start(O["new_shift_sample"][l].rearrange("b (r c) -> (b r) c", c=P), shr[14:126, :]).then_inc(sem["out"], 16)
                sp.wait_ge(sem["Soc"], 9 * l + 9)
                for h2 in range(2):
                    for b in range(NB):
                        sp.dma_start(O["new_wkv_sample"][l, b].rearrange("(f h) i j -> h i f j", h=2)[h2],
                                     Sout[h2 * HD:(h2 + 1) * HD, b]).then_inc(sem["souts"], 16)
                    sp.dma_start(O["new_wkv_prompt"][l, 0].rearrange("(f h) i j -> h i f j", h=2)[h2],
                                 SoutP[h2 * HD:(h2 + 1) * HD]).then_inc(sem["souts"], 16)

                def cache(b):
                    s = sem[f"cache{b % 2}"]
                    for src, dst in (("cache_a_k", cK[b % 2]), ("cache_a_v", cV[b % 2])):
                        rows = I[src][l, b].rearrange("r h d -> r (h d)")
                        old = rows[0:1536].rearrange("(n g r) c -> n g r c", n=6, r=16)
                        for n in range(6):
                            sp.dma_start(dst[:, n, :], old[n, :, 0:8, :]).then_inc(s, 16)
                        sp.dma_start(dst[:, 6:10, :], rows[1536:2048].rearrange("(p r) c -> p r c", p=P)).then_inc(s, 16)
                    sp.dma_start(ckc[b % 2][:], I["cache_c_k"][l, b].rearrange("r h d -> r (h d)")).then_inc(s, 16)
                    sp.dma_start(cvc[b % 2][:], I["cache_c_v"][l, b].rearrange("r h d -> r (h d)")).then_inc(s, 16)

                sp.wait_ge(sem["rw"], l + 1)
                cache(0)
                cache(1)
                sp.wait_ge(sem["kvc"], 9 * (l + 1))
                for q in range(2):
                    rows = slice(q * P, (q + 1) * P)
                    sp.dma_start(O["new_a_k_prompt"][l, 0, rows].rearrange("t h d -> t (h d)"), tk[0][:, q, :]).then_inc(sem["out"], 16)
                    sp.dma_start(O["new_a_v_prompt"][l, 0, rows].rearrange("t h d -> t (h d)"), tk[1][:, q, :]).then_inc(sem["out"], 16)
                sp.dma_start(O["new_c_k_prompt"][l, 0].rearrange("t h d -> t (h d)"), tk[2][:, 1, 0:P]).then_inc(sem["out"], 16)
                sp.dma_start(O["new_c_v_prompt"][l, 0].rearrange("t h d -> t (h d)"), tk[2][:, 1, P:2 * P]).then_inc(sem["out"], 16)
                for name, src in (("new_a_k_sample", tk[0][64:128, 2, :]), ("new_a_v_sample", tk[1][64:128, 2, :]),
                                  ("new_c_k_sample", tk[2][64:128, 2, 0:P]), ("new_c_v_sample", tk[2][64:128, 2, P:2 * P])):
                    sp.dma_start(O[name][l].rearrange("b t h d -> (b t) (h d)"), src).then_inc(sem["out"], 16)
                for b in range(2, NB):
                    sp.wait_ge(sem["bpv"], NB * l + b - 1)
                    cache(b)
                sp.wait_ge(sem["out"], 16 * 12 * (l + 1))
                sp.wait_ge(sem["souts"], 16 * 18 * (l + 1))
                sp.wait_ge(sem["mix"], 4 * l + 4)
                stream(l, "out")
                for c in range(NCH):
                    stream(l, "gu", c)
                    stream(l, "down", c)
            for q in range(3):
                sp.wait_ge(sem["finc"], 4 * (q + 1))
                if q < 2:
                    sp.dma_start(O["y_prompt"][0, q * P:(q + 1) * P, :], yout[q][:]).then_inc(sem["fin"], 16)
                else:
                    sp.dma_start(O["y_sample"].rearrange("b t d -> (b t) d"), yout[2][0:NS, :]).then_inc(sem["fin"], 16)
            sp.wait_ge(sem["fin"], 48)
            sp.wait_ge(sem["out"], 16 * 12 * DEPTH)
            sp.wait_ge(sem["souts"], 16 * 18 * DEPTH)

        @block.gpsimd
        def _(pool):
            for l in range(DEPTH):
                if l:
                    pool.wait_ge(sem["ev"], layer_first[l])
                for i in range(4):
                    pool.memset(lora[i][:], 0.0)
                pool.memset(S0in[:], 0.0).then_inc(sem["zero"], 1)
                pool.wait_ge(sem["xm"], l + 1)
                pool.memset(S0P[:], 0.0)
                pool.memset(eA[:], 0.0)
                pool.memset(eB[:], 0.0)
                pool.memset(eR[:], 0.0).then_inc(sem["zero"], 1)
                pool.wait_ge(sem["rw"], l + 1)
                pool.memset(qdA[:], 0.0)
                pool.memset(qdC[:], 0.0).then_inc(sem["qz"], 1)

        @block.scalar
        def _(act):
            want = Tally()

            def take(name, by=1):
                act.wait_ge(sem[name], want(sem[name], by))

            def split(n0, i, j, kts, nd):
                act.wait_ge(sem[f"w{j}"], 16 * nd * i + (landed[n0] + 16 * nd))
                if not (n0 == 0 and isinstance(i, int) and i == 0):
                    act.wait_ge(sem["mm"], 2 * i + (n0 + j - 1))
                act.activation(wh[j][:, 0:kts], raw[j][:, 0:kts], ACT.Copy).then_inc(sem["wh"], 1)

            def stream(l, kind, c=0, ready=False, ahead=None):
                _, _, _, n0, blocks, kts, nd = seg(l, kind, c)
                if not ready:
                    split(n0, 0, 0, kts, nd)

                def pair(i, last):
                    split(n0, i, 1, kts, nd)
                    if kind == "gu":
                        act.wait_ge(sem["mm"], 2 * i + (n0 + 1))
                        act.activation(ge[:], PS[:, 0, 0:TOK], ACT.Exp, scale=-1.0).then_inc(sem["gexp"], 1)
                    if not last:
                        split(n0, i + 1, 0, kts, nd)
                    elif ahead:
                        _, _, _, m0, _, k2, d2 = seg(*ahead)
                        split(m0, 0, 0, k2, d2)
                if blocks > 2:
                    with act.Fori(0, blocks // 2 - 1) as i:
                        pair(i, False)
                pair(blocks // 2 - 1, True)

            def squares():
                act.activation(sq[:], xT[:], ACT.Square).then_inc(sem["sq"], 1)

            def root(x):
                take("vr")
                act.activation(x[:], x[:], ACT.Sqrt).then_inc(sem["sd"], 1)

            def hi_parts():
                root(rsb)
                for g in range(4):
                    take("ht")
                    act.activation(hh[:, 4 * g:4 * g + 4], ht[g % 2][:], ACT.Copy).then_inc(sem["hh"], 1)

            for q in range(12):
                take("xtr")
                nt = P if q < 8 else NS
                tau, k0 = q // 4, q % 4 * 4
                act.activation(xT[:, k0:k0 + 4, tau * P:tau * P + nt],
                               PS[:, 2 + q % 4, 0:4 * nt].rearrange("p (k t) -> p k t", k=4), ACT.Copy).then_inc(sem["xtc"], 1)
            act.wait_ge(sem["xtc"], 12)
            for l in range(DEPTH):
                if l:
                    act.wait_ge(sem["ev"], layer_first[l])
                squares()
                hi_parts()
                stream(l, "in", ahead=(l, "inq"))
                stream(l, "inq", ready=True, ahead=(l, "inkv"))
                stream(l, "inkv", ready=True)
                take("xm")
                act.activation(th12[:], xm[:, 12, :], ACT.Tanh).then_inc(sem["th"], 1)
                act.activation(sg13[:], xm[:, 13, :], ACT.Exp, scale=-1.0).then_inc(sem["th"], 1)
                take("z")
                for f in range(4):
                    a = act.activation(e1[:, f], PS[:, f, 0:TOK], ACT.Exp, scale=-1.0, bias=npar[:, f:f + 1])
                a.then_inc(sem["zexp"], 1)
                take("aa")
                for f in range(4):
                    a = act.activation(e2[:, f], PS[:, 4 + f, 0:TOK], ACT.Exp, scale=-1.0, bias=npar[:, 4 + f:5 + f])
                a.then_inc(sem["aexp"], 1)
                take("g")
                act.activation(gg[:], PS[:, 0:4, 0:TOK], ACT.Copy).then_inc(sem["gc"], 1)
                root(e2)
                take("clr", 2)
                act.activation(dR[:], cl[:], ACT.Exp)
                act.activation(dK[:], cl[:], ACT.Exp, scale=-1.0)
                act.activation(dA[:], dA[:], ACT.Exp).then_inc(sem["expd"], 1)
                for r in range(8):
                    take("st")
                    act.activation(S0T[:, r], PS[:, 4 + r % 4, :].rearrange("p (f i) -> p f i", f=4), ACT.Copy).then_inc(sem["stc"], 1)
                for tau in range(3):
                    nt = P if tau < 2 else NS
                    for q, dst in enumerate((vt, at_, bt, kt_)):
                        take("tok")
                        act.activation(dst[0:nt, :], PS[0:nt, q, :], ACT.Copy).then_inc(sem["tokc"], 1)
                    for size in LEVELS if tau < 2 else LEVELS[:2]:
                        take("Z")
                        act.activation(ZZ[0:nt, 0:8 * nt].rearrange("p (b n) -> p b n", b=2), PS[0:nt, 6:8, 0:4 * nt], ACT.Copy).then_inc(sem["Zc"], 1)
                    take("TA")
                    act.activation(tat[:, 0:4 * nt], PS[:, 4, 0:4 * nt], ACT.Copy).then_inc(sem["TAc"], 1)
                take("U1")
                act.activation(u1s[:], PS[:, 7, 0:256].rearrange("p (f t) -> p f t", f=4), ACT.Copy).then_inc(sem["U1c"], 1)
                for r in range(9):
                    take("So")
                    for h2 in range(2):
                        rows, cols = slice(h2 * HD, h2 * HD + HD), slice(h2 * HD, h2 * HD + HD)
                        src = PS[rows, 4 + r % 4, :].rearrange("p (f j) -> p f j", f=4)[:, :, cols]
                        dst = Sout[rows, r] if r < 8 else SoutP[rows]
                        a = act.activation(dst, src, ACT.Copy)
                    a.then_inc(sem["Soc"], 1)
                root(e1)
                act.wait_ge(sem["souts"], 16 * 18 * (l + 1))
                for q in range(9):
                    take("kv")
                    n = 512 if q % 3 < 2 else 256
                    act.activation(tk[q % 3][:, q // 3, :], PS[:, q % 6, 0:n], ACT.Copy).then_inc(sem["kvc"], 1)
                for u in range(24 + 2):
                    if u < 24:
                        take("nmx")
                        for q in range(2):
                            cols = slice(0, P) if q == 0 else slice(P, 384)
                            a = act.activation(psm[u % 2][:, cols], psm[u % 2][:, cols], ACT.Exp,
                                               bias=nm[u % 2][:, q:q + 1], accum_out=sums[u % 2][:, q:q + 1])
                        if u >= 8:
                            h = (u - 8) // 2 + 8 * (u % 2)
                            a = act.activation(psk[u % 2][:], nm[u % 2][:], ACT.Exp, bias=sink[:, h:h + 1])
                        a.then_inc(sem["pex"], 1)
                    if 1 <= u <= 24:
                        v = u - 1
                        take("PT")
                        if v >= 2:
                            act.wait_ge(sem["O"], 24 * l + v - 1)
                        act.activation(ppt[v % 2][:], PS[:, 2 + v % 2, 0:384], ACT.Copy).then_inc(sem["ptc"], 1)
                    if u >= 2:
                        v = u - 2
                        par2 = v % 2
                        tile = QA + v // 2 if v < 8 else QC + (v - 8) // 2
                        take("O")
                        rows = slice(par2 * HD, par2 * HD + HD)
                        act.activation(pT[rows, tile, 0:SEQ], PS[rows, 4 + par2, 0:SEQ], ACT.Copy).then_inc(sem["oc"], 1)
                for b in range(NB):
                    for kt in range(11):
                        take("ktp")
                        if kt < 10:
                            if b or kt > 2:
                                act.wait_ge(sem["sc"], 11 * (NB * l + b) + kt - 2 - (1 if kt < 3 else 0))
                            act.activation(ktr[kt % 3][:], PS[:, 2 + kt % 3, :].rearrange("p (f k) -> p f k", f=4), ACT.Copy).then_inc(sem["ktc"], 1)
                        else:
                            act.activation(kct[:], PS[:, 3, 0:P], ACT.Copy).then_inc(sem["ktc"], 1)
                    take("bsub")
                    act.activation(sms[b % 2][:], sms[b % 2][:], ACT.Exp)
                    act.activation(es[:], es[:], ACT.Exp).then_inc(sem["bex"], 1)
                for g, t0 in enumerate((QA, BR, QC, QC + 4)):
                    act.wait_ge(sem["bo"], NB * (l + 1))
                    act.activation(hh[:, 4 * g:4 * g + 4], pT[:, t0:t0 + 4], ACT.Copy).then_inc(sem["hh"], 1)
                act.wait_ge(sem["mix"], 4 * l + 4)
                stream(l, "out")
                act.wait_ge(sem["ev"], start_of(l, "gu", 0))
                squares()
                hi_parts()
                for c in range(NCH):
                    stream(l, "gu", c, ready=c > 0, ahead=(l, "down", c))
                    stream(l, "down", c, ready=True, ahead=(l, "gu", c + 1) if c < NCH - 1 else None)
            act.wait_ge(sem["ev"], segs[-1][3] + segs[-1][4])
            squares()
            root(rsb)

        @block.vector
        def _(dve):
            want = Tally()

            def take(name, by=1):
                dve.wait_ge(sem[name], want(sem[name], by))

            def done(ins, name="dve"):
                ins.then_inc(sem[name], 1)
                dve.wait_ge(sem[name], want(sem[name]))

            tt, ts, stt = dve.tensor_tensor, dve.tensor_scalar, dve.scalar_tensor_tensor

            def split(n, j, kts):
                dve.wait_ge(sem["wh"], n + 1)
                tt(wl[j][:, 0:kts], raw[j][:, 0:kts], wh[j][:, 0:kts].bitcast(F32), ALU.subtract).then_inc(sem["wl"], 1)

            def stream(l, kind, c=0, ready=False, ahead=None):
                _, _, _, n0, blocks, kts, nd = seg(l, kind, c)
                tile0 = {"in": 0, "inq": QC, "inkv": KC}.get(kind, 0)
                if not ready:
                    split(n0, 0, kts)

                def drain(i, j):
                    if kind in ("in", "inq", "inkv"):
                        dve.wait_ge(sem["mm"], 2 * i + (n0 + j + 1))
                        dve.tensor_copy(pT[:, bass.ds(2 * i + (tile0 + j), 1), :].rearrange("p o t -> p (o t)"), PS[:, j, 0:TOK]).then_inc(sem["ev"], 1)
                    elif kind in ("out", "down"):
                        dve.wait_ge(sem["mm"], 2 * i + (n0 + j + 1))
                        x = xT[:, bass.ds(2 * i + j, 1), :].rearrange("p o t -> p (o t)")
                        tt(x, x, PS[:, j, 0:TOK], ALU.add).then_inc(sem["ev"], 1)
                    elif j == 0:
                        pairs = (l * NCH + c) * FC
                        dve.wait_ge(sem["gexp"], i + (pairs + 1))
                        ts(gt[:], ge[:], 1.0, None, ALU.add).then_inc(sem["act"], 1)
                        dve.wait_ge(sem["act"], 5 * (i + pairs) + 1)
                        dve.reciprocal(gt[:], gt[:]).then_inc(sem["act"], 1)
                        dve.wait_ge(sem["act"], 5 * (i + pairs) + 2)
                        tt(gt[:], gt[:], PS[:, 0, 0:TOK], ALU.mult).then_inc(sem["ev"], 1)
                    else:
                        pairs = (l * NCH + c) * FC
                        dve.wait_ge(sem["mm"], 2 * i + (n0 + 2))
                        dve.wait_ge(sem["ev"], 2 * i + (n0 + 1))
                        hi = ah[:, bass.ds(i, 1), :].rearrange("p o t -> p (o t)")
                        lo = al[:, bass.ds(i, 1), :].rearrange("p o t -> p (o t)")
                        tt(hi, gt[:], PS[:, 1, 0:TOK], ALU.mult).then_inc(sem["act"], 1)
                        tt(ga[:], gt[:], PS[:, 1, 0:TOK], ALU.mult).then_inc(sem["ev"], 1)
                        dve.wait_ge(sem["act"], 5 * (i + pairs) + 3)
                        dve.wait_ge(sem["ev"], 2 * i + (n0 + 2))
                        tt(lo, ga[:], hi.bitcast(F32), ALU.subtract).then_inc(sem["act"], 2)

                def pair(i, last):
                    split(2 * i + (n0 + 1), 1, kts)
                    drain(i, 0)
                    if not last:
                        split(2 * i + (n0 + 2), 0, kts)
                    elif ahead:
                        _, _, _, m0, _, k2, _ = seg(*ahead)
                        split(m0, 0, k2)
                    drain(i, 1)
                if blocks > 2:
                    with dve.Fori(0, blocks // 2 - 1) as i:
                        pair(i, False)
                pair(blocks // 2 - 1, True)
                dve.wait_ge(sem["ev"], n0 + blocks)

            def rms():
                take("sq")
                done(dve.tensor_reduce(ssum[:], sq[:].rearrange("p k t -> p t k"), AX_X, ALU.add), "ssum")
                take("nmm")
                done(ts(rsb[:], PS[:, 2, 0:TOK], 1.0 / D, 1e-6, ALU.mult, ALU.add), "vr")
                take("sd")
                done(dve.reciprocal(rsb[:], rsb[:]))

            def norm(g0):
                rms()
                for g in range(4):
                    for k in range(4):
                        a = stt(ht[g % 2][:, k], xT[:, 4 * g + k], par[:, g0 + 4 * g + k:g0 + 4 * g + k + 1], rsb[:], ALU.mult, ALU.mult)
                    done(a, "ht")
                    take("hh")
                    done(tt(hl[:, 4 * g:4 * g + 4], ht[g % 2][:], hh[:, 4 * g:4 * g + 4].bitcast(F32), ALU.subtract), "hl")

            def banks(b, nt):
                return PS[0:nt, b:b + 2, 0:4 * nt].rearrange("p b (h t) -> p b h t", h=4)

            def heads(x, nt):
                return x[0:nt, 0:8 * nt].rearrange("p (b h t) -> p b h t", b=2, h=4)

            def mask(name, nt):
                return C(name, nt, nt).unsqueeze(1).unsqueeze(1).broadcast_to([nt, 2, 4, nt])

            def halves():
                return [slice(0, HD), slice(HD, P)]

            def rwkv(l):
                pB = pT[:, BR:BR + 14]
                sam = lambda x: x[:, :, SEQ:TOK].rearrange("p k (b t) -> p k b t", b=NB)
                tt(xm[:, :, 1:SEQ], pB[:, :, 0:SEQ - 1], pB[:, :, 1:SEQ], ALU.subtract)
                ts(xm[:, :, 0:1], pB[:, :, 0:1], -1.0, None, ALU.mult)
                for b in range(NB):
                    o = SEQ + b * TS
                    tt(xm[:, :, o + 1:o + TS], pB[:, :, o:o + TS - 1], pB[:, :, o + 1:o + TS], ALU.subtract)
                tt(sam(xm[:])[:, :, :, 0], shf[:].rearrange("p b k -> p k b"), sam(pB)[:, :, :, 0], ALU.subtract)
                dve.tensor_copy(shc[:, 0, :], pB[:, :, SEQ - 1])
                done(dve.tensor_copy(shc[:, 1:9, :].rearrange("p b k -> p k b"), sam(pB)[:, :, :, TS - 1]), "shc")
                for k in range(14):
                    a = stt(xm[:, k], xm[:, k], par[:, MU + k:MU + k + 1], pB[:, k], ALU.mult, ALU.add)
                done(a, "xm")
                take("sht")
                done(dve.tensor_copy(shr[:], PS[0:126, 2, 0:P]), "shrc")
                take("th", 2)
                done(ts(sg13[:], sg13[:], 1.0, None, ALU.add))
                done(dve.reciprocal(sg13[:], sg13[:]), "sg")
                xr, xk, xv = xm[:, 0:4], xm[:, 4:8], xm[:, 8:12]
                col = lambda r, f: par[:, r + f:r + f + 1]
                for f in range(4):
                    a = ts(kk[:, f], xk[:, f], col(KK, f), None, ALU.mult)
                done(a)
                take("zexp")
                done(ts(e1[:], e1[:], 1.0, None, ALU.add))
                done(dve.reciprocal(e1[:], e1[:]))
                done(ts(lw[:], e1[:], DECAY, None, ALU.mult))
                done(tt(e1[:], kk[:], kk[:], ALU.mult), "ksq")
                take("aexp")
                done(ts(e2[:], e2[:], 1.0, None, ALU.add))
                done(dve.reciprocal(aa[:], e2[:]))
                take("kss")
                done(ts(e2[:], PS[:, 4:8, 0:TOK], 1e-24, None, ALU.max), "vr")
                take("sd")
                done(dve.reciprocal(e2[:], e2[:]))
                done(tt(kk[:], kk[:], e2[:], ALU.mult))
                for f in range(4):
                    a = ts(e2[:, f], aa[:, f], 1.0, col(KA_, f), ALU.subtract, ALU.mult)
                done(a)
                done(stt(xk, e2[:], 1.0, xk, ALU.add, ALU.mult))
                for f in range(4):
                    a = stt(e1[:, f], xr[:, f], col(RK_, f), xk[:, f], ALU.mult, ALU.mult)
                done(a, "rkp")
                pro = lambda x: x[:, :, 0:SEQ].rearrange("p f (c t) -> p f c t", t=HD)
                dve.tensor_copy(cl[:, :, 0:SEQ], lw[:, :, 0:SEQ])
                done(dve.tensor_copy(e2[:, :, SEQ:TOK], lw[:, :, SEQ:TOK]))
                for step in range(6):
                    s = 1 << step
                    for view, src, dst in ([(pro, cl, e2) if step % 2 == 0 else (pro, e2, cl)]
                                           + ([(sam, e2, cl) if step % 2 == 0 else (sam, cl, e2)] if step < 3 else [])):
                        x, y = view(src[:]), view(dst[:])
                        n = x.shape[3]
                        for f in range(4):
                            tt(y[:, f, :, s:n], x[:, f, :, s:n], x[:, f, :, 0:n - s], ALU.add)
                        a = dve.tensor_copy(y[:, :, :, 0:s], x[:, :, :, 0:s])
                    done(a, "clr" if step == 5 else "dve")
                done(tt(dA[:], cl[:], lw[:], ALU.subtract), "clr")
                done(tt(dB[:], kk[:], aa[:], ALU.mult))
                take("expd")
                dve.tensor_copy(pc[:, :, 0:4], dR[:, :, HD - 1:SEQ:HD])
                done(dve.tensor_copy(pc[:, :, 4:12], dR[:, :, SEQ + TS - 1:TOK:TS]))
                tt(dB[:], dB[:], dK[:], ALU.mult)
                tt(dA[:], dA[:], kk[:], ALU.mult)
                tt(dR[:], dR[:], xr, ALU.mult)
                done(tt(dK[:], dK[:], xk, ALU.mult), "abkr")
                take("rks")
                done(tt(xk, PS[:, 0:4, 0:TOK], xv, ALU.mult), "bon")
                dve.wait_ge(sem["zero"], 2 * l + 2)
                for tau in range(3):
                    c0, nt = tau * P, P if tau < 2 else NS
                    kind = "P" if tau < 2 else "S"
                    for x, y in ((dA, eA), (dB, eB), (dR, eR)):
                        for h2, rows in enumerate(halves()):
                            a = dve.tensor_copy(y[rows, :, h2, 0:nt], x[rows, :, c0:c0 + nt])
                    done(a, "exd")
                    take("G")
                    done(dve.tensor_copy(heads(MT, nt), banks(4, nt)), "Gc")
                    done(tt(heads(WT, nt), heads(MT, nt), mask("negE1T", nt), ALU.mult))
                    done(tt(heads(WT, nt), heads(WT, nt), mask("ident", nt), ALU.add))
                    take("G")
                    done(tt(heads(TT, nt), banks(6, nt), mask("negE1", nt), ALU.mult))
                    done(tt(heads(TT, nt), heads(TT, nt), mask("ident", nt), ALU.add))
                    take("G")
                    tt(heads(NTm, nt), banks(0, nt), mask("strict" + kind, nt), ALU.mult)
                    take("G")
                    tt(heads(RBm, nt), banks(2, nt), mask("incl" + kind, nt), ALU.mult)
                    take("G")
                    done(tt(heads(RKm, nt), banks(4, nt), mask("incl" + kind, nt), ALU.mult))
                    for size in LEVELS if tau < 2 else LEVELS[:2]:
                        done(tt(heads(ET, nt), heads(MT, nt), mask(f"lev{size}", nt), ALU.mult), "et")
                        take("TZ")
                        tt(heads(TT, nt), heads(TT, nt), banks(0, nt), ALU.subtract)
                        done(tt(heads(WT, nt), heads(WT, nt), banks(2, nt), ALU.subtract), "TW")
                    take("NV")
                    done(dve.tensor_copy(nvs[0:nt, :], PS[0:nt, 5, :]), "NVc")
                    take("TNV")
                    done(dve.tensor_copy(tnv[0:nt, :], PS[0:nt, 6, :]))
                    for c in range(2) if tau < 2 else range(1):
                        r = slice(c * HD, c * HD + HD)
                        take("U")
                        done(stt(uu[r, :], PS[r, 7 if tau < 2 else 1, :], -1.0, tnv[r, :], ALU.mult, ALU.subtract), "Uc")
                        if tau < 2:
                            take("Sm")
                            ps = PS[:, 1, :].rearrange("p (f i) -> p f i", f=4)
                            done(tt(S0P[:], S0P[:], ps, ALU.add))
                            ch = 2 * tau + c
                            done(tt(S0P[:], S0P[:], pc[:, :, ch:ch + 1].broadcast_to([P, 4, P]), ALU.mult))
                            done(tt(S0P[:], S0P[:], C("headones").unsqueeze(1).broadcast_to([P, 4, P]), ALU.mult), "SP")
                    take("Y")
                    if tau == 0:
                        dve.wait_ge(sem["out"], 16 * 12 * l + 32)
                    done(dve.tensor_copy(yy[:, :, c0:c0 + nt], PS[:, 0, 0:4 * nt].rearrange("p (f t) -> p f t", f=4)), "Yc")
                own = C("own", NS).unsqueeze(2).broadcast_to([NS, NB, HD])
                for f in range(4):
                    if f:
                        dve.wait_ge(sem["Se"], 4 * l + f)
                    for h2 in range(2):
                        cols = slice((2 * f + h2) * HD, (2 * f + h2 + 1) * HD)
                        tt(ux[:, h2], uu[0:NS, cols].unsqueeze(1).broadcast_to([NS, NB, HD]), own, ALU.mult)
                        a = tt(vx[:, h2], vt[0:NS, cols].unsqueeze(1).broadcast_to([NS, NB, HD]), own, ALU.mult)
                    done(a, "ux")
                    take("Se")
                    for h2, rows in enumerate(halves()):
                        tmp = stmp[rows, :].rearrange("p (b i) -> p b i", b=NB)
                        s0 = S0T[rows, :, f, h2 * HD:h2 * HD + HD]
                        done(tt(tmp, s0, PS[rows, 2 + f % 2, :].rearrange("p (b i) -> p b i", b=NB), ALU.add))
                        a = tt(s0, tmp, pc[rows, f, 4:12].unsqueeze(2).broadcast_to([HD, NB, HD]), ALU.mult)
                    done(a, "SF")
                take("gn")
                done(ts(e1[:], PS[:, 0:4, 0:TOK], 1.0 / HD, None, ALU.mult))
                done(tt(yy[:], yy[:], e1[:], ALU.subtract))
                done(tt(e1[:], yy[:], yy[:], ALU.mult), "ysq")
                take("gv")
                done(ts(e1[:], PS[:, 0:4, 0:TOK], 1.0 / HD, 64e-5, ALU.mult, ALU.add), "vr")
                take("sd")
                done(dve.reciprocal(e1[:], e1[:]))
                done(tt(yy[:], yy[:], e1[:], ALU.mult))
                for f in range(4):
                    a = ts(yy[:, f], yy[:, f], col(LNW, f), col(LNB, f), ALU.mult, ALU.add)
                done(a)
                done(tt(yy[:], yy[:], xk, ALU.add))
                dve.wait_ge(sem["Soc"], 9 * (l + 1))
                done(tt(pT[:, BR:BR + 4], yy[:], gg[:], ALU.mult), "rw")

            def attention(l):
                for u, tile in enumerate(list(range(QA, VA)) + list(range(QC, VC))):
                    take("rot")
                    t1, t2 = sms[u % 2][:, 0:TOK], sms[u % 2][:, 480:480 + TOK]
                    done(tt(t1, PS[:, 4 + u % 4, 0:TOK], C("sin"), ALU.mult), "rotc")
                    done(tt(t2, pT[:, tile], C("cos"), ALU.mult))
                    a = tt(pT[:, tile], t1, t2, ALU.add)
                done(a)
                take("qz")
                for h2, rows in enumerate(halves()):
                    for f in range(4):
                        dve.tensor_copy(qdA[rows, :, f, h2, :], pT[rows, QA + f, SEQ:TOK].rearrange("p (b t) -> p b t", b=NB))
                    for i in range(8):
                        a = dve.tensor_copy(qdC[rows, :, h2, i, :], pT[rows, QC + i, SEQ:TOK].rearrange("p (b t) -> p b t", b=NB))
                done(a, "qbd")
                for u in range(24 + 1):
                    if u < 24:
                        take("S")
                        x = psm[u % 2]
                        if u >= 2:
                            dve.wait_ge(sem["PT"], 24 * l + u - 1)
                        done(stt(x[:], PS[:, u % 2, 0:384], SCALE, C("maskA" if u < 8 else "maskC"), ALU.mult, ALU.add), "sm")
                        dve.tensor_reduce(nm[u % 2][:, 0:1], x[:, 0:P], AX_X, ALU.max, negate=True)
                        done(dve.tensor_reduce(nm[u % 2][:, 1:2], x[:, P:384], AX_X, ALU.max, negate=True), "nmx")
                    if u >= 1:
                        v = u - 1
                        take("pex")
                        if v >= 8:
                            done(tt(sums[v % 2][:], sums[v % 2][:], psk[v % 2][:], ALU.add))
                        done(dve.reciprocal(sums[v % 2][:], sums[v % 2][:]))
                        y = psm[v % 2]
                        ts(y[:, 0:P], y[:, 0:P], sums[v % 2][:, 0:1], None, ALU.mult)
                        done(ts(y[:, P:384], y[:, P:384], sums[v % 2][:, 1:2], None, ALU.mult), "pn")
                for b in range(NB):
                    x = sms[b % 2]
                    take("bS")
                    if b >= 2:
                        dve.wait_ge(sem["bpv"], NB * l + b - 1)
                    stt(x[:, 0:512], PS[:, 0, :], SCALE, C("maskF")[:, 0:512], ALU.mult, ALU.add)
                    stt(x[:, 512:768], PS[:, 1, 0:256], SCALE, C("maskF")[:, 512:768], ALU.mult, ALU.add)
                    done(stt(x[:, 768:960], PS[:, 1, 256:448], SCALE, C("maskN")[:, 192 * b:192 * b + 192], ALU.mult, ALU.add), "smb")

                    def over(out, op, name):
                        done(dve.tensor_reduce(out[:, 0:64], x[:, 0:640].rearrange("p (k c) -> p c k", k=10), AX_X, op))
                        tt(out[:, 0:64], out[:, 0:64], x[:, 768:832], op)
                        done(tt(out[:, 64:192], x[:, 640:768], x[:, 832:960], op), name)
                    over(mx, ALU.max, "mxt")
                    take("bc")
                    dve.tensor_reduce(rm[:, 0:1], PS[:, 5, 0:P], AX_X, ALU.max)
                    done(dve.tensor_reduce(rm[0:64, 1:2], PS[0:64, 5, P:2 * P], AX_X, ALU.max))
                    ts(dg[:, 0:P], ident, rm[:, 0:1], None, ALU.mult)
                    done(ts(dg[0:64, P:192], C("ident", 64, 64), rm[0:64, 1:2], None, ALU.mult), "dgm")
                    take("bc")
                    done(dve.tensor_copy(mb[:], PS[:, 6, 0:192]))
                    xa = x[:, 0:640].rearrange("p (k c) -> p k c", k=10)
                    tt(xa, xa, mb[:, 0:64].unsqueeze(1).broadcast_to([P, 10, 64]), ALU.subtract)
                    tt(x[:, 640:768], x[:, 640:768], mb[:, 64:192], ALU.subtract)
                    tt(x[:, 768:960], x[:, 768:960], mb[:], ALU.subtract)
                    done(tt(es[:], sink[:].unsqueeze(2).broadcast_to([P, 16, TS]), mb[:, 64:192].rearrange("p (g t) -> p g t", t=TS), ALU.subtract), "bsub")
                    take("bex")
                    over(dn, ALU.add, "dnm")
                    take("bsum")
                    dve.tensor_copy(rden[:, 0:64], PS[:, 6, 0:64])
                    done(tt(rden[:, 64:192], PS[:, 6, 64:192], es[:].rearrange("p g t -> p (g t)"), ALU.add))
                    done(dve.reciprocal(rden[:], rden[:]))
                    take("bpv")
                    o = SEQ + b * TS
                    for h2, rows in enumerate(halves()):
                        v4 = lambda y: y.rearrange("p (f h t) -> p f h t", f=4, h=2)[:, :, h2]
                        tt(pT[rows, QA:QA + 4, o:o + TS], v4(PS[rows, 7, 0:64]), v4(rden[rows, 0:64]), ALU.mult)
                        v8 = lambda y: y.rearrange("p (k i t) -> p k i t", k=2, i=8)[:, h2]
                        a = tt(pT[rows, QC:QC + 8, o:o + TS], v8(PS[rows, 7, 64:192]), v8(rden[rows, 64:192]), ALU.mult)
                    done(a, "bo")
                for g, t0 in enumerate((QA, BR, QC, QC + 4)):
                    take("hh")
                    if g == 0:
                        dve.wait_ge(sem["oc"], 24 * (l + 1))
                    done(tt(hl[:, 4 * g:4 * g + 4], pT[:, t0:t0 + 4], hh[:, 4 * g:4 * g + 4].bitcast(F32), ALU.subtract), "mix")

            for l in range(DEPTH):
                take("part")
                dve.tensor_copy(par[:], PS[:, 6, 0:N_PAR])
                done(dve.tensor_copy(shf[:].rearrange("p b k -> p (b k)"), PS[:, 7, 0:NB * 14]))
                done(ts(npar[:], par[:, W0:W0 + 8], -1.0, None, ALU.mult), "parc")
                if l == 0:
                    dve.wait_ge(sem["xtc"], 12)
                norm(G_MIX)
                stream(l, "in", ahead=(l, "inq"))
                stream(l, "inq", ready=True, ahead=(l, "inkv"))
                stream(l, "inkv", ready=True)
                rwkv(l)
                attention(l)
                stream(l, "out")
                norm(G_FFN)
                for c in range(NCH):
                    stream(l, "gu", c, ready=c > 0, ahead=(l, "down", c))
                    stream(l, "down", c, ready=True, ahead=(l, "gu", c + 1) if c < NCH - 1 else None)
            rms()
            for k in range(KT):
                a = stt(xT[:, k], xT[:, k], par[:, G_FIN + k:G_FIN + k + 1], rsb[:], ALU.mult, ALU.mult)
            done(a, "ht")
            for q in range(12):
                tau, k0 = q // 4, q % 4 * 4
                nt = P if tau < 2 else NS
                take("fint")
                dve.tensor_copy(yout[tau][0:nt, k0 * P:(k0 + 4) * P], PS[0:nt, q % 4, :]).then_inc(sem["finc"], 1)

        @block.tensor
        def _(pe):
            want = Tally()

            def take(name, by=1):
                pe.wait_ge(sem[name], want(sem[name], by))

            mm = lambda out, lhsT, rhs, start=True, stop=True: pe.matmul(out, lhsT, rhs, start=start, stop=stop, skip_group_check=True)
            tr = lambda out, x: pe.transpose(out, x, con[0:x.shape[0], at["ident"][0]:at["ident"][0] + x.shape[0]])

            def stream(l, kind, c=0):
                _, _, _, n0, blocks, kts, nd = seg(l, kind, c)
                xh, xl = (ah, al) if kind == "down" else (hh, hl)

                def pair(i, first):
                    for j in range(2):
                        pe.wait_ge(sem["wl"], 2 * i + (n0 + j + 1))
                        if not (first and n0 == 0):
                            pe.wait_ge(sem["ev"], 2 * i + (n0 + j - 1))
                        for k in range(kts):
                            mm(PS[:, j, 0:TOK], wh[j][:, k], xh[:, k], k == 0, False)
                            mm(PS[:, j, 0:TOK], wh[j][:, k], xl[:, k], False, False)
                            a = mm(PS[:, j, 0:TOK], wl[j][:, k], xh[:, k], False, k == kts - 1)
                        a.then_inc(sem["mm"], 1)
                pair(0, True)
                if blocks > 2:
                    with pe.Fori(1, blocks // 2) as i:
                        pair(i, False)

            def token_sums():
                take("ssum")
                mm(PS[:, 2, 0:TOK], C("ones"), ssum[:]).then_inc(sem["nmm"], 1)

            def bank2(b, h, nt):
                return PS[0:nt, b + h // 4, (h % 4) * nt:(h % 4 + 1) * nt]

            def head(x, h, nt):
                return x[0:nt, h * nt:(h + 1) * nt]

            def rwkv(l):
                take("shc")
                tr(PS[0:126, 2, 0:P], shc[:].rearrange("p b k -> p (b k)")).then_inc(sem["sht"], 1)
                pe.wait_ge(sem["lora"], 64 * (l + 1))
                take("shrc")
                take("sg")
                for f in range(4):
                    a = mm(PS[:, f, 0:TOK], lora[0][:, f * P:(f + 1) * P], th12[:])
                a.then_inc(sem["z"], 1)
                for f in range(4):
                    mm(PS[:, 4 + f, 0:TOK], lora[1][:, f * P:(f + 1) * P], xm[:, 12], True, False)
                    a = mm(PS[:, 4 + f, 0:TOK], lora[2][:, f * P:(f + 1) * P], xm[:, 13], False, True)
                a.then_inc(sem["aa"], 1)
                take("zexp")
                for f in range(4):
                    a = mm(PS[:, f, 0:TOK], lora[3][:, f * P:(f + 1) * P], sg13[:])
                a.then_inc(sem["g"], 1)

                def head_sums(x, b0, name):
                    for f in range(4):
                        a = mm(PS[:, b0 + f, 0:TOK], C("headones"), x[:, f])
                    a.then_inc(sem[name], 1)
                take("ksq")
                take("aexp")
                head_sums(e1, 4, "kss")
                take("rkp")
                take("gc")
                head_sums(e1, 0, "rks")
                take("abkr")
                pe.wait_ge(sem["s0"], 16 * 16 * (l + 1))
                for r in range(8):
                    if r >= 4:
                        pe.wait_ge(sem["stc"], 8 * l + r - 3)
                    for f in range(4):
                        a = tr(PS[:, 4 + r % 4, f * P:(f + 1) * P], S0in[:, r, f])
                    a.then_inc(sem["st"], 1)
                take("bon")
                pe.wait_ge(sem["stc"], 8 * l + 8)
                for tau in range(3):
                    c0, nt = tau * P, P if tau < 2 else NS
                    cols = slice(c0, c0 + nt)
                    for q, x in enumerate((xm[:, 8:12], dA, dB, dK)):
                        for f in range(4):
                            a = tr(PS[0:nt, q, f * P:(f + 1) * P], x[:, f, cols])
                        a.then_inc(sem["tok"], 1)
                    take("exd")
                    def gram(b, x, y):
                        for f in range(4):
                            a = mm(PS[0:nt, b + f // 2, (f % 2) * 2 * nt:(f % 2 + 1) * 2 * nt], x[:, f, cols],
                                   y[:, f, :, 0:nt])
                        a.then_inc(sem["G"], 1)
                    gram(4, dB, eA)
                    gram(6, dA, eB)
                    take("tokc", 4)
                    gram(0, dK, eA)
                    gram(2, dB, eR)
                    take("Gc")
                    gram(4, dK, eR)
                    levels = LEVELS if tau < 2 else LEVELS[:2]
                    for size in levels:
                        take("et")
                        for h in range(8):
                            a = mm(bank2(6, h, nt), head(ET, h, nt), head(TT, h, nt))
                        a.then_inc(sem["Z"], 1)
                        take("Zc")
                        for h in range(8):
                            mm(bank2(0, h, nt), head(WT, h, nt), head(ZZ, h, nt))
                        for h in range(8):
                            a = mm(bank2(2, h, nt), head(ZZ, h, nt), head(WT, h, nt))
                        a.then_inc(sem["TZ"], 1)
                        take("TW")
                    for h in range(8):
                        r = slice(h % 2 * HD, h % 2 * HD + HD)
                        a = mm(PS[r, 4, (h // 2) * nt:(h // 2 + 1) * nt], at_[0:nt, h * HD:(h + 1) * HD], head(WT, h, nt))
                    a.then_inc(sem["TA"], 1)
                    for h in range(8):
                        a = mm(PS[0:nt, 5, h * HD:(h + 1) * HD], head(NTm, h, nt), vt[0:nt, h * HD:(h + 1) * HD])
                    a.then_inc(sem["NV"], 1)
                    take("NVc")
                    for h in range(8):
                        a = mm(PS[0:nt, 6, h * HD:(h + 1) * HD], head(WT, h, nt), nvs[0:nt, h * HD:(h + 1) * HD])
                    a.then_inc(sem["TNV"], 1)
                    take("TAc")
                    ybank = lambda f, a0, a1: PS[:, 0, f * nt + a0:f * nt + a1]
                    if tau < 2:
                        for c in range(2):
                            r = slice(c * HD, c * HD + HD)
                            if tau or c:
                                take("SP")
                            for f in range(4):
                                a = mm(PS[r, 7, f * P:(f + 1) * P], tat[:, f * P + c * HD:f * P + c * HD + HD], S0P[:, f])
                            a.then_inc(sem["U"], 1)
                            for f in range(4):
                                mm(ybank(f, c * HD, c * HD + HD), S0P[:, f], dR[:, f, c0 + c * HD:c0 + c * HD + HD], c == 0 and f == 0, False)
                            take("Uc")
                            for f in range(4):
                                fc = slice(f * P, (f + 1) * P)
                                mm(PS[:, 1, fc], bt[r, fc], uu[r, fc], True, False)
                                a = mm(PS[:, 1, fc], kt_[r, fc], vt[r, fc], False, True)
                            a.then_inc(sem["Sm"], 1)
                        if tau == 1:
                            take("SP")
                    else:
                        for f in range(4):
                            for b in range(NB):
                                a = mm(PS[:, 7, f * nt + b * TS:f * nt + (b + 1) * TS], S0T[:, b, f], tat[:, f * nt + b * TS:f * nt + (b + 1) * TS])
                        a.then_inc(sem["U1"], 1)
                        for f in range(4):
                            for b in range(NB):
                                mm(ybank(f, b * TS, (b + 1) * TS), S0T[:, b, f], dR[:, f, c0 + b * TS:c0 + (b + 1) * TS], f == 0 and b == 0, False)
                        take("U1c")
                        for f in range(4):
                            a = tr(PS[0:NS, 1, f * P:(f + 1) * P], u1s[:, f])
                        a.then_inc(sem["U"], 1)
                        take("Uc")
                    for h in range(8):
                        out = PS[h % 2 * HD:h % 2 * HD + HD, 0, (h // 2) * nt:(h // 2 + 1) * nt]
                        mm(out, uu[0:nt, h * HD:(h + 1) * HD], head(RBm, h, nt), False, False)
                        a = mm(out, vt[0:nt, h * HD:(h + 1) * HD], head(RKm, h, nt), False, True)
                    a.then_inc(sem["Y"], 1)
                    take("Yc")
                for f in range(4):
                    take("ux")
                    for h2 in range(2):
                        hc = slice((2 * f + h2) * HD, (2 * f + h2 + 1) * HD)
                        out = PS[h2 * HD:h2 * HD + HD, 2 + f % 2, :]
                        mm(out, bt[0:NS, hc], ux[:, h2].rearrange("p b i -> p (b i)"), True, False)
                        a = mm(out, kt_[0:NS, hc], vx[:, h2].rearrange("p b i -> p (b i)"), False, True)
                    a.then_inc(sem["Se"], 1)
                take("SF", 4)
                for r in range(9):
                    if r >= 4:
                        pe.wait_ge(sem["Soc"], 9 * l + r - 3)
                    for f in range(4):
                        a = tr(PS[:, 4 + r % 4, f * P:(f + 1) * P], S0T[:, r, f] if r < 8 else S0P[:, f])
                    a.then_inc(sem["So"], 1)
                head_sums(yy, 0, "gn")
                take("ysq")
                head_sums(e1, 0, "gv")

            def attention(l):
                take("rw")
                tiles = list(range(QA, VA)) + list(range(QC, VC))
                for u, tile in enumerate(tiles):
                    if u >= 4:
                        pe.wait_ge(sem["rotc"], len(tiles) * l + u - 3)
                    mm(PS[:, 4 + u % 4, 0:TOK], C("rot"), pT[:, tile]).then_inc(sem["rot"], 1)
                take("qbd")
                for q in range(9):
                    if q >= 6:
                        pe.wait_ge(sem["kvc"], 9 * l + q - 5)
                    t0 = (0, P, TOK - P)[q // 3]
                    for i, tile in enumerate([range(KA, KA + 4), range(VA, VA + 4), (KC, VC)][q % 3]):
                        a = tr(PS[:, q % 6, i * P:(i + 1) * P], pT[:, tile, t0:t0 + P])
                    a.then_inc(sem["kv"], 1)
                pe.wait_ge(sem["kvc"], 9 * l + 9)
                for u in range(24 + 2):
                    if u < 24:
                        qt, kt = (QA + u // 2, KA + u // 2) if u < 8 else (QC + (u - 8) // 2, KC)
                        rows = slice(u % 2 * HD, u % 2 * HD + HD)
                        if u >= 2:
                            pe.wait_ge(sem["sm"], 24 * l + u - 1)
                        mm(PS[:, u % 2, 0:P], pT[rows, qt, 0:P], pT[rows, kt, 0:P])
                        mm(PS[:, u % 2, P:384], pT[rows, qt, P:SEQ], pT[rows, kt, 0:SEQ]).then_inc(sem["S"], 1)
                    if 1 <= u <= 24:
                        v = u - 1
                        if v >= 2:
                            pe.wait_ge(sem["ptc"], 24 * l + v - 1)
                        take("pn")
                        x = psm[v % 2]
                        for i in range(3):
                            a = tr(PS[:, 2 + v % 2, i * P:(i + 1) * P], x[:, i * P:(i + 1) * P])
                        a.then_inc(sem["PT"], 1)
                    if u >= 2:
                        v = u - 2
                        r = slice(v % 2 * HD, v % 2 * HD + HD)
                        vals = tk[1][:, :, (v * HD):(v + 1) * HD] if v < 8 else tk[2][:, :, P + v % 2 * HD:P + (v % 2 + 1) * HD]
                        pe.wait_ge(sem["ptc"], 24 * l + v + 1)
                        if v >= 2:
                            pe.wait_ge(sem["oc"], 24 * l + v - 1)
                        mm(PS[r, 4 + v % 2, 0:SEQ], vals[:, 0, :], ppt[v % 2][:, 0:SEQ], True, False)
                        mm(PS[r, 4 + v % 2, P:SEQ], vals[:, 1, :], ppt[v % 2][:, SEQ:384], False, True).then_inc(sem["O"], 1)
                pe.wait_ge(sem["oc"], 24 * (l + 1))
                for b in range(NB):
                    g = NB * l + b
                    n = g // 2 if DEPTH * NB % 2 == 0 else 0
                    pe.wait_ge(sem[f"cache{b % 2}"], 16 * CACHE_DMAS * (n + 1))
                    if b:
                        pe.wait_ge(sem["smb"], g)

                    def turn(kt):
                        if kt < 10:
                            for f in range(4):
                                a = tr(PS[:, 2 + kt % 3, f * P:(f + 1) * P], cK[b % 2][:, kt, f * P:(f + 1) * P])
                        else:
                            a = tr(PS[:, 3, 0:P], ckc[b % 2][:])
                        a.then_inc(sem["ktp"], 1)

                    def score(kt):
                        pe.wait_ge(sem["ktc"], 11 * g + kt + 1)
                        if kt < 10:
                            for f in range(4):
                                a = mm(PS[:, kt // 8, (kt % 8) * 64 + f * 16:(kt % 8) * 64 + (f + 1) * 16], ktr[kt % 3][:, f], qdA[:, b, f].rearrange("p h t -> p (h t)"))
                        else:
                            a = mm(PS[:, 1, P:2 * P], kct[:], qdC[:, b].rearrange("p k i t -> p (k i t)"))
                        a.then_inc(sem["sc"], 1)
                    turn(0)
                    turn(1)
                    for kt in range(11):
                        if kt + 2 < 11:
                            if kt:
                                pe.wait_ge(sem["ktc"], 11 * g + kt)
                            turn(kt + 2)
                        score(kt)
                    for f in range(4):
                        mm(PS[:, 1, 256 + f * 16:256 + (f + 1) * 16], pT[:, KA + f, TOK - P:TOK], qdA[:, b, f].rearrange("p h t -> p (h t)"))
                    mm(PS[:, 1, 320:448], pT[:, KC, TOK - P:TOK], qdC[:, b].rearrange("p k i t -> p (k i t)")).then_inc(sem["bS"], 1)
                    x = sms[b % 2]
                    take("mxt")
                    tr(PS[:, 5, 0:P], mx[:, 0:P])
                    tr(PS[0:64, 5, P:2 * P], mx[:, P:192]).then_inc(sem["bc"], 1)
                    take("dgm")
                    mm(PS[:, 6, 0:P], C("ones"), dg[:, 0:P])
                    mm(PS[:, 6, P:192], C("ones", 64), dg[0:64, P:192]).then_inc(sem["bc"], 1)
                    take("dnm")
                    mm(PS[:, 6, 0:192], C("ones"), dn[:]).then_inc(sem["bsum"], 1)
                    if b:
                        pe.wait_ge(sem["bo"], g)
                    for f in range(4):
                        for kt in range(11):
                            v = cV[b % 2][:, kt, f * P:(f + 1) * P] if kt < 10 else tk[1][:, 2, f * P:(f + 1) * P]
                            o = kt * 64 if kt < 10 else 768
                            mm(PS[:, 7, f * 16:(f + 1) * 16], v, x[:, o + f * 16:o + (f + 1) * 16], kt == 0, kt == 10)
                    mm(PS[:, 7, 64:192], cvc[b % 2][:], x[:, 640:768], True, False)
                    mm(PS[:, 7, 64:192], tk[2][:, 2, P:2 * P], x[:, 832:960], False, True).then_inc(sem["bpv"], 1)

            pe.wait_ge(sem["con"], 16)
            pe.wait_ge(sem["x"], 48)
            for q in range(12):
                tau, k0 = q // 4, q % 4 * 4
                nt = P if tau < 2 else NS
                if q >= 4:
                    pe.wait_ge(sem["xtc"], q - 3)
                for k in range(4):
                    a = tr(PS[:, 2 + q % 4, k * nt:(k + 1) * nt], xin[0:nt, tau, (k0 + k) * P:(k0 + k + 1) * P])
                a.then_inc(sem["xtr"], 1)
            pe.wait_ge(sem["xtc"], 12)
            for l in range(DEPTH):
                pe.wait_ge(sem["par"], 16 * 13 * (l + 1))
                tr(PS[:, 6, 0:N_PAR], prow[:])
                tr(PS[:, 7, 0:NB * 14], srow[:]).then_inc(sem["part"], 1)
                token_sums()
                pe.wait_ge(sem["hl"], 8 * l + 4)
                stream(l, "in")
                stream(l, "inq")
                stream(l, "inkv")
                pe.wait_ge(sem["ev"], start_of(l, "out"))
                rwkv(l)
                attention(l)
                pe.wait_ge(sem["mix"], 4 * l + 4)
                stream(l, "out")
                token_sums()
                pe.wait_ge(sem["hl"], 8 * l + 8)
                for c in range(NCH):
                    stream(l, "gu", c)
                    pe.wait_ge(sem["act"], 5 * FC * (l * NCH + c + 1))
                    stream(l, "down", c)
            token_sums()
            pe.wait_ge(sem["ht"], 8 * DEPTH + 1)
            for q in range(12):
                tau, k0 = q // 4, q % 4 * 4
                nt = P if tau < 2 else NS
                if q >= 4:
                    pe.wait_ge(sem["finc"], q - 3)
                for k in range(4):
                    a = tr(PS[0:nt, q % 4, k * P:(k + 1) * P], xT[:, k0 + k, tau * P:tau * P + nt])
                a.then_inc(sem["fint"], 1)


_OUTS = [
    ("y_prompt", (1, SEQ, D)), ("y_sample", (NB, TS, D)),
    ("new_a_k_prompt", (DEPTH, 1, SEQ, 8, HD)), ("new_a_v_prompt", (DEPTH, 1, SEQ, 8, HD)),
    ("new_c_k_prompt", (DEPTH, 1, P, 2, HD)), ("new_c_v_prompt", (DEPTH, 1, P, 2, HD)),
    ("new_wkv_prompt", (DEPTH, 1, 8, HD, HD)), ("new_shift_prompt", (DEPTH, 1, B_COLS)),
    ("new_a_k_sample", (DEPTH, NB, TS, 8, HD)), ("new_a_v_sample", (DEPTH, NB, TS, 8, HD)),
    ("new_c_k_sample", (DEPTH, NB, TS, 2, HD)), ("new_c_v_sample", (DEPTH, NB, TS, 2, HD)),
    ("new_wkv_sample", (DEPTH, NB, 8, HD, HD)), ("new_shift_sample", (DEPTH, NB, B_COLS)),
]


def kernel(**inputs):
    import concourse.bacc as bacc
    from concourse.bass_utils import run_bass_kernel_spmd

    nc = bacc.Bacc("TRN2", target_bir_lowering=False, num_devices=1)
    con, at = constants()
    arrays = {"in_con": con}
    handles = {"con": nc.dram_tensor("in_con", con.shape, F32, kind="ExternalInput").ap()}
    for name, a in inputs.items():
        a = np.ascontiguousarray(a)
        arrays[f"in_{name}"] = a
        handles[name] = nc.dram_tensor(f"in_{name}", a.shape, mybir.dt.from_np(a.dtype), kind="ExternalInput").ap()
    outs = {n: nc.dram_tensor(f"out_{n}", s, F32, kind="ExternalOutput").ap() for n, s in _OUTS}
    build(nc, handles, outs, at)
    r = run_bass_kernel_spmd(nc, [arrays], core_ids=[0])
    return tuple(r.results[0][f"out_{n}"] for n, _ in _OUTS)
```

```python
import math
from contextlib import ExitStack

import numpy as np

import concourse.bass as bass
from concourse import mybir

ALU = mybir.AluOpType
ACT = mybir.ActivationFunctionType
AX_X = mybir.AxisListType.X
F32 = mybir.dt.float32
F32R = mybir.dt.float32r

P = 128
D = 2048
DEPTH = 2
SEQ = 256
NB = 8
TS = 8
NS = NB * TS
TOK = SEQ + NS
KT = D // P
HD = 64
DFF = 5632
FC = 11
NCH = DFF // P // FC
PAST = 2048
B_COLS = 1792
LORA_W, LORA_A, LORA_G = 96, 96, 64
SCALE = HD ** -0.5
NEG = -1.0e30
DECAY = -math.exp(-0.5)
QA, KA, VA, BR, QC, KC, VC = 0, 4, 8, 12, 26, 34, 35
NP_TILES = 36
G_MIX, G_FFN, MU, W0, A0, KK, KA_, RK_, LNW, LNB, G_FIN, N_PAR = 0, 16, 32, 46, 50, 54, 58, 62, 66, 70, 74, 90
LEVELS = (2, 4, 8, 16, 32)
FFN = [("gu", 0)] + [x for c in range(1, NCH) for x in (("gu", c), ("down", c - 1))] + [("down", NCH - 1)]


def constants():
    parts, at = [], {}

    def put(name, a):
        a = np.asarray(a, np.float64).reshape(a.shape[0], -1)
        full = np.zeros((P, a.shape[1]))
        full[:a.shape[0]] = a
        at[name] = (sum(x.shape[1] for x in parts), a.shape[1])
        parts.append(full)

    p = np.arange(P)
    put("ident", np.eye(P))
    put("ones", np.ones((P, P)))
    put("headones", (p[:, None] // HD == p[None, :] // HD) * 1.0)
    rot = np.zeros((P, P))
    for m in range(P):
        d = m % HD
        if d < 8:
            rot[m + 8, m] = -1.0
        elif d < 16:
            rot[m - 8, m] = 1.0
    put("rot", rot)
    pos = np.concatenate([np.arange(SEQ), np.tile(PAST + np.arange(TS), NB)]).astype(np.float32)
    inv = np.exp(np.float32(-math.log(500000.0)) * np.arange(8, dtype=np.float32) * np.float32(2.0) / np.float32(16)).astype(np.float32)
    ang = (pos[None, :] * inv[:, None]).astype(np.float32).astype(np.float64)
    cos, sin = np.ones((P, TOK)), np.zeros((P, TOK))
    for m in range(P):
        if m % HD < 16:
            cos[m], sin[m] = np.cos(ang[m % 8]), np.sin(ang[m % 8])
    put("cos", cos)
    put("sin", sin)

    def branches(dist):
        n = ((dist >= 0) & (dist <= 128)) * 1 + ((dist >= 0) & (dist <= 512) & (dist % 4 == 0)) * 1
        n = n + ((dist >= 0) & (dist <= 2048) & (dist % 16 == 0)) * 1
        return np.where(n > 0, np.log(np.maximum(n, 1)), NEG)

    def window(dist):
        return np.where((dist >= 0) & (dist <= 128), 0.0, NEG)

    k = np.arange(SEQ)
    for name, f in (("maskA", branches), ("maskC", window)):
        put(name, np.concatenate([f(p[:, None] - k[None, :P]), f(P + p[:, None] - k[None, :])], 1))
    t = p % TS
    rows = [(kt * 16 + p // 8) * 16 + p % 8 for kt in range(6)] + [PAST - 512 + 4 * p + kt for kt in range(4)]
    put("oldA", np.concatenate([branches(PAST + t[:, None] - r[None, :]) for r in rows], 1))
    put("oldC", window(P + t[:, None] - p[None, :]))
    key = np.arange(NS)
    dist = t[:, None] - key[None, :] % TS

    def own_of(seq, f):
        return np.where(seq == key[None, :] // TS, f(dist), NEG)

    put("newA", np.concatenate([own_of(2 * q + p[:, None] // 64, branches) for q in range(NB // 2)], 1))
    put("newC", np.concatenate([own_of(b + 0 * p[:, None], window) for b in range(NB)], 1))
    put("headof", (p[:, None] % 64 // TS == np.arange(8)[None, :]) * 1.0)
    put("selA", (p[:, None] // 64 * TS + t[:, None] == np.arange(16)[None, :]) * 1.0)
    put("selC", (p[:, None] % 64 == np.arange(64)[None, :]) * 1.0)
    s, c = p[:, None], p[None, :]

    def pair(size):
        return ((s // (2 * size) == c // (2 * size)) & (s // size % 2 == 0) & (c // size % 2 == 1)) * 1.0

    put("negE1T", -pair(1))
    put("negE1", -pair(1).T)
    for size in LEVELS:
        put(f"lev{size}", pair(size))
    for name, size in (("P", 64), ("S", TS)):
        put("strict" + name, ((s // size == c // size) & (s < c)) * 1.0)
        put("incl" + name, ((s // size == c // size) & (s <= c)) * 1.0)
    put("own", (np.arange(NS)[:, None] // TS == np.arange(NB)[None, :]) * 1.0)
    return np.concatenate(parts, 1).astype(np.float32), at


class Tally:

    def __init__(self):
        self.n = {}

    def __call__(self, sem, by=1):
        self.n[id(sem)] = self.n.get(id(sem), 0) + by
        return self.n[id(sem)]


def segments():
    out, n = [], 0
    for l in range(DEPTH):
        for kind, c, blocks, kt, nd in (
            [("in", 0, 26, KT, 1), ("inq", 0, 8, KT, 2), ("inkv", 0, 2, KT, 1), ("out", 0, 16, KT, 3)]
            + [(kind, c, 2 * FC, KT, 1) if kind == "gu" else (kind, c, 16, FC, 1) for kind, c in FFN]
        ):
            out.append((l, kind, c, n, blocks, kt, nd))
            n += blocks
    return out


def build(nc, I, O, at):
    ctx = ExitStack()
    with ctx:
        base = [16512]

        def region(size):
            o = base[0]
            base[0] += size
            return o

        def place(name, shape, offset, dt=F32):
            return nc.alloc_sbuf_tensor_at(name, shape, dt, offset=offset)

        ncon = max(o + n for o, n in at.values())
        RX, RC, RP, RH, RW = region(20480), region(ncon * 4), region(46080), region(40960), region(49152)
        RS, RM = region(31744), region(1440)

        xT = place("xT", [P, KT, TOK], RX)
        con = place("con", [P, ncon], RC)
        par = place("par", [P, N_PAR], RM)
        npar = place("npar", [P, 8], RM + 384)
        shf = place("shf", [P, NB, 14], RM + 416)
        shc = place("shc", [P, 9, 14], RM + 864)
        sink = place("sink", [P, 16], RM + 1376)
        pT = place("pT", [P, NP_TILES, TOK], RP)
        hh = place("hh", [P, KT, TOK], RH, F32R)
        hl = place("hl", [P, KT, TOK], RH + 20480, F32R)
        sq = place("sq", [P, KT, TOK], RH + 20480)
        raw = [place(f"raw{i}", [P, KT, P], RW + 8192 * i) for i in range(2)]
        wh = [place(f"wh{i}", [P, KT, P], RW + 16384 + 8192 * i, F32R) for i in range(2)]
        wl = [place(f"wl{i}", [P, KT, P], RW + 32768 + 8192 * i, F32R) for i in range(2)]
        ah = [place(f"ah{i}", [P, FC, TOK], (RP, RS)[i], F32R) for i in range(2)]
        al = [place(f"al{i}", [P, FC, TOK], (RP, RS)[i] + 14080, F32R) for i in range(2)]
        ge = place("ge", [P, TOK], RP + 28160)
        gt = place("gt", [P, TOK], RP + 29440)
        ga = place("ga", [P, TOK], RP + 30720)
        ht = [place(f"ht{i}", [P, 4, TOK], RP + 32000 + 5120 * i) for i in range(2)]
        ssum = place("ssum", [P, TOK], RP + 42240)
        rsb = place("rsb", [P, TOK], RP + 43520)
        prow = place("prow", [N_PAR, P], RP)
        srow = place("srow", [NB * 14, P], RP + 512)
        xin = place("xin", [P, 3, D], RH)
        yout = [place(f"yout{i}", [P, D], RW + 8192 * i) for i in range(3)]
        xm = place("xm", [P, 14, TOK], RH)
        lw = place("lw", [P, 4, TOK], RH + 17920)
        cl = place("cl", [P, 4, TOK], RH + 23040)
        aa = place("aa", [P, 4, TOK], RH + 28160)
        kk = place("kk", [P, 4, TOK], RH + 33280)
        th12 = place("th12", [P, TOK], RH + 38400)
        sg13 = place("sg13", [P, TOK], RH + 39680)
        S0T = place("S0T", [P, NB, 4, P], RH + 17920)
        RKm = place("RKm", [P, 1024], RH + 34304)
        dA, dB, dK, dR, gg, e1, e2, yy = (place(n, [P, 4, TOK], RW + 5120 * i) for i, n in enumerate(
            ("dA", "dB", "dK", "dR", "gg", "e1", "e2", "yy")))
        vt, at_, bt, kt_ = (place(n, [P, 512], RW + 25600 + 2048 * i) for i, n in enumerate(("vt", "at_", "bt", "kt_")))
        S0P = place("S0P", [P, 4, P], RW + 40960)
        uu, tnv, nvs = (place(n, [P, 512], RW + 43008 + 2048 * i) for i, n in enumerate(("uu", "tnv", "nvs")))
        eA, eB, eR = (place(n, [P, 4, 2, P], RP + 20480 + 4096 * i) for i, n in enumerate(("eA", "eB", "eR")))
        mkb = [place(f"mk{i}", [P, NB * (P + TS) + HD], RP + 20480 + 4608 * i) for i in range(2)]
        mk = [m[:, 0:NB * P].rearrange("p (b c) -> p b c", b=NB) for m in mkb]
        mkd = [[m[:, j * HD:j * HD + NB * (P + TS)].rearrange("p (b c) -> p b c", b=NB) for j in range(2)] for m in mkb]
        pc = place("pc", [P, 4, 12], RP + 20480 + 12288)
        MT, WT, TT, ET, ZZ, NTm, RBm = (place(n, [P, 1024], RS + 4096 * i) for i, n in enumerate(
            ("MT", "WT", "TT", "ET", "ZZ", "NTm", "RBm")))
        tat = place("tat", [P, 512], RS + 28672)
        lora = [place(f"lora{i}", [P, 512], RS + 2048 * i) for i in range(4)]
        S0in = place("S0in", [P, NB, 4, P], RS + 8192)
        ux, vx = ([place(f"{n}{j}", [NS, 2, NB, HD], RS + (12288, 0)[j] + 4096 * i) for j in range(2)] for i, n in enumerate(("ux", "vx")))
        Sout = place("Sout", [P, NB, 4, HD], RS)
        SoutP = place("SoutP", [P, 4, HD], RS + 8192)
        stmp = place("stmp", [P, 512], RS + 20480)
        shr = place("shr", [126, P], RW + 35840)
        cK = [place(f"cK{i}", [P, 10, 512], RH if i == 0 else RW) for i in range(2)]
        cV = [place(f"cV{i}", [P, 10, 512], (RH if i == 0 else RW) + 20480) for i in range(2)]
        ktr = [place(f"ktr{i}", [P, 512], RW + 40960 + 2048 * i) for i in range(3)]
        omC = place("omC", [P, 2, P], RW + 47104)
        q0 = RP + 20480
        qdA = [place(f"qdA{i}", [P, 4, 2, 64], q0 + 2048 * i) for i in range(2)]
        qdC = [place(f"qdC{i}", [P, 2, 2, 8, TS], q0 + 4096 + 1024 * i) for i in range(2)]
        ckc = [place(f"ckc{i}", [P, P], q0 + 6144 + 512 * i) for i in range(2)]
        cvc = [place(f"cvc{i}", [P, P], q0 + 7168 + 512 * i) for i in range(2)]
        ptC = place("ptC", [P, 2, 2, P], q0 + 8192)
        om = place("om", [P, 512], q0 + 10240)
        tk = [place(f"tk{i}", [P, 3, n], RS + o) for i, (n, o) in enumerate(((512, 0), (512, 6144), (256, 12288)))]
        ptA = place("ptA", [P, 11, P], RS)
        smA = [place(f"smA{i}", [P, 1344], RS + 15360 + 5376 * i) for i in range(2)]
        smC = [place(f"smC{i}", [P, 2, 192], RS + 26112 + 1536 * i) for i in range(2)]
        psm = [place(f"psm{i}", [P, 384], RS + 15360 + 1536 * i) for i in range(3)]
        ppt = [place(f"ppt{i}", [P, 384], RS + 19968 + 1536 * i) for i in range(2)]
        rt = [place(f"rt{i}", [P, 2, TOK], RS + 15360 + 2560 * i) for i in range(2)]
        nm = [place(f"nm{i}", [P, 2], RS + 29184 + 64 * i) for i in range(3)]
        sums = [place(f"sums{i}", [P, 2], RS + 29376 + 64 * i) for i in range(3)]
        psk = [place(f"psk{i}", [P, 2], RS + 29568 + 64 * i) for i in range(3)]
        snm = [place(f"snm{i}", [P, 3], RS + 29760 + 64 * i) for i in range(2)]
        ssu = [place(f"ssu{i}", [P, 3], RS + 29888 + 64 * i) for i in range(2)]
        ssk = [place(f"ssk{i}", [P, 2], RS + 30016 + 64 * i) for i in range(2)]
        snk = place("snk", [P, 1], RS + 30144)

        PS = ctx.enter_context(nc.psum_tensor("PS", [P, 8, 512], F32))

        def C(name, rows=P, cols=None):
            o, n = at[name]
            return con[0:rows, o:o + (cols or n)]

        ident = C("ident")
        names = """con con2 x par lora s0 cK0 cK1 cV0 cV1 w0 w1 wh wl mm ev gexp al
            xtr xtc sq ssum nmm ht hh hl part parc
            zero xm shc sht shrc th sg z aa zexp aexp g gc ksq kss rkp rks clr expd abkr bon st stc
            tok tokc exd G Gc et Z Zc TZ TW TA TAc NV NVc TNV U Y0 Uc Sm SP Y Yc mz mk U1 U1c ux Se SF So Soc
            gn ysq gv vr sd rw rot rotc kv kvc qz qbd
            S sm nmx pex pn PT ptc O oc
            rope snk ktp ktc sc bS smb bnm bex pt2 ptd pv1 om sel bo mix dve act fin fint finc out souts pool""".split()
        sem = {n: ctx.enter_context(nc.semaphore("s_" + n)) for n in names}
        segs = segments()
        block = ctx.enter_context(nc.Block())

        landed, count = {}, 0
        for (l, kind, c, n0, blocks, kts, nd) in segs:
            landed[n0] = count
            count += 16 * nd * (blocks // 2)

        def start_of(l, kind, c=0):
            return next(x[3] for x in segs if x[:3] == (l, kind, c))

        def seg(l, kind, c=0):
            return next(x for x in segs if x[:3] == (l, kind, c))

        layer_first = [start_of(l, "in") for l in range(DEPTH)]
        CACHE_DMAS = 8
        QUADS = ((0, 4), (4, 4), (8, 2))

        @block.sync
        def _(sp):
            want = Tally()
            outs = Tally()

            def load(j, l, kind, c, b):
                r = raw[j]
                inc = sem[f"w{j}"]
                if kind in ("in", "inkv"):
                    w = I["w_in"][l].rearrange("(k p) n -> p k n", p=P)
                    c0 = 0 if kind == "in" else KC * P
                    sp.dma_start(r[:], w[:, :, bass.ds(b * P + c0, P)]).then_inc(inc, 16)
                elif kind == "inq":
                    w = I["w_in"][l].rearrange("(k p) n -> p k n", p=P)
                    for half in range(2):
                        sp.dma_start(r[:, :, half * HD:(half + 1) * HD],
                                     w[:, :, bass.ds(b * HD + (QC * P + half * 512), HD)]).then_inc(inc, 16)
                elif kind == "out":
                    w = I["w_out"][l]
                    sp.dma_start(r[:, 0:8], w[0:1024].rearrange("(k p) n -> p k n", p=P)[:, :, bass.ds(b * P, P)]).then_inc(inc, 16)
                    for half in range(2):
                        rows = w[1024 + 512 * half:1536 + 512 * half].rearrange("(k p) n -> p k n", p=HD)
                        sp.dma_start(r[half * HD:(half + 1) * HD, 8:16], rows[:, :, bass.ds(b * P, P)]).then_inc(inc, 16)
                elif kind == "down":
                    w = I["w_down"][l][c * FC * P:(c + 1) * FC * P].rearrange("(k p) n -> p k n", p=P)
                    sp.dma_start(r[:, 0:FC], w[:, :, bass.ds(b * P, P)]).then_inc(inc, 16)

            def load_gu(j, l, c, i):
                w = I["w_gate" if j == 0 else "w_up"][l].rearrange("(k p) n -> p k n", p=P)
                sp.dma_start(raw[j][:], w[:, :, bass.ds(i * P + c * FC * P, P)]).then_inc(sem[f"w{j}"], 16)

            def stream(l, kind, c=0):
                _, _, _, n0, blocks, kts, nd = seg(l, kind, c)

                def pair(i, first):
                    for j in range(2):
                        if not (first and n0 == 0):
                            sp.wait_ge(sem["wl"], 2 * i + (n0 + j - 1))
                        load_gu(j, l, c, i) if kind == "gu" else load(j, l, kind, c, 2 * i + j)
                pair(0, True)
                if blocks > 2:
                    with sp.Fori(1, blocks // 2) as i:
                        pair(i, False)

            sp.dma_start(con[:, 0:P], I["con"][:, 0:P]).then_inc(sem["con"], 16)
            for q in range(2):
                sp.dma_start(xin[:, q, :], I["x_prompt"][0, q * P:(q + 1) * P, :]).then_inc(sem["x"], 16)
            sp.dma_start(xin[0:NS, 2, :], I["x_sample"].rearrange("b t d -> (b t) d")).then_inc(sem["x"], 16)
            sp.dma_start(con[:, P:ncon], I["con"][:, P:ncon]).then_inc(sem["con2"], 16)
            for l in range(DEPTH):
                if l:
                    sp.wait_ge(sem["ev"], layer_first[l])
                for name, r0, n in (("g_mix", G_MIX, 16), ("g_ffn", G_FFN, 16), ("b_mu", MU, 14), ("b_w0", W0, 4),
                                    ("b_a0", A0, 4), ("b_k_k", KK, 4), ("b_k_a", KA_, 4), ("b_r_k", RK_, 4),
                                    ("b_lnx_w", LNW, 4), ("b_lnx_b", LNB, 4)):
                    sp.dma_start(prow[r0:r0 + n, :], I[name][l].rearrange("(r c) -> r c", c=P)).then_inc(sem["par"], 16)
                sp.dma_start(prow[G_FIN:G_FIN + 16, :], I["g_final"].rearrange("(r c) -> r c", c=P)).then_inc(sem["par"], 16)
                sp.dma_start(srow[:], I["state_b_shift"][l].rearrange("b (r c) -> (b r) c", c=P)).then_inc(sem["par"], 16)
                sp.dma_start(sink[:], I["c_sink"][l].rearrange("k g -> (k g)").rearrange("(o n) -> o n", o=1).broadcast_to([P, 16])).then_inc(sem["par"], 16)
                sp.wait_ge(sem["zero"], 2 * l + 1)
                sp.dma_start(lora[0][0:LORA_W, :], I["b_w2"][l]).then_inc(sem["lora"], 16)
                sp.dma_start(lora[1][96:128, :], I["b_a2"][l][0:32]).then_inc(sem["lora"], 16)
                sp.dma_start(lora[2][0:64, :], I["b_a2"][l][32:96]).then_inc(sem["lora"], 16)
                sp.dma_start(lora[3][64:128, :], I["b_g2"][l]).then_inc(sem["lora"], 16)
                for b in range(NB):
                    for h2 in range(2):
                        sp.dma_start(S0in[h2 * HD:(h2 + 1) * HD, b, :, h2 * HD:(h2 + 1) * HD],
                                     I["state_b_wkv"][l, b].rearrange("(f h) i j -> h i f j", h=2)[h2]).then_inc(sem["s0"], 16)
                stream(l, "in")
                stream(l, "inq")
                stream(l, "inkv")
                sp.wait_ge(sem["shrc"], l + 1)
                sp.dma_start(O["new_shift_prompt"][l, 0].rearrange("(r c) -> r c", c=P), shr[0:14, :]).then_inc(sem["out"], 16)
                sp.dma_start(O["new_shift_sample"][l].rearrange("b (r c) -> (b r) c", c=P), shr[14:126, :]).then_inc(sem["out"], 16)
                sp.wait_ge(sem["Soc"], 9 * l + 9)
                for h2 in range(2):
                    for b in range(NB):
                        sp.dma_start(O["new_wkv_sample"][l, b].rearrange("(f h) i j -> h i f j", h=2)[h2],
                                     Sout[h2 * HD:(h2 + 1) * HD, b]).then_inc(sem["souts"], 16)
                    sp.dma_start(O["new_wkv_prompt"][l, 0].rearrange("(f h) i j -> h i f j", h=2)[h2],
                                 SoutP[h2 * HD:(h2 + 1) * HD]).then_inc(sem["souts"], 16)

                def cache(b, which):
                    s = sem[f"c{which}{b % 2}"]
                    dst, small = (cK, ckc) if which == "K" else (cV, cvc)
                    rows = I["cache_a_" + which.lower()][l, b].rearrange("r h d -> r (h d)")
                    old = rows[0:1536].rearrange("(n g r) c -> n g r c", n=6, r=16)
                    for n in range(6):
                        sp.dma_start(dst[b % 2][:, n, :], old[n, :, 0:8, :]).then_inc(s, 16)
                    sp.dma_start(dst[b % 2][:, 6:10, :], rows[1536:2048].rearrange("(p r) c -> p r c", p=P)).then_inc(s, 16)
                    sp.dma_start(small[b % 2][:], I["cache_c_" + which.lower()][l, b].rearrange("r h d -> r (h d)")).then_inc(s, 16)

                sp.wait_ge(sem["rw"], l + 1)
                for which in "KV":
                    cache(0, which)
                    cache(1, which)
                sp.wait_ge(sem["kvc"], 9 * (l + 1))
                sp.dma_start(snk[:], I["c_sink"][l].rearrange("k g -> (k g)").unsqueeze(1).unsqueeze(2).broadcast_to([16, TS, 1])).then_inc(sem["snk"], 16)
                for q in range(2):
                    rows = slice(q * P, (q + 1) * P)
                    sp.dma_start(O["new_a_k_prompt"][l, 0, rows].rearrange("t h d -> t (h d)"), tk[0][:, q, :]).then_inc(sem["out"], 16)
                    sp.dma_start(O["new_a_v_prompt"][l, 0, rows].rearrange("t h d -> t (h d)"), tk[1][:, q, :]).then_inc(sem["out"], 16)
                sp.dma_start(O["new_c_k_prompt"][l, 0].rearrange("t h d -> t (h d)"), tk[2][:, 1, 0:P]).then_inc(sem["out"], 16)
                sp.dma_start(O["new_c_v_prompt"][l, 0].rearrange("t h d -> t (h d)"), tk[2][:, 1, P:2 * P]).then_inc(sem["out"], 16)
                for name, src in (("new_a_k_sample", tk[0][0:NS, 2, :]), ("new_a_v_sample", tk[1][0:NS, 2, :]),
                                  ("new_c_k_sample", tk[2][0:NS, 2, 0:P]), ("new_c_v_sample", tk[2][0:NS, 2, P:2 * P])):
                    sp.dma_start(O[name][l].rearrange("b t h d -> (b t) (h d)"), src).then_inc(sem["out"], 16)

                def next_keys(b):
                    sp.wait_ge(sem["sc"], 13 * (NB * l + b - 1))
                    cache(b, "K")

                def next_values(b):
                    sp.wait_ge(sem["pv1"], NB * l + b - 1)
                    cache(b, "V")
                for b in (2, 3, 4, 5):
                    next_keys(b)
                for b in (2, 3):
                    next_values(b)
                for b in (6, 7):
                    next_keys(b)
                for b in (4, 5, 6, 7):
                    next_values(b)
                sp.wait_ge(sem["out"], 16 * 12 * (l + 1))
                sp.wait_ge(sem["souts"], 16 * 18 * (l + 1))
                sp.wait_ge(sem["sc"], 13 * NB * (l + 1))
                stream(l, "out")
                for kind, c in FFN:
                    stream(l, kind, c)
            for q in range(3):
                sp.wait_ge(sem["finc"], 4 * (q + 1))
                if q < 2:
                    sp.dma_start(O["y_prompt"][0, q * P:(q + 1) * P, :], yout[q][:]).then_inc(sem["fin"], 16)
                else:
                    sp.dma_start(O["y_sample"].rearrange("b t d -> (b t) d"), yout[2][0:NS, :]).then_inc(sem["fin"], 16)
            sp.wait_ge(sem["fin"], 48)
            sp.wait_ge(sem["out"], 16 * 12 * DEPTH)
            sp.wait_ge(sem["souts"], 16 * 18 * DEPTH)

        @block.gpsimd
        def _(pool):
            for l in range(DEPTH):
                if l:
                    pool.wait_ge(sem["ev"], layer_first[l])
                for i in range(4):
                    pool.memset(lora[i][:], 0.0)
                pool.memset(S0in[:], 0.0).then_inc(sem["zero"], 1)
                pool.wait_ge(sem["xm"], l + 1)
                pool.memset(S0P[:], 0.0)
                pool.memset(eA[:], 0.0)
                pool.memset(eB[:], 0.0)
                pool.memset(eR[:], 0.0).then_inc(sem["zero"], 1)
                pool.wait_ge(sem["G"], 15 * (l + 1))
                pool.memset(mkb[0][:], 0.0)
                pool.memset(mkb[1][:], 0.0).then_inc(sem["mz"], 1)
                pool.wait_ge(sem["rw"], l + 1)
                for i in range(2):
                    pool.memset(qdA[i][:], 0.0)
                    z = pool.memset(qdC[i][:], 0.0)
                z.then_inc(sem["qz"], 1)
                pool.wait_ge(sem["qz"], l + 1)
                pool.wait_ge(sem["rope"], l + 1)
                for q in range(NB // 2):
                    if q >= 2:
                        pool.wait_ge(sem["bS"], 4 * l + q - 1)
                    o = SEQ + 2 * TS * q
                    for h2 in range(2):
                        rows = slice(h2 * HD, h2 * HD + HD)
                        for f in range(4):
                            c0 = (2 * f + h2) * TS
                            pool.tensor_copy(qdA[q % 2][rows, f, :, c0:c0 + TS], pT[rows, QA + f, o:o + 2 * TS].rearrange("p (b t) -> p b t", b=2))
                        for b2 in range(2):
                            a = pool.tensor_copy(qdC[q % 2][rows, b2, h2], pT[rows, QC:QC + 8, o + b2 * TS:o + b2 * TS + TS])
                    a.then_inc(sem["qbd"], 1)

        @block.scalar
        def _(act):
            want = Tally()

            def take(name, by=1):
                act.wait_ge(sem[name], want(sem[name], by))

            def split(n0, i, j, kts, nd):
                act.wait_ge(sem[f"w{j}"], 16 * nd * i + (landed[n0] + 16 * nd))
                if not (n0 == 0 and isinstance(i, int) and i == 0):
                    act.wait_ge(sem["mm"], 2 * i + (n0 + j - 1))
                act.activation(wh[j][:, 0:kts], raw[j][:, 0:kts], ACT.Copy).then_inc(sem["wh"], 1)

            def stream(l, kind, c=0, ready=False, ahead=None):
                _, _, _, n0, blocks, kts, nd = seg(l, kind, c)
                if not ready:
                    split(n0, 0, 0, kts, nd)

                def pair(i, last):
                    split(n0, i, 1, kts, nd)
                    if kind == "gu":
                        act.wait_ge(sem["mm"], 2 * i + (n0 + 1))
                        act.activation(ge[:], PS[:, 0, 0:TOK], ACT.Exp, scale=-1.0).then_inc(sem["gexp"], 1)
                    if not last:
                        split(n0, i + 1, 0, kts, nd)
                    elif ahead:
                        _, _, _, m0, _, k2, d2 = seg(*ahead)
                        split(m0, 0, 0, k2, d2)
                if blocks > 2:
                    with act.Fori(0, blocks // 2 - 1) as i:
                        pair(i, False)
                pair(blocks // 2 - 1, True)

            def squares():
                act.activation(sq[:], xT[:], ACT.Square).then_inc(sem["sq"], 1)

            def root(x):
                take("vr")
                act.activation(x[:], x[:], ACT.Sqrt).then_inc(sem["sd"], 1)

            def hi_parts():
                root(rsb)
                for g in range(4):
                    take("ht")
                    act.activation(hh[:, 4 * g:4 * g + 4], ht[g % 2][:], ACT.Copy).then_inc(sem["hh"], 1)

            for q in range(12):
                take("xtr")
                nt = P if q < 8 else NS
                tau, k0 = q // 4, q % 4 * 4
                act.activation(xT[:, k0:k0 + 4, tau * P:tau * P + nt],
                               PS[:, 2 + q % 4, 0:4 * nt].rearrange("p (k t) -> p k t", k=4), ACT.Copy).then_inc(sem["xtc"], 1)
            act.wait_ge(sem["xtc"], 12)
            for l in range(DEPTH):
                if l:
                    act.wait_ge(sem["ev"], layer_first[l])
                squares()
                hi_parts()
                stream(l, "in", ahead=(l, "inq"))
                stream(l, "inq", ready=True, ahead=(l, "inkv"))
                stream(l, "inkv", ready=True)
                take("xm")
                act.activation(th12[:], xm[:, 12, :], ACT.Tanh).then_inc(sem["th"], 1)
                act.activation(sg13[:], xm[:, 13, :], ACT.Exp, scale=-1.0).then_inc(sem["th"], 1)
                take("z")
                for f in range(4):
                    a = act.activation(e1[:, f], PS[:, f, 0:TOK], ACT.Exp, scale=-1.0, bias=npar[:, f:f + 1])
                a.then_inc(sem["zexp"], 1)
                take("aa")
                for f in range(4):
                    a = act.activation(e2[:, f], PS[:, 4 + f, 0:TOK], ACT.Exp, scale=-1.0, bias=npar[:, 4 + f:5 + f])
                a.then_inc(sem["aexp"], 1)
                take("g")
                act.activation(gg[:], PS[:, 0:4, 0:TOK], ACT.Copy).then_inc(sem["gc"], 1)
                root(e2)
                take("clr", 2)
                act.activation(dR[:], cl[:], ACT.Exp)
                act.activation(dK[:], cl[:], ACT.Exp, scale=-1.0)
                act.activation(dA[:], dA[:], ACT.Exp).then_inc(sem["expd"], 1)
                for r in range(8):
                    take("st")
                    act.activation(S0T[:, r], PS[:, 4 + r % 4, :].rearrange("p (f i) -> p f i", f=4), ACT.Copy).then_inc(sem["stc"], 1)
                for tau in range(3):
                    nt = P if tau < 2 else NS
                    for q, dst in enumerate((vt, at_, bt, kt_)):
                        take("tok")
                        act.activation(dst[0:nt, :], PS[0:nt, q, :], ACT.Copy).then_inc(sem["tokc"], 1)
                    for size in LEVELS if tau < 2 else LEVELS[:2]:
                        for hf in range(2):
                            take("Z")
                            act.activation(ZZ[0:nt, hf * 4 * nt:(hf + 1) * 4 * nt], PS[0:nt, 6 + hf, 0:4 * nt], ACT.Copy).then_inc(sem["Zc"], 1)
                    take("TA")
                    act.activation(tat[:, 0:4 * nt], PS[:, 4, 0:4 * nt], ACT.Copy).then_inc(sem["TAc"], 1)
                take("U1", 4)
                act.activation(nvs[NS:2 * NS, :], PS[NS:2 * NS, 7, :], ACT.Copy).then_inc(sem["U1c"], 1)
                for r in range(9):
                    take("So")
                    for h2 in range(2):
                        rows, cols = slice(h2 * HD, h2 * HD + HD), slice(h2 * HD, h2 * HD + HD)
                        src = PS[rows, 4 + r % 4, :].rearrange("p (f j) -> p f j", f=4)[:, :, cols]
                        dst = Sout[rows, r] if r < 8 else SoutP[rows]
                        a = act.activation(dst, src, ACT.Copy)
                    a.then_inc(sem["Soc"], 1)
                root(e1)
                act.wait_ge(sem["souts"], 16 * 18 * (l + 1))
                for q in range(9):
                    take("kv")
                    n = 512 if q % 3 < 2 else 256
                    nt = P if q < 6 else NS
                    act.activation(tk[q % 3][0:nt, q // 3, :], PS[0:nt, q % 6, 0:n], ACT.Copy).then_inc(sem["kvc"], 1)
                for u in range(24 + 3):
                    if u < 24:
                        take("nmx")
                        for q in range(2):
                            cols = slice(0, P) if q == 0 else slice(P, 384)
                            a = act.activation(psm[u % 3][:, cols], psm[u % 3][:, cols], ACT.Exp,
                                               bias=nm[u % 3][:, q:q + 1], accum_out=sums[u % 3][:, q:q + 1])
                        if u >= 8:
                            h = (u - 8) // 2 + 8 * (u % 2)
                            a = act.activation(psk[u % 3][:], nm[u % 3][:], ACT.Exp, bias=sink[:, h:h + 1])
                        a.then_inc(sem["pex"], 1)
                    if 2 <= u < 26:
                        v = u - 2
                        take("PT")
                        if v >= 2:
                            act.wait_ge(sem["O"], 24 * l + v - 1)
                        act.activation(ppt[v % 2][:], PS[:, 2 + v % 2, 0:384], ACT.Copy).then_inc(sem["ptc"], 1)
                    if u >= 3:
                        v = u - 3
                        par2 = v % 2
                        tile = QA + v // 2 if v < 8 else QC + (v - 8) // 2
                        take("O")
                        rows = slice(par2 * HD, par2 * HD + HD)
                        act.activation(pT[rows, tile, 0:SEQ], PS[rows, 4 + par2, 0:SEQ], ACT.Copy).then_inc(sem["oc"], 1)
                def key_tiles(q):
                    for b in (2 * q, 2 * q + 1):
                        for m in range(13):
                            n = QUADS[m // 4][1] * P if m < 12 else P
                            take("ktp")
                            if NB * l + b or m >= 3:
                                act.wait_ge(sem["sc"], 13 * (NB * l + b) + m - 2)
                            act.activation(ktr[m % 3 if m < 12 else 0][:, 0:n], PS[:, 4 + (13 * b + m) % 2, 0:n], ACT.Copy).then_inc(sem["ktc"], 1)

                def exps(q):
                    take("bnm")
                    i = q % 2
                    act.activation(smA[i][:], smA[i][:], ACT.Exp, bias=snm[i][:, 0:1], accum_out=ssu[i][:, 0:1])
                    for b2 in range(2):
                        act.activation(smC[i][:, b2], smC[i][:, b2], ACT.Exp, bias=snm[i][:, 1 + b2:2 + b2], accum_out=ssu[i][:, 1 + b2:2 + b2])
                    act.activation(ssk[i][:], snm[i][:, 1:3], ACT.Exp, bias=snk[:, 0:1]).then_inc(sem["bex"], 1)

                act.wait_ge(sem["snk"], 16 * (l + 1))
                key_tiles(0)
                exps(0)
                for q in range(NB // 2):
                    if q < NB // 2 - 1:
                        key_tiles(q + 1)
                    if q == 0:
                        act.wait_ge(sem["out"], 16 * 12 * (l + 1))
                    for r in range(4):
                        take("pt2")
                        bank = PS[:, 6 + r % 2, :].rearrange("p (k c) -> p k c", k=4)
                        if r < 2:
                            a = act.activation(ptA[:, 4 * r:4 * r + 4], bank, ACT.Copy)
                        elif r == 2:
                            act.activation(ptA[:, 8:10], bank[:, 0:2], ACT.Copy)
                            a = act.activation(ptA[0:NS, 10], bank[0:NS, 2], ACT.Copy)
                        else:
                            bank = PS[:, 7, :].rearrange("p (b k c) -> p b k c", b=2, k=2)
                            act.activation(ptC[:, :, 0], bank[:, :, 0], ACT.Copy)
                            a = act.activation(ptC[0:NS, :, 1], bank[0:NS, :, 1], ACT.Copy)
                        a.then_inc(sem["ptd"], 1)
                    if q < NB // 2 - 1:
                        exps(q + 1)
                act.wait_ge(sem["bo"], 4 * (l + 1))
                _, _, _, n0, _, kts, nd = seg(l, "out")
                split(n0, 0, 0, kts, nd)
                for g, t0 in enumerate((QA, BR, QC, QC + 4)):
                    act.activation(hh[:, 4 * g:4 * g + 4], pT[:, t0:t0 + 4], ACT.Copy).then_inc(sem["hh"], 1)
                stream(l, "out", ready=True)
                act.wait_ge(sem["ev"], start_of(l, "gu", 0))
                squares()
                hi_parts()
                for i, (kind, c) in enumerate(FFN):
                    stream(l, kind, c, ready=i > 0, ahead=(l, *FFN[i + 1]) if i + 1 < len(FFN) else None)
            act.wait_ge(sem["ev"], segs[-1][3] + segs[-1][4])
            squares()
            root(rsb)

        @block.vector
        def _(dve):
            want = Tally()

            def take(name, by=1):
                dve.wait_ge(sem[name], want(sem[name], by))

            def done(ins, name="dve"):
                ins.then_inc(sem[name], 1)
                dve.wait_ge(sem[name], want(sem[name]))

            tt, ts, stt = dve.tensor_tensor, dve.tensor_scalar, dve.scalar_tensor_tensor

            def split(n, j, kts):
                dve.wait_ge(sem["wh"], n + 1)
                tt(wl[j][:, 0:kts], raw[j][:, 0:kts], wh[j][:, 0:kts].bitcast(F32), ALU.subtract).then_inc(sem["wl"], 1)

            def stream(l, kind, c=0, ready=False, ahead=None):
                _, _, _, n0, blocks, kts, nd = seg(l, kind, c)
                tile0 = {"in": 0, "inq": QC, "inkv": KC}.get(kind, 0)
                if not ready:
                    split(n0, 0, kts)

                def drain(i, j):
                    if kind in ("in", "inq", "inkv"):
                        dve.wait_ge(sem["mm"], 2 * i + (n0 + j + 1))
                        dve.tensor_copy(pT[:, bass.ds(2 * i + (tile0 + j), 1), :].rearrange("p o t -> p (o t)"), PS[:, j, 0:TOK]).then_inc(sem["ev"], 1)
                    elif kind in ("out", "down"):
                        dve.wait_ge(sem["mm"], 2 * i + (n0 + j + 1))
                        x = xT[:, bass.ds(2 * i + j, 1), :].rearrange("p o t -> p (o t)")
                        tt(x, x, PS[:, j, 0:TOK], ALU.add).then_inc(sem["ev"], 1)
                    elif j == 0:
                        pairs = (l * NCH + c) * FC
                        dve.wait_ge(sem["gexp"], i + (pairs + 1))
                        ts(gt[:], ge[:], 1.0, None, ALU.add).then_inc(sem["act"], 1)
                        dve.wait_ge(sem["act"], 5 * (i + pairs) + 1)
                        dve.reciprocal(gt[:], gt[:]).then_inc(sem["act"], 1)
                        dve.wait_ge(sem["act"], 5 * (i + pairs) + 2)
                        tt(gt[:], gt[:], PS[:, 0, 0:TOK], ALU.mult).then_inc(sem["ev"], 1)
                    else:
                        pairs = (l * NCH + c) * FC
                        dve.wait_ge(sem["mm"], 2 * i + (n0 + 2))
                        dve.wait_ge(sem["ev"], 2 * i + (n0 + 1))
                        hi = ah[c % 2][:, bass.ds(i, 1), :].rearrange("p o t -> p (o t)")
                        lo = al[c % 2][:, bass.ds(i, 1), :].rearrange("p o t -> p (o t)")
                        tt(hi, gt[:], PS[:, 1, 0:TOK], ALU.mult).then_inc(sem["act"], 1)
                        tt(ga[:], gt[:], PS[:, 1, 0:TOK], ALU.mult).then_inc(sem["ev"], 1)
                        dve.wait_ge(sem["act"], 5 * (i + pairs) + 3)
                        dve.wait_ge(sem["ev"], 2 * i + (n0 + 2))
                        tt(lo, ga[:], hi.bitcast(F32), ALU.subtract).then_inc(sem["act"], 2)

                def pair(i, last):
                    split(2 * i + (n0 + 1), 1, kts)
                    drain(i, 0)
                    if not last:
                        split(2 * i + (n0 + 2), 0, kts)
                    elif ahead:
                        _, _, _, m0, _, k2, _ = seg(*ahead)
                        split(m0, 0, k2)
                    drain(i, 1)
                if blocks > 2:
                    with dve.Fori(0, blocks // 2 - 1) as i:
                        pair(i, False)
                pair(blocks // 2 - 1, True)
                dve.wait_ge(sem["ev"], n0 + blocks)

            def rms():
                take("sq")
                done(dve.tensor_reduce(ssum[:], sq[:].rearrange("p k t -> p t k"), AX_X, ALU.add), "ssum")
                take("nmm")
                done(ts(rsb[:], PS[:, 2, 0:TOK], 1.0 / D, 1e-6, ALU.mult, ALU.add), "vr")
                take("sd")
                done(dve.reciprocal(rsb[:], rsb[:]))

            def norm(g0):
                rms()

                def scaled(g):
                    for k in range(4):
                        a = stt(ht[g % 2][:, k], xT[:, 4 * g + k], par[:, g0 + 4 * g + k:g0 + 4 * g + k + 1], rsb[:], ALU.mult, ALU.mult)
                    done(a, "ht")
                scaled(0)
                scaled(1)
                for g in range(4):
                    take("hh")
                    done(tt(hl[:, 4 * g:4 * g + 4], ht[g % 2][:], hh[:, 4 * g:4 * g + 4].bitcast(F32), ALU.subtract), "hl")
                    if g < 2:
                        scaled(g + 2)

            def banks(b, nt):
                return PS[0:nt, b:b + 2, 0:4 * nt].rearrange("p b (h t) -> p b h t", h=4)

            def heads(x, nt):
                return x[0:nt, 0:8 * nt].rearrange("p (b h t) -> p b h t", b=2, h=4)

            def mask(name, nt):
                return C(name, nt, nt).unsqueeze(1).unsqueeze(1).broadcast_to([nt, 2, 4, nt])

            def halves():
                return [slice(0, HD), slice(HD, P)]

            def rwkv(l):
                pB = pT[:, BR:BR + 14]
                sam = lambda x: x[:, :, SEQ:TOK].rearrange("p k (b t) -> p k b t", b=NB)
                tt(xm[:, :, 1:SEQ], pB[:, :, 0:SEQ - 1], pB[:, :, 1:SEQ], ALU.subtract)
                ts(xm[:, :, 0:1], pB[:, :, 0:1], -1.0, None, ALU.mult)
                for b in range(NB):
                    o = SEQ + b * TS
                    tt(xm[:, :, o + 1:o + TS], pB[:, :, o:o + TS - 1], pB[:, :, o + 1:o + TS], ALU.subtract)
                tt(sam(xm[:])[:, :, :, 0], shf[:].rearrange("p b k -> p k b"), sam(pB)[:, :, :, 0], ALU.subtract)
                dve.tensor_copy(shc[:, 0, :], pB[:, :, SEQ - 1])
                done(dve.tensor_copy(shc[:, 1:9, :].rearrange("p b k -> p k b"), sam(pB)[:, :, :, TS - 1]), "shc")
                for k in range(14):
                    a = stt(xm[:, k], xm[:, k], par[:, MU + k:MU + k + 1], pB[:, k], ALU.mult, ALU.add)
                done(a, "xm")
                take("sht")
                done(dve.tensor_copy(shr[:], PS[0:126, 2, 0:P]), "shrc")
                take("th", 2)
                done(ts(sg13[:], sg13[:], 1.0, None, ALU.add))
                done(dve.reciprocal(sg13[:], sg13[:]), "sg")
                xr, xk, xv = xm[:, 0:4], xm[:, 4:8], xm[:, 8:12]
                col = lambda r, f: par[:, r + f:r + f + 1]
                for f in range(4):
                    a = ts(kk[:, f], xk[:, f], col(KK, f), None, ALU.mult)
                done(a)
                take("zexp")
                done(ts(e1[:], e1[:], 1.0, None, ALU.add))
                done(dve.reciprocal(e1[:], e1[:]))
                done(ts(lw[:], e1[:], DECAY, None, ALU.mult))
                done(tt(e1[:], kk[:], kk[:], ALU.mult), "ksq")
                take("aexp")
                done(ts(e2[:], e2[:], 1.0, None, ALU.add))
                done(dve.reciprocal(aa[:], e2[:]))
                take("kss")
                done(ts(e2[:], PS[:, 4:8, 0:TOK], 1e-24, None, ALU.max), "vr")
                take("sd")
                done(dve.reciprocal(e2[:], e2[:]))
                done(tt(kk[:], kk[:], e2[:], ALU.mult))
                for f in range(4):
                    a = ts(e2[:, f], aa[:, f], 1.0, col(KA_, f), ALU.subtract, ALU.mult)
                done(a)
                done(stt(xk, e2[:], 1.0, xk, ALU.add, ALU.mult))
                for f in range(4):
                    a = stt(e1[:, f], xr[:, f], col(RK_, f), xk[:, f], ALU.mult, ALU.mult)
                done(a, "rkp")
                pro = lambda x: x[:, :, 0:SEQ].rearrange("p f (c t) -> p f c t", t=HD)
                dve.tensor_copy(cl[:, :, 0:SEQ], lw[:, :, 0:SEQ])
                done(dve.tensor_copy(e2[:, :, SEQ:TOK], lw[:, :, SEQ:TOK]))
                for step in range(6):
                    s = 1 << step
                    for view, src, dst in ([(pro, cl, e2) if step % 2 == 0 else (pro, e2, cl)]
                                           + ([(sam, e2, cl) if step % 2 == 0 else (sam, cl, e2)] if step < 3 else [])):
                        x, y = view(src[:]), view(dst[:])
                        n = x.shape[3]
                        for f in range(4):
                            tt(y[:, f, :, s:n], x[:, f, :, s:n], x[:, f, :, 0:n - s], ALU.add)
                        a = dve.tensor_copy(y[:, :, :, 0:s], x[:, :, :, 0:s])
                    done(a, "clr" if step == 5 else "dve")
                done(tt(dA[:], cl[:], lw[:], ALU.subtract), "clr")
                done(tt(dB[:], kk[:], aa[:], ALU.mult))
                take("expd")
                dve.tensor_copy(pc[:, :, 0:4], dR[:, :, HD - 1:SEQ:HD])
                done(dve.tensor_copy(pc[:, :, 4:12], dR[:, :, SEQ + TS - 1:TOK:TS]))
                tt(dB[:], dB[:], dK[:], ALU.mult)
                tt(dA[:], dA[:], kk[:], ALU.mult)
                tt(dR[:], dR[:], xr, ALU.mult)
                done(tt(dK[:], dK[:], xk, ALU.mult), "abkr")
                take("rks")
                done(tt(xk, PS[:, 0:4, 0:TOK], xv, ALU.mult), "bon")
                dve.wait_ge(sem["zero"], 2 * l + 2)
                for tau in range(3):
                    c0, nt = tau * P, P if tau < 2 else NS
                    kind = "P" if tau < 2 else "S"
                    for x, y in ((dA, eA), (dB, eB), (dR, eR)):
                        for h2, rows in enumerate(halves()):
                            a = dve.tensor_copy(y[rows, :, h2, 0:nt], x[rows, :, c0:c0 + nt])
                    done(a, "exd")
                    take("G")
                    done(dve.tensor_copy(heads(MT, nt), banks(4, nt)), "Gc")
                    done(tt(heads(WT, nt), heads(MT, nt), mask("negE1T", nt), ALU.mult))
                    done(tt(heads(WT, nt), heads(WT, nt), mask("ident", nt), ALU.add))
                    take("G")
                    done(tt(heads(TT, nt), banks(6, nt), mask("negE1", nt), ALU.mult))
                    done(tt(heads(TT, nt), heads(TT, nt), mask("ident", nt), ALU.add))
                    take("G")
                    tt(heads(NTm, nt), banks(0, nt), mask("strict" + kind, nt), ALU.mult)
                    take("G")
                    tt(heads(RBm, nt), banks(2, nt), mask("incl" + kind, nt), ALU.mult)
                    take("G")
                    done(tt(heads(RKm, nt), banks(4, nt), mask("incl" + kind, nt), ALU.mult))
                    levels = LEVELS if tau < 2 else LEVELS[:2]
                    quad = lambda x, hf: x[0:nt, hf * 4 * nt:(hf + 1) * 4 * nt].rearrange("p (h t) -> p h t", h=4)
                    qbank = lambda b, hf: PS[0:nt, b + hf, 0:4 * nt].rearrange("p (h t) -> p h t", h=4)

                    def corner(size, hf):
                        m = C(f"lev{size}", nt, nt).unsqueeze(1).broadcast_to([nt, 4, nt])
                        done(tt(quad(ET, hf), quad(MT, hf), m, ALU.mult), "et")
                    corner(levels[0], 0)
                    corner(levels[0], 1)
                    for i, size in enumerate(levels):
                        last = i == len(levels) - 1
                        for hf in range(2):
                            take("TZ")
                            if not last:
                                tt(quad(TT, hf), quad(TT, hf), qbank(0, hf), ALU.subtract)
                            done(tt(quad(WT, hf), quad(WT, hf), qbank(2, hf), ALU.subtract), "TW")
                            if not last:
                                corner(levels[i + 1], hf)
                    take("NV")
                    done(dve.tensor_copy(nvs[0:nt, :], PS[0:nt, 5, :]), "NVc")
                    take("TNV")
                    done(dve.tensor_copy(tnv[0:nt, :], PS[0:nt, 6, :]))
                    for c in range(2) if tau < 2 else range(1):
                        r = slice(c * HD, c * HD + HD)
                        if tau < 2:
                            take("U")
                        else:
                            dve.wait_ge(sem["TAc"], 3 * (l + 1))
                            take("mz")
                            for f in range(4):
                                if f >= 2:
                                    dve.wait_ge(sem["U1"], 4 * l + f - 1)
                                dve.tensor_copy(mkd[f % 2][0][:, :, 0:TS], tat[:, f * NS:(f + 1) * NS].rearrange("p (b t) -> p b t", b=NB))
                                done(dve.tensor_copy(mkd[f % 2][1][:, :, 0:TS], dR[:, f, SEQ:TOK].rearrange("p (b t) -> p b t", b=NB)), "mk")
                            take("U1", 4)
                        done(stt(uu[r, :], PS[r, 7, :], -1.0, tnv[r, :], ALU.mult, ALU.subtract), "Uc")
                        if tau < 2:
                            take("Sm")
                            ps = PS[:, 1, :].rearrange("p (f i) -> p f i", f=4)
                            done(tt(S0P[:], S0P[:], ps, ALU.add))
                            ch = 2 * tau + c
                            done(tt(S0P[:], S0P[:], pc[:, :, ch:ch + 1].broadcast_to([P, 4, P]), ALU.mult))
                            done(tt(S0P[:], S0P[:], C("headones").unsqueeze(1).broadcast_to([P, 4, P]), ALU.mult), "SP")
                    take("Y")
                    if tau == 0:
                        dve.wait_ge(sem["out"], 16 * 12 * l + 32)
                    done(dve.tensor_copy(yy[:, :, c0:c0 + nt], PS[:, 0, 0:4 * nt].rearrange("p (f t) -> p f t", f=4)), "Yc")
                own = C("own", NS).unsqueeze(2).broadcast_to([NS, NB, HD])

                def expand(f):
                    for h2 in range(2):
                        cols = slice((2 * f + h2) * HD, (2 * f + h2 + 1) * HD)
                        tt(ux[f % 2][:, h2], uu[0:NS, cols].unsqueeze(1).broadcast_to([NS, NB, HD]), own, ALU.mult)
                        a = tt(vx[f % 2][:, h2], vt[0:NS, cols].unsqueeze(1).broadcast_to([NS, NB, HD]), own, ALU.mult)
                    done(a, "ux")
                expand(0)
                expand(1)
                for f in range(4):
                    take("Se")
                    for h2, rows in enumerate(halves()):
                        tmp = stmp[rows, :].rearrange("p (b i) -> p b i", b=NB)
                        s0 = S0T[rows, :, f, h2 * HD:h2 * HD + HD]
                        done(tt(tmp, s0, PS[rows, 2 + f % 2, :].rearrange("p (b i) -> p b i", b=NB), ALU.add))
                        a = tt(s0, tmp, pc[rows, f, 4:12].unsqueeze(2).broadcast_to([HD, NB, HD]), ALU.mult)
                    done(a, "SF")
                    if f < 2:
                        expand(f + 2)
                take("gn")
                done(ts(e1[:], PS[:, 0:4, 0:TOK], 1.0 / HD, None, ALU.mult))
                done(tt(yy[:], yy[:], e1[:], ALU.subtract))
                done(tt(e1[:], yy[:], yy[:], ALU.mult), "ysq")
                take("gv")
                done(ts(e1[:], PS[:, 0:4, 0:TOK], 1.0 / HD, 64e-5, ALU.mult, ALU.add), "vr")
                take("sd")
                done(dve.reciprocal(e1[:], e1[:]))
                done(tt(yy[:], yy[:], e1[:], ALU.mult))
                for f in range(4):
                    a = ts(yy[:, f], yy[:, f], col(LNW, f), col(LNB, f), ALU.mult, ALU.add)
                done(a)
                done(tt(yy[:], yy[:], xk, ALU.add))
                dve.wait_ge(sem["Soc"], 9 * (l + 1))
                done(tt(pT[:, BR:BR + 4], yy[:], gg[:], ALU.mult), "rw")

            def attention(l):
                for u, tile in enumerate(list(range(QA, VA)) + list(range(QC, VC))):
                    take("rot")
                    t1, t2 = rt[u % 2][:, 0], rt[u % 2][:, 1]
                    done(tt(t1, PS[:, 4 + u % 4, 0:TOK], C("sin"), ALU.mult), "rotc")
                    done(tt(t2, pT[:, tile], C("cos"), ALU.mult))
                    a = tt(pT[:, tile], t1, t2, ALU.add)
                done(a, "rope")
                for u in range(24 + 1):
                    if u < 24:
                        take("S")
                        x = psm[u % 3]
                        if u >= 3:
                            dve.wait_ge(sem["PT"], 24 * l + u - 2)
                        done(stt(x[:], PS[:, u % 2, 0:384], SCALE, C("maskA" if u < 8 else "maskC"), ALU.mult, ALU.add), "sm")
                        dve.tensor_reduce(nm[u % 3][:, 0:1], x[:, 0:P], AX_X, ALU.max, negate=True)
                        done(dve.tensor_reduce(nm[u % 3][:, 1:2], x[:, P:384], AX_X, ALU.max, negate=True), "nmx")
                    if u >= 1:
                        v = u - 1
                        take("pex")
                        if v >= 8:
                            done(tt(sums[v % 3][:], sums[v % 3][:], psk[v % 3][:], ALU.add))
                        done(dve.reciprocal(sums[v % 3][:], sums[v % 3][:]))
                        y = psm[v % 3]
                        ts(y[:, 0:P], y[:, 0:P], sums[v % 3][:, 0:1], None, ALU.mult)
                        done(ts(y[:, P:384], y[:, P:384], sums[v % 3][:, 1:2], None, ALU.mult), "pn")
                dve.wait_ge(sem["PT"], 24 * (l + 1))
                dve.wait_ge(sem["O"], 24 * (l + 1))

                def scores(q):
                    x, y, i = smA[q % 2], smC[q % 2], q % 2
                    take("bS")
                    if q >= 2:
                        dve.wait_ge(sem["pt2"], 4 * (4 * l + q - 1))
                    for k in range(3):
                        n = 512 if k < 2 else 256
                        stt(x[:, 512 * k:512 * k + n], PS[:, k, 0:n], SCALE, C("oldA")[:, 512 * k:512 * k + n], ALU.mult, ALU.add)
                    stt(x[:, 1280:1344], PS[:, 2, 256:320], SCALE, C("newA")[:, 64 * q:64 * q + 64], ALU.mult, ALU.add)
                    ps = PS[:, 3, 0:384].rearrange("p (b k) -> p b k", b=2)
                    stt(y[:, :, 0:P], ps[:, :, 0:P], SCALE, C("oldC").unsqueeze(1).broadcast_to([P, 2, P]), ALU.mult, ALU.add)
                    done(stt(y[:, :, P:192], ps[:, :, P:192], SCALE, C("newC")[:, 128 * q:128 * q + 128].rearrange("p (b k) -> p b k", b=2), ALU.mult, ALU.add), "smb")
                    dve.tensor_reduce(snm[i][:, 0:1], x[:], AX_X, ALU.max, negate=True)
                    done(dve.tensor_reduce(snm[i][:, 1:3], y[:], AX_X, ALU.max, negate=True), "bnm")

                def weighted(q):
                    i = q % 2
                    take("bex")
                    done(tt(ssu[i][:, 1:3], ssu[i][:, 1:3], ssk[i][:], ALU.add))
                    done(dve.reciprocal(ssu[i][:], ssu[i][:]))
                    take("pv1", 2)
                    v3 = lambda z: z.rearrange("p (h d) -> p h d", h=8)
                    stt(v3(om[:]), v3(PS[:, 6, :]), ssu[i][:, 0:1], C("headof").unsqueeze(2).broadcast_to([P, 8, HD]), ALU.mult, ALU.mult)
                    for b2 in range(2):
                        a = stt(omC[:, b2], PS[:, 7, b2 * P:(b2 + 1) * P], ssu[i][:, 1 + b2:2 + b2], C("headones"), ALU.mult, ALU.mult)
                    done(a, "om")

                def outputs(q):
                    take("sel")
                    o = SEQ + 2 * TS * q
                    dve.tensor_copy(pT[:, QA:QA + 4, o:o + 2 * TS], PS[:, 7, 256:320].rearrange("p (f t) -> p f t", f=4))
                    for b2 in range(2):
                        a = dve.tensor_copy(pT[:, QC:QC + 8, o + b2 * TS:o + b2 * TS + TS],
                                            PS[:, 7, 320 + 64 * b2:384 + 64 * b2].rearrange("p (i t) -> p i t", i=8))
                    done(a, "bo")
                scores(0)
                for q in range(NB // 2):
                    if q < NB // 2 - 1:
                        scores(q + 1)
                    if q:
                        outputs(q - 1)
                    weighted(q)
                outputs(NB // 2 - 1)
                split(start_of(l, "out"), 0, KT)
                for g, t0 in enumerate((QA, BR, QC, QC + 4)):
                    take("hh")
                    if g == 0:
                        dve.wait_ge(sem["oc"], 24 * (l + 1))
                    done(tt(hl[:, 4 * g:4 * g + 4], pT[:, t0:t0 + 4], hh[:, 4 * g:4 * g + 4].bitcast(F32), ALU.subtract), "mix")

            dve.wait_ge(sem["con2"], 16)
            for l in range(DEPTH):
                take("part")
                dve.tensor_copy(par[:], PS[:, 6, 0:N_PAR])
                done(dve.tensor_copy(shf[:].rearrange("p b k -> p (b k)"), PS[:, 7, 0:NB * 14]))
                done(ts(npar[:], par[:, W0:W0 + 8], -1.0, None, ALU.mult), "parc")
                if l == 0:
                    dve.wait_ge(sem["xtc"], 12)
                norm(G_MIX)
                stream(l, "in", ahead=(l, "inq"))
                stream(l, "inq", ready=True, ahead=(l, "inkv"))
                stream(l, "inkv", ready=True)
                rwkv(l)
                attention(l)
                stream(l, "out", ready=True)
                norm(G_FFN)
                for i, (kind, c) in enumerate(FFN):
                    stream(l, kind, c, ready=i > 0, ahead=(l, *FFN[i + 1]) if i + 1 < len(FFN) else None)
            rms()
            for k in range(KT):
                a = stt(xT[:, k], xT[:, k], par[:, G_FIN + k:G_FIN + k + 1], rsb[:], ALU.mult, ALU.mult)
            done(a, "ht")
            for q in range(12):
                tau, k0 = q // 4, q % 4 * 4
                nt = P if tau < 2 else NS
                take("fint")
                dve.tensor_copy(yout[tau][0:nt, k0 * P:(k0 + 4) * P], PS[0:nt, q % 4, :]).then_inc(sem["finc"], 1)

        @block.tensor
        def _(pe):
            want = Tally()

            def take(name, by=1):
                pe.wait_ge(sem[name], want(sem[name], by))

            mm = lambda out, lhsT, rhs, start=True, stop=True: pe.matmul(out, lhsT, rhs, start=start, stop=stop, skip_group_check=True)
            tr = lambda out, x: pe.transpose(out, x, con[0:x.shape[0], at["ident"][0]:at["ident"][0] + x.shape[0]])

            def stream(l, kind, c=0, inputs=0):
                _, _, _, n0, blocks, kts, nd = seg(l, kind, c)
                xh, xl = (ah[c % 2], al[c % 2]) if kind == "down" else (hh, hl)

                def pair(i, first):
                    for j in range(2):
                        pe.wait_ge(sem["wl"], 2 * i + (n0 + j + 1))
                        if not (first and n0 == 0):
                            pe.wait_ge(sem["ev"], 2 * i + (n0 + j - 1))
                        for k in range(kts):
                            if first and j == 0 and k % 4 == 0 and kind in ("in", "gu") and c == 0:
                                pe.wait_ge(sem["hl"], inputs + k // 4 + 1)
                            mm(PS[:, j, 0:TOK], wh[j][:, k], xh[:, k], k == 0, False)
                            mm(PS[:, j, 0:TOK], wh[j][:, k], xl[:, k], False, False)
                            a = mm(PS[:, j, 0:TOK], wl[j][:, k], xh[:, k], False, k == kts - 1)
                        a.then_inc(sem["mm"], 1)
                pair(0, True)
                if blocks > 2:
                    with pe.Fori(1, blocks // 2) as i:
                        pair(i, False)

            def token_sums():
                pe.wait_ge(sem["con2"], 16)
                take("ssum")
                mm(PS[:, 2, 0:TOK], C("ones"), ssum[:]).then_inc(sem["nmm"], 1)

            def bank2(b, h, nt):
                return PS[0:nt, b + h // 4, (h % 4) * nt:(h % 4 + 1) * nt]

            def head(x, h, nt):
                return x[0:nt, h * nt:(h + 1) * nt]

            def rwkv(l):
                take("shc")
                tr(PS[0:126, 2, 0:P], shc[:].rearrange("p b k -> p (b k)")).then_inc(sem["sht"], 1)
                pe.wait_ge(sem["lora"], 64 * (l + 1))
                take("shrc")
                take("sg")
                for f in range(4):
                    a = mm(PS[:, f, 0:TOK], lora[0][:, f * P:(f + 1) * P], th12[:])
                a.then_inc(sem["z"], 1)
                for f in range(4):
                    mm(PS[:, 4 + f, 0:TOK], lora[1][:, f * P:(f + 1) * P], xm[:, 12], True, False)
                    a = mm(PS[:, 4 + f, 0:TOK], lora[2][:, f * P:(f + 1) * P], xm[:, 13], False, True)
                a.then_inc(sem["aa"], 1)
                take("zexp")
                for f in range(4):
                    a = mm(PS[:, f, 0:TOK], lora[3][:, f * P:(f + 1) * P], sg13[:])
                a.then_inc(sem["g"], 1)

                def head_sums(x, b0, name):
                    for f in range(4):
                        a = mm(PS[:, b0 + f, 0:TOK], C("headones"), x[:, f])
                    a.then_inc(sem[name], 1)
                take("ksq")
                take("aexp")
                head_sums(e1, 4, "kss")
                take("rkp")
                take("gc")
                head_sums(e1, 0, "rks")
                take("abkr")
                pe.wait_ge(sem["s0"], 16 * 16 * (l + 1))
                for r in range(8):
                    if r >= 4:
                        pe.wait_ge(sem["stc"], 8 * l + r - 3)
                    for f in range(4):
                        a = tr(PS[:, 4 + r % 4, f * P:(f + 1) * P], S0in[:, r, f])
                    a.then_inc(sem["st"], 1)
                take("bon")
                pe.wait_ge(sem["stc"], 8 * l + 8)
                for tau in range(3):
                    c0, nt = tau * P, P if tau < 2 else NS
                    cols = slice(c0, c0 + nt)
                    for q, x in enumerate((xm[:, 8:12], dA, dB, dK)):
                        for f in range(4):
                            a = tr(PS[0:nt, q, f * P:(f + 1) * P], x[:, f, cols])
                        a.then_inc(sem["tok"], 1)
                    take("exd")
                    def gram(b, x, y):
                        for f in range(4):
                            a = mm(PS[0:nt, b + f // 2, (f % 2) * 2 * nt:(f % 2 + 1) * 2 * nt], x[:, f, cols],
                                   y[:, f, :, 0:nt])
                        a.then_inc(sem["G"], 1)
                    gram(4, dB, eA)
                    gram(6, dA, eB)
                    take("tokc", 4)
                    gram(0, dK, eA)
                    gram(2, dB, eR)
                    take("Gc")
                    gram(4, dK, eR)
                    levels = LEVELS if tau < 2 else LEVELS[:2]
                    for size in levels:
                        for hf in range(2):
                            take("et")
                            for h in range(4 * hf, 4 * hf + 4):
                                a = mm(bank2(6, h, nt), head(ET, h, nt), head(TT, h, nt))
                            a.then_inc(sem["Z"], 1)
                        for hf in range(2):
                            take("Zc")
                            if size != levels[-1]:
                                for h in range(4 * hf, 4 * hf + 4):
                                    mm(bank2(0, h, nt), head(WT, h, nt), head(ZZ, h, nt))
                            for h in range(4 * hf, 4 * hf + 4):
                                a = mm(bank2(2, h, nt), head(ZZ, h, nt), head(WT, h, nt))
                            a.then_inc(sem["TZ"], 1)
                    take("TW", 2 * len(levels))
                    for h in range(8):
                        r = slice(h % 2 * HD, h % 2 * HD + HD)
                        a = mm(PS[r, 4, (h // 2) * nt:(h // 2 + 1) * nt], at_[0:nt, h * HD:(h + 1) * HD], head(WT, h, nt))
                    a.then_inc(sem["TA"], 1)
                    for h in range(8):
                        a = mm(PS[0:nt, 5, h * HD:(h + 1) * HD], head(NTm, h, nt), vt[0:nt, h * HD:(h + 1) * HD])
                    a.then_inc(sem["NV"], 1)
                    take("NVc")
                    for h in range(8):
                        a = mm(PS[0:nt, 6, h * HD:(h + 1) * HD], head(WT, h, nt), nvs[0:nt, h * HD:(h + 1) * HD])
                    a.then_inc(sem["TNV"], 1)
                    take("TAc")
                    ybank = lambda f, a0, a1: PS[:, 0, f * nt + a0:f * nt + a1]
                    if tau < 2:
                        for c in range(2):
                            r = slice(c * HD, c * HD + HD)
                            if tau or c:
                                take("SP")
                            for f in range(4):
                                a = mm(PS[r, 7, f * P:(f + 1) * P], tat[:, f * P + c * HD:f * P + c * HD + HD], S0P[:, f])
                            a.then_inc(sem["U"], 1)
                            for f in range(4):
                                mm(ybank(f, c * HD, c * HD + HD), S0P[:, f], dR[:, f, c0 + c * HD:c0 + c * HD + HD], c == 0 and f == 0, False)
                            take("Uc")
                            for f in range(4):
                                fc = slice(f * P, (f + 1) * P)
                                mm(PS[:, 1, fc], bt[r, fc], uu[r, fc], True, False)
                                a = mm(PS[:, 1, fc], kt_[r, fc], vt[r, fc], False, True)
                            a.then_inc(sem["Sm"], 1)
                        if tau == 1:
                            take("SP")
                    else:
                        for f in range(4):
                            take("mk")
                            for b in range(NB):
                                a = mm(PS[:, 7, f * P:(f + 1) * P], mk[f % 2][:, b], S0T[:, b, f], b == 0, b == NB - 1)
                            a.then_inc(sem["U1"], 1)
                        take("U1c")
                        for f in range(4):
                            mm(ybank(f, 0, NS), nvs[NS:2 * NS, f * P:(f + 1) * P], ident[NS:2 * NS, NS:2 * NS], f == 0, False)
                        take("Uc")
                    for h in range(8):
                        out = PS[h % 2 * HD:h % 2 * HD + HD, 0, (h // 2) * nt:(h // 2 + 1) * nt]
                        mm(out, uu[0:nt, h * HD:(h + 1) * HD], head(RBm, h, nt), False, False)
                        a = mm(out, vt[0:nt, h * HD:(h + 1) * HD], head(RKm, h, nt), False, True)
                    a.then_inc(sem["Y"], 1)
                    take("Yc")
                for f in range(4):
                    take("ux")
                    for h2 in range(2):
                        hc = slice((2 * f + h2) * HD, (2 * f + h2 + 1) * HD)
                        out = PS[h2 * HD:h2 * HD + HD, 2 + f % 2, :]
                        mm(out, bt[0:NS, hc], ux[f % 2][:, h2].rearrange("p b i -> p (b i)"), True, False)
                        a = mm(out, kt_[0:NS, hc], vx[f % 2][:, h2].rearrange("p b i -> p (b i)"), False, True)
                    a.then_inc(sem["Se"], 1)
                take("SF", 4)
                for r in range(9):
                    if r >= 4:
                        pe.wait_ge(sem["Soc"], 9 * l + r - 3)
                    for f in range(4):
                        a = tr(PS[:, 4 + r % 4, f * P:(f + 1) * P], S0T[:, r, f] if r < 8 else S0P[:, f])
                    a.then_inc(sem["So"], 1)
                head_sums(yy, 0, "gn")
                take("ysq")
                head_sums(e1, 0, "gv")

            def attention(l):
                take("rw")
                tiles = list(range(QA, VA)) + list(range(QC, VC))
                for u, tile in enumerate(tiles):
                    if u >= 4:
                        pe.wait_ge(sem["rotc"], len(tiles) * l + u - 3)
                    mm(PS[:, 4 + u % 4, 0:TOK], C("rot"), pT[:, tile]).then_inc(sem["rot"], 1)
                take("rope")
                for q in range(9):
                    if q >= 6:
                        pe.wait_ge(sem["kvc"], 9 * l + q - 5)
                    t0, nt = q // 3 * P, P if q < 6 else NS
                    for i, tile in enumerate([range(KA, KA + 4), range(VA, VA + 4), (KC, VC)][q % 3]):
                        a = tr(PS[0:nt, q % 6, i * P:(i + 1) * P], pT[:, tile, t0:t0 + nt])
                    a.then_inc(sem["kv"], 1)
                pe.wait_ge(sem["kvc"], 9 * l + 9)
                for u in range(24 + 3):
                    if u < 24:
                        qt, kt = (QA + u // 2, KA + u // 2) if u < 8 else (QC + (u - 8) // 2, KC)
                        rows = slice(u % 2 * HD, u % 2 * HD + HD)
                        if u >= 2:
                            pe.wait_ge(sem["sm"], 24 * l + u - 1)
                        mm(PS[:, u % 2, 0:P], pT[rows, qt, 0:P], pT[rows, kt, 0:P])
                        mm(PS[:, u % 2, P:384], pT[rows, qt, P:SEQ], pT[rows, kt, 0:SEQ]).then_inc(sem["S"], 1)
                    if 2 <= u < 26:
                        v = u - 2
                        if v >= 2:
                            pe.wait_ge(sem["ptc"], 24 * l + v - 1)
                        take("pn")
                        x = psm[v % 3]
                        for i in range(3):
                            a = tr(PS[:, 2 + v % 2, i * P:(i + 1) * P], x[:, i * P:(i + 1) * P])
                        a.then_inc(sem["PT"], 1)
                    if u >= 3:
                        v = u - 3
                        r = slice(v % 2 * HD, v % 2 * HD + HD)
                        vals = tk[1][:, :, (v * HD):(v + 1) * HD] if v < 8 else tk[2][:, :, P + v % 2 * HD:P + (v % 2 + 1) * HD]
                        pe.wait_ge(sem["ptc"], 24 * l + v + 1)
                        if v >= 2:
                            pe.wait_ge(sem["oc"], 24 * l + v - 1)
                        mm(PS[r, 4 + v % 2, 0:SEQ], vals[:, 0, :], ppt[v % 2][:, 0:SEQ], True, False)
                        mm(PS[r, 4 + v % 2, P:SEQ], vals[:, 1, :], ppt[v % 2][:, SEQ:384], False, True).then_inc(sem["O"], 1)
                pe.wait_ge(sem["oc"], 24 * (l + 1))

                def keys(q):
                    take("qbd")
                    if q:
                        pe.wait_ge(sem["smb"], 4 * l + q)
                    for b in (2 * q, 2 * q + 1):
                        g, b2 = 13 * (NB * l + b), b % 2
                        pe.wait_ge(sem[f"cK{b2}"], 16 * CACHE_DMAS * (NB // 2 * l + q + 1))

                        def turn(m):
                            bank = PS[:, 4 + (13 * b + m) % 2, :]
                            if m >= 2 or b:
                                pe.wait_ge(sem["ktc"], g + m - 1)
                            if m < 12:
                                f, (k0, n) = m % 4, QUADS[m // 4]
                                for k in range(n):
                                    a = tr(bank[:, k * P:(k + 1) * P], cK[b2][:, k0 + k, f * P:(f + 1) * P])
                            else:
                                a = tr(bank[:, 0:P], ckc[b2][:])
                            a.then_inc(sem["ktp"], 1)

                        def score(m):
                            pe.wait_ge(sem["ktc"], g + m + 1)
                            if m < 12:
                                f, n = m % 4, QUADS[m // 4][1] * P
                                a = mm(PS[b2 * 64:b2 * 64 + 64, m // 4, 0:n], qdA[q % 2][:, f, b2], ktr[m % 3][:, 0:n], f == 0, f == 3)
                            else:
                                a = mm(PS[:, 3, b2 * 192:b2 * 192 + P], qdC[q % 2][:, b2].rearrange("p k i t -> p (k i t)"), ktr[0][:, 0:P])
                            a.then_inc(sem["sc"], 1)
                        turn(0)
                        turn(1)
                        for m in range(13):
                            if m + 2 < 13:
                                turn(m + 2)
                            score(m)
                    for f in range(4):
                        mm(PS[:, 2, 256:320], qdA[q % 2][:, f].rearrange("p b c -> p (b c)"), pT[:, KA + f, SEQ:TOK], f == 0, f == 3)
                    for b2 in range(2):
                        a = mm(PS[:, 3, b2 * 192 + P:b2 * 192 + 192], qdC[q % 2][:, b2].rearrange("p k i t -> p (k i t)"), pT[:, KC, SEQ:TOK])
                    a.then_inc(sem["bS"], 1)

                def values(q):
                    pe.wait_ge(sem["bex"], 4 * l + q + 1)
                    x, y = smA[q % 2], smC[q % 2]
                    for r in range(4):
                        if r >= 2:
                            pe.wait_ge(sem["ptd"], 4 * (4 * l + q) + r - 1)
                        elif r == 1 and q:
                            pe.wait_ge(sem["bo"], 4 * l + q)
                        bank = PS[:, 6 + r % 2, :].rearrange("p (k c) -> p k c", k=4)
                        if r < 3:
                            for k in range(4 * r, min(4 * r + 4, 11)):
                                n = P if k < 10 else NS
                                a = tr(bank[0:n, k % 4], x[:, k * P:k * P + n])
                        else:
                            for b2 in range(2):
                                tr(bank[:, 2 * b2], y[:, b2, 0:P])
                                a = tr(bank[0:NS, 2 * b2 + 1], y[:, b2, P:192])
                        a.then_inc(sem["pt2"], 1)
                    pe.wait_ge(sem["ptd"], 4 * (4 * l + q) + 4)
                    mm(PS[:, 6, :], ptA[0:NS, 10], tk[1][0:NS, 2, :], True, False)
                    for b2 in range(2):
                        pe.wait_ge(sem[f"cV{b2}"], 16 * CACHE_DMAS * (NB // 2 * l + q + 1))
                        mm(PS[:, 7, b2 * P:(b2 + 1) * P], ptC[:, b2, 0], cvc[b2][:], True, False)
                        mm(PS[:, 7, b2 * P:(b2 + 1) * P], ptC[0:NS, b2, 1], tk[2][0:NS, 2, P:2 * P], False, True)
                        for k in range(10):
                            a = mm(PS[b2 * 64:b2 * 64 + 64, 6, :], ptA[:, k, b2 * 64:b2 * 64 + 64], cV[b2][:, k, :], False, k == 9)
                        a.then_inc(sem["pv1"], 1)

                def select(q):
                    take("om")
                    for f in range(4):
                        mm(PS[:, 7, 256 + 16 * f:272 + 16 * f], om[:, f * P:(f + 1) * P], C("selA"))
                    for b2 in range(2):
                        a = mm(PS[:, 7, 320 + 64 * b2:384 + 64 * b2], omC[:, b2], C("selC"))
                    a.then_inc(sem["sel"], 1)
                keys(0)
                for q in range(NB // 2):
                    if q < NB // 2 - 1:
                        keys(q + 1)
                    if q:
                        select(q - 1)
                    values(q)
                select(NB // 2 - 1)

            pe.wait_ge(sem["con"], 16)
            pe.wait_ge(sem["x"], 48)
            for q in range(12):
                tau, k0 = q // 4, q % 4 * 4
                nt = P if tau < 2 else NS
                if q >= 4:
                    pe.wait_ge(sem["xtc"], q - 3)
                for k in range(4):
                    a = tr(PS[:, 2 + q % 4, k * nt:(k + 1) * nt], xin[0:nt, tau, (k0 + k) * P:(k0 + k + 1) * P])
                a.then_inc(sem["xtr"], 1)
            pe.wait_ge(sem["xtc"], 12)
            for l in range(DEPTH):
                pe.wait_ge(sem["par"], 16 * 13 * (l + 1))
                tr(PS[:, 6, 0:N_PAR], prow[:])
                tr(PS[:, 7, 0:NB * 14], srow[:]).then_inc(sem["part"], 1)
                token_sums()
                stream(l, "in", inputs=8 * l)
                stream(l, "inq")
                stream(l, "inkv")
                pe.wait_ge(sem["ev"], start_of(l, "out"))
                rwkv(l)
                attention(l)
                pe.wait_ge(sem["mix"], 4 * l + 4)
                stream(l, "out")
                token_sums()
                for i, (kind, c) in enumerate(FFN):
                    if kind == "down":
                        pe.wait_ge(sem["act"], 5 * FC * (l * NCH + c + 1))
                    stream(l, kind, c, inputs=0 if i else 8 * l + 4)
            token_sums()
            pe.wait_ge(sem["ht"], 8 * DEPTH + 1)
            for q in range(12):
                tau, k0 = q // 4, q % 4 * 4
                nt = P if tau < 2 else NS
                if q >= 4:
                    pe.wait_ge(sem["finc"], q - 3)
                for k in range(4):
                    a = tr(PS[0:nt, q % 4, k * P:(k + 1) * P], xT[:, k0 + k, tau * P:tau * P + nt])
                a.then_inc(sem["fint"], 1)


_OUTS = [
    ("y_prompt", (1, SEQ, D)), ("y_sample", (NB, TS, D)),
    ("new_a_k_prompt", (DEPTH, 1, SEQ, 8, HD)), ("new_a_v_prompt", (DEPTH, 1, SEQ, 8, HD)),
    ("new_c_k_prompt", (DEPTH, 1, P, 2, HD)), ("new_c_v_prompt", (DEPTH, 1, P, 2, HD)),
    ("new_wkv_prompt", (DEPTH, 1, 8, HD, HD)), ("new_shift_prompt", (DEPTH, 1, B_COLS)),
    ("new_a_k_sample", (DEPTH, NB, TS, 8, HD)), ("new_a_v_sample", (DEPTH, NB, TS, 8, HD)),
    ("new_c_k_sample", (DEPTH, NB, TS, 2, HD)), ("new_c_v_sample", (DEPTH, NB, TS, 2, HD)),
    ("new_wkv_sample", (DEPTH, NB, 8, HD, HD)), ("new_shift_sample", (DEPTH, NB, B_COLS)),
]


def kernel(**inputs):
    import concourse.bacc as bacc
    from concourse.bass_utils import run_bass_kernel_spmd

    nc = bacc.Bacc("TRN2", target_bir_lowering=False, num_devices=1)
    con, at = constants()
    arrays = {"in_con": con}
    handles = {"con": nc.dram_tensor("in_con", con.shape, F32, kind="ExternalInput").ap()}
    for name, a in inputs.items():
        a = np.ascontiguousarray(a)
        arrays[f"in_{name}"] = a
        handles[name] = nc.dram_tensor(f"in_{name}", a.shape, mybir.dt.from_np(a.dtype), kind="ExternalInput").ap()
    outs = {n: nc.dram_tensor(f"out_{n}", s, F32, kind="ExternalOutput").ap() for n, s in _OUTS}
    build(nc, handles, outs, at)
    r = run_bass_kernel_spmd(nc, [arrays], core_ids=[0])
    return tuple(r.results[0][f"out_{n}"] for n, _ in _OUTS)
```

```python
import math
from contextlib import ExitStack

import numpy as np

import concourse.bass as bass
from concourse import mybir

ALU = mybir.AluOpType
ACT = mybir.ActivationFunctionType
AX_X = mybir.AxisListType.X
F32 = mybir.dt.float32
F32R = mybir.dt.float32r

P = 128
D = 2048
DEPTH = 2
SEQ = 256
NB = 8
TS = 8
NS = NB * TS
TOK = SEQ + NS
KT = D // P
HD = 64
DFF = 5632
FC = 11
NCH = DFF // P // FC
PAST = 2048
B_COLS = 1792
LORA_W, LORA_A, LORA_G = 96, 96, 64
SCALE = HD ** -0.5
NEG = -1.0e30
DECAY = -math.exp(-0.5)
GN_EPS = 64e-5
QA, KA, VA, BR, QC, KC, VC = 0, 4, 8, 12, 26, 34, 35
NP_TILES = 36
G_MIX, G_FFN, MU, W0, A0, KK, KA_, RK_, LNW, LNB, G_FIN, N_PAR = 0, 16, 32, 46, 50, 54, 58, 62, 66, 70, 74, 90
LEVELS = (2, 4, 8, 16, 32)
FFN = [("gu", 0)] + [x for c in range(1, NCH) for x in (("gu", c), ("down", c - 1))] + [("down", NCH - 1)]


def constants():
    parts, at = [], {}

    def put(name, a):
        a = np.asarray(a, np.float64).reshape(a.shape[0], -1)
        full = np.zeros((P, a.shape[1]))
        full[:a.shape[0]] = a
        at[name] = (sum(x.shape[1] for x in parts), a.shape[1])
        parts.append(full)

    p = np.arange(P)
    put("ident", np.eye(P))
    put("ones", np.ones((P, P)))
    put("headones", (p[:, None] // HD == p[None, :] // HD) * 1.0)
    rot = np.zeros((P, P))
    for m in range(P):
        d = m % HD
        if d < 8:
            rot[m + 8, m] = -1.0
        elif d < 16:
            rot[m - 8, m] = 1.0
    put("rot", rot)
    pos = np.concatenate([np.arange(SEQ), np.tile(PAST + np.arange(TS), NB)]).astype(np.float32)
    inv = np.exp(np.float32(-math.log(500000.0)) * np.arange(8, dtype=np.float32) * np.float32(2.0) / np.float32(16)).astype(np.float32)
    ang = (pos[None, :] * inv[:, None]).astype(np.float32).astype(np.float64)
    cos, sin = np.ones((P, TOK)), np.zeros((P, TOK))
    for m in range(P):
        if m % HD < 16:
            cos[m], sin[m] = np.cos(ang[m % 8]), np.sin(ang[m % 8])
    put("cos", cos)
    put("sin", sin)

    def branches(dist):
        n = ((dist >= 0) & (dist <= 128)) * 1 + ((dist >= 0) & (dist <= 512) & (dist % 4 == 0)) * 1
        n = n + ((dist >= 0) & (dist <= 2048) & (dist % 16 == 0)) * 1
        return np.where(n > 0, np.log(np.maximum(n, 1)), NEG)

    def window(dist):
        return np.where((dist >= 0) & (dist <= 128), 0.0, NEG)

    k = np.arange(SEQ)
    for name, f in (("maskA", branches), ("maskC", window)):
        put(name, np.concatenate([f(p[:, None] - k[None, :P]), f(P + p[:, None] - k[None, :])], 1))
    t = p % TS
    rows = [(kt * 16 + p // 8) * 16 + p % 8 for kt in range(6)] + [PAST - 512 + 4 * p + kt for kt in range(4)]
    put("oldA", np.concatenate([branches(PAST + t[:, None] - r[None, :]) for r in rows], 1))
    put("oldC", window(P + t[:, None] - p[None, :]))
    key = np.arange(NS)
    dist = t[:, None] - key[None, :] % TS

    def own_of(seq, f):
        return np.where(seq == key[None, :] // TS, f(dist), NEG)

    put("newA", np.concatenate([own_of(2 * q + p[:, None] // 64, branches) for q in range(NB // 2)], 1))
    put("newC", np.concatenate([own_of(b + 0 * p[:, None], window) for b in range(NB)], 1))
    put("headof", (p[:, None] % 64 // TS == np.arange(8)[None, :]) * 1.0)
    put("selA", (p[:, None] // 64 * TS + t[:, None] == np.arange(16)[None, :]) * 1.0)
    put("selC", (p[:, None] % 64 == np.arange(64)[None, :]) * 1.0)
    s, c = p[:, None], p[None, :]

    def pair(size):
        return ((s // (2 * size) == c // (2 * size)) & (s // size % 2 == 0) & (c // size % 2 == 1)) * 1.0

    put("negE1T", -pair(1))
    put("negE1", -pair(1).T)
    for size in LEVELS:
        put(f"lev{size}", pair(size))
    for name, size in (("P", 64), ("S", TS)):
        put("strict" + name, ((s // size == c // size) & (s < c)) * 1.0)
        put("incl" + name, ((s // size == c // size) & (s <= c)) * 1.0)
    put("gneps", np.full((P, 1), GN_EPS))
    put("spread", (p[:, None] % 32 == c // HD * 16) * 1.0)
    put("own", (np.arange(NS)[:, None] // TS == np.arange(NB)[None, :]) * 1.0)
    return np.concatenate(parts, 1).astype(np.float32), at


class Tally:

    def __init__(self):
        self.n = {}

    def __call__(self, sem, by=1):
        self.n[id(sem)] = self.n.get(id(sem), 0) + by
        return self.n[id(sem)]


def segments():
    out, n = [], 0
    for l in range(DEPTH):
        for kind, c, blocks, kt, nd in (
            [("in", 0, 26, KT, 1), ("inq", 0, 8, KT, 2), ("inkv", 0, 2, KT, 1), ("out", 0, 16, KT, 3)]
            + [(kind, c, 2 * FC, KT, 1) if kind == "gu" else (kind, c, 16, FC, 1) for kind, c in FFN]
        ):
            out.append((l, kind, c, n, blocks, kt, nd))
            n += blocks
    return out


def build(nc, I, O, at):
    ctx = ExitStack()
    with ctx:
        base = [16512]

        def region(size):
            o = base[0]
            base[0] += size
            return o

        def place(name, shape, offset, dt=F32):
            return nc.alloc_sbuf_tensor_at(name, shape, dt, offset=offset)

        ncon = max(o + n for o, n in at.values())
        RX, RC, RP, RH, RW = region(20480), region(-(-ncon // 8) * 32), region(46080), region(40960), region(49152)
        RS, RM = region(30720), region(1472)

        xT = place("xT", [P, KT, TOK], RX)
        con = place("con", [P, ncon], RC)
        par = place("par", [P, N_PAR], RM)
        npar = place("npar", [P, 8], RM + 384)
        kap = place("kap", [P, 8], RM + 1440)
        shf = place("shf", [P, NB, 14], RM + 416)
        shc = place("shc", [P, 9, 14], RM + 864)
        sink = place("sink", [P, 16], RM + 1376)
        pT = place("pT", [P, NP_TILES, TOK], RP)
        hh = place("hh", [P, KT, TOK], RH, F32R)
        hl = place("hl", [P, KT, TOK], RH + 20480, F32R)
        sq = place("sq", [P, KT, TOK], RH + 20480)
        raw = [place(f"raw{i}", [P, KT, P], RW + 8192 * i) for i in range(2)]
        wh = [place(f"wh{i}", [P, KT, P], RW + 16384 + 8192 * i, F32R) for i in range(2)]
        wl = [place(f"wl{i}", [P, KT, P], RW + 32768 + 8192 * i, F32R) for i in range(2)]
        ah = [place(f"ah{i}", [P, FC, TOK], (RP, RS)[i], F32R) for i in range(2)]
        al = [place(f"al{i}", [P, FC, TOK], (RP, RS)[i] + 14080, F32R) for i in range(2)]
        ge = place("ge", [P, TOK], RP + 28160)
        gt = place("gt", [P, TOK], RP + 29440)
        ga = place("ga", [P, TOK], RP + 30720)
        ht = [place(f"ht{i}", [P, 4, TOK], RP + o) for i, o in enumerate((32000, 37120, 1280))]
        ssum = place("ssum", [P, TOK], RP + 42240)
        rsb = place("rsb", [P, TOK], RP + 43520)
        prow = place("prow", [N_PAR, P], RP)
        srow = place("srow", [NB * 14, P], RP + 512)
        xin = place("xin", [P, 3, D], RH)
        yout = [place(f"yout{i}", [P, D], RW + 8192 * i) for i in range(3)]
        xm = place("xm", [P, 14, TOK], RH)
        lw = place("lw", [P, 4, TOK], RH + 17920)
        cl = place("cl", [P, 4, TOK], RH + 23040)
        aa = place("aa", [P, 4, TOK], RH + 28160)
        kk = place("kk", [P, 4, TOK], RH + 33280)
        th12 = place("th12", [P, TOK], RH + 38400)
        sg13 = place("sg13", [P, TOK], RH + 39680)
        keep = place("keep", [P, TOK], RW + 37120)
        S0T = place("S0T", [P, NB, 4, P], RH + 17920)
        RKm = place("RKm", [P, 1024], RH + 34304)
        dA, dB, dK, dR, gg, e1, e2, yy = (place(n, [P, 4, TOK], RW + 5120 * i) for i, n in enumerate(
            ("dA", "dB", "dK", "dR", "gg", "e1", "e2", "yy")))
        vt, at_, bt, kt_ = (place(n, [P, 512], RW + 25600 + 2048 * i) for i, n in enumerate(("vt", "at_", "bt", "kt_")))
        S0P = place("S0P", [P, 4, P], RW + 40960)
        uu, tnv, nvs = (place(n, [P, 512], RW + 43008 + 2048 * i) for i, n in enumerate(("uu", "tnv", "nvs")))
        eA, eB, eR = (place(n, [P, 4, 2, P], RP + 20480 + 4096 * i) for i, n in enumerate(("eA", "eB", "eR")))
        mkb = [place(f"mk{i}", [P, NB * (P + TS) + HD], RP + 20480 + 4608 * i) for i in range(2)]
        mk = [m[:, 0:NB * P].rearrange("p (b c) -> p b c", b=NB) for m in mkb]
        mkd = [[m[:, j * HD:j * HD + NB * (P + TS)].rearrange("p (b c) -> p b c", b=NB) for j in range(2)] for m in mkb]
        pc = place("pc", [P, 4, 12], RP + 20480 + 12288)
        MT, WT, TT, ET, ZZ, NTm, RBm = (place(n, [P, 1024], RS + 4096 * i) for i, n in enumerate(
            ("MT", "WT", "TT", "ET", "ZZ", "NTm", "RBm")))
        tat = place("tat", [P, 512], RS + 28672)
        lora = [place(f"lora{i}", [P, 512], RS + 2048 * i) for i in range(4)]
        S0in = place("S0in", [P, NB, 4, P], RS + 8192)
        ux, vx = ([place(f"{n}{j}", [NS, 2, NB, HD], RS + (12288, 0)[j] + 4096 * i) for j in range(2)] for i, n in enumerate(("ux", "vx")))
        Sout = place("Sout", [P, NB, 4, HD], RP + 20480)
        SoutP = place("SoutP", [P, 4, HD], RP + 28672)
        stmp = place("stmp", [P, 512], RS + 20480)
        shr = place("shr", [126, P], RW + 35840)
        cK = [place(f"cK{i}", [P, 10, 512], RH if i == 0 else RW) for i in range(2)]
        cV = [place(f"cV{i}", [P, 10, 512], (RH if i == 0 else RW) + 20480) for i in range(2)]
        ktr = [place(f"ktr{i}", [P, 512], RW + 40960 + 2048 * i) for i in range(3)]
        omC = place("omC", [P, 2, P], RW + 47104)
        q0 = RP + 20480
        qdA = [place(f"qdA{i}", [P, 4, 2, 64], q0 + 2048 * i) for i in range(2)]
        qdC = [place(f"qdC{i}", [P, 2, 2, 8, TS], q0 + 4096 + 1024 * i) for i in range(2)]
        ckc = [place(f"ckc{i}", [P, P], q0 + 6144 + 512 * i) for i in range(2)]
        cvc = [place(f"cvc{i}", [P, P], q0 + 7168 + 512 * i) for i in range(2)]
        ptC = place("ptC", [P, 2, 2, P], q0 + 8192)
        om = place("om", [P, 512], q0 + 10240)
        tk = [place(f"tk{i}", [P, 3, n], RS + o) for i, (n, o) in enumerate(((512, 0), (512, 6144), (256, 12288)))]
        ptA = place("ptA", [P, 11, P], RS)
        smA = [place(f"smA{i}", [P, 1344], RS + 15360 + 5376 * i) for i in range(2)]
        smC = [place(f"smC{i}", [P, 2, 192], RS + 26112 + 1536 * i) for i in range(2)]
        psm = [place(f"psm{i}", [P, 384], RS + 15360 + 1536 * i) for i in range(3)]
        ppt = [place(f"ppt{i}", [P, 384], RS + 19968 + 1536 * i) for i in range(2)]
        rt = place("rt", [P, 2, TOK], RH + 38400)
        nm = [place(f"nm{i}", [P, 2], RS + 29184 + 64 * i) for i in range(3)]
        sums = [place(f"sums{i}", [P, 2], RS + 29376 + 64 * i) for i in range(3)]
        psk = [place(f"psk{i}", [P, 2], RS + 29568 + 64 * i) for i in range(3)]
        snm = [place(f"snm{i}", [P, 3], RS + 29760 + 64 * i) for i in range(2)]
        ssu = [place(f"ssu{i}", [P, 3], RS + 29888 + 64 * i) for i in range(2)]
        ssk = [place(f"ssk{i}", [P, 2], RS + 30016 + 64 * i) for i in range(2)]
        snk = place("snk", [P, 1], RS + 30144)

        PS = ctx.enter_context(nc.psum_tensor("PS", [P, 8, 512], F32))

        def C(name, rows=P, cols=None):
            o, n = at[name]
            return con[0:rows, o:o + (cols or n)]

        ident = C("ident")
        names = """con con2 x par lora s0 cK0 cK1 cV0 cV1 w0 w1 wh wl mm ev gexp al
            xtr xtc sq ssum nmm ht hh hl part parc
            zero xm shc sht shrc th sg z aa zexp aexp g gc ksq kss rkp rks clr expd abkr bon st stc
            tok tokc exd G Gc et Z Zc TZ TW TA TAc NV NVc TNV U Y0 Uc Sm SP Y Yc mz mk U1 U1c ux Se SF So Soc
            gn gnc ysq gv vr sd rn gsd grn xl xs keep kf cl drr bl vx TT WZ rk2 xrs sqd ssd hlp hpp et0 rts E1 NT RB tnv rw rot rotc kv kvc qz qbd
            S sm nmx pex pn PT ptc O oc
            rope snk ktp ktc sc bS smb bnm bex pt2 ptd pv1 om sel bo mix dve act fin fint finc fina out souts pool""".split()
        sem = {n: ctx.enter_context(nc.semaphore("s_" + n)) for n in names}
        segs = segments()
        block = ctx.enter_context(nc.Block())

        landed, count = {}, 0
        for (l, kind, c, n0, blocks, kts, nd) in segs:
            landed[n0] = count
            count += 16 * nd * (blocks // 2)

        def start_of(l, kind, c=0):
            return next(x[3] for x in segs if x[:3] == (l, kind, c))

        def seg(l, kind, c=0):
            return next(x for x in segs if x[:3] == (l, kind, c))

        layer_first = [start_of(l, "in") for l in range(DEPTH)]
        CACHE_DMAS = 8
        ROTATED = [slice(t, min(t + 2, end)) for t0, end in ((QA, VA), (QC, VC)) for t in range(t0, end, 2)]
        QUADS = ((0, 4), (4, 4), (8, 2))

        @block.sync
        def _(sp):
            want = Tally()
            outs = Tally()

            def load(j, l, kind, c, b):
                r = raw[j]
                inc = sem[f"w{j}"]
                if kind in ("in", "inkv"):
                    w = I["w_in"][l].rearrange("(k p) n -> p k n", p=P)
                    c0 = 0 if kind == "in" else KC * P
                    sp.dma_start(r[:], w[:, :, bass.ds(b * P + c0, P)]).then_inc(inc, 16)
                elif kind == "inq":
                    w = I["w_in"][l].rearrange("(k p) n -> p k n", p=P)
                    for half in range(2):
                        sp.dma_start(r[:, :, half * HD:(half + 1) * HD],
                                     w[:, :, bass.ds(b * HD + (QC * P + half * 512), HD)]).then_inc(inc, 16)
                elif kind == "out":
                    w = I["w_out"][l]
                    sp.dma_start(r[:, 0:8], w[0:1024].rearrange("(k p) n -> p k n", p=P)[:, :, bass.ds(b * P, P)]).then_inc(inc, 16)
                    for half in range(2):
                        rows = w[1024 + 512 * half:1536 + 512 * half].rearrange("(k p) n -> p k n", p=HD)
                        sp.dma_start(r[half * HD:(half + 1) * HD, 8:16], rows[:, :, bass.ds(b * P, P)]).then_inc(inc, 16)
                elif kind == "down":
                    w = I["w_down"][l][c * FC * P:(c + 1) * FC * P].rearrange("(k p) n -> p k n", p=P)
                    sp.dma_start(r[:, 0:FC], w[:, :, bass.ds(b * P, P)]).then_inc(inc, 16)

            def load_gu(j, l, c, i):
                w = I["w_gate" if j == 0 else "w_up"][l].rearrange("(k p) n -> p k n", p=P)
                sp.dma_start(raw[j][:], w[:, :, bass.ds(i * P + c * FC * P, P)]).then_inc(sem[f"w{j}"], 16)

            def stream(l, kind, c=0):
                _, _, _, n0, blocks, kts, nd = seg(l, kind, c)

                def pair(i, first):
                    for j in range(2):
                        if not (first and n0 == 0):
                            sp.wait_ge(sem["wl"], 2 * i + (n0 + j - 1))
                        load_gu(j, l, c, i) if kind == "gu" else load(j, l, kind, c, 2 * i + j)
                pair(0, True)
                if blocks > 2:
                    with sp.Fori(1, blocks // 2) as i:
                        pair(i, False)

            sp.dma_start(con[:, 0:P], I["con"][:, 0:P]).then_inc(sem["con"], 16)
            for q in range(2):
                sp.dma_start(xin[:, q, :], I["x_prompt"][0, q * P:(q + 1) * P, :]).then_inc(sem["x"], 16)
            sp.dma_start(xin[0:NS, 2, :], I["x_sample"].rearrange("b t d -> (b t) d")).then_inc(sem["x"], 16)
            sp.dma_start(con[:, P:ncon], I["con"][:, P:ncon]).then_inc(sem["con2"], 16)
            for l in range(DEPTH):
                if l:
                    sp.wait_ge(sem["ev"], layer_first[l])
                for name, r0, n in (("g_mix", G_MIX, 16), ("g_ffn", G_FFN, 16), ("b_mu", MU, 14), ("b_w0", W0, 4),
                                    ("b_a0", A0, 4), ("b_k_k", KK, 4), ("b_k_a", KA_, 4), ("b_r_k", RK_, 4),
                                    ("b_lnx_w", LNW, 4), ("b_lnx_b", LNB, 4)):
                    sp.dma_start(prow[r0:r0 + n, :], I[name][l].rearrange("(r c) -> r c", c=P)).then_inc(sem["par"], 16)
                sp.dma_start(prow[G_FIN:G_FIN + 16, :], I["g_final"].rearrange("(r c) -> r c", c=P)).then_inc(sem["par"], 16)
                sp.dma_start(srow[:], I["state_b_shift"][l].rearrange("b (r c) -> (b r) c", c=P)).then_inc(sem["par"], 16)
                sp.dma_start(sink[:], I["c_sink"][l].rearrange("k g -> (k g)").rearrange("(o n) -> o n", o=1).broadcast_to([P, 16])).then_inc(sem["par"], 16)
                sp.wait_ge(sem["zero"], 2 * l + 1)
                sp.dma_start(lora[0][0:LORA_W, :], I["b_w2"][l]).then_inc(sem["lora"], 16)
                sp.dma_start(lora[1][96:128, :], I["b_a2"][l][0:32]).then_inc(sem["lora"], 16)
                sp.dma_start(lora[2][0:64, :], I["b_a2"][l][32:96]).then_inc(sem["lora"], 16)
                sp.dma_start(lora[3][64:128, :], I["b_g2"][l]).then_inc(sem["lora"], 16)
                for b in range(NB):
                    for h2 in range(2):
                        sp.dma_start(S0in[h2 * HD:(h2 + 1) * HD, b, :, h2 * HD:(h2 + 1) * HD],
                                     I["state_b_wkv"][l, b].rearrange("(f h) i j -> h i f j", h=2)[h2]).then_inc(sem["s0"], 16)
                stream(l, "in")
                stream(l, "inq")
                stream(l, "inkv")
                sp.wait_ge(sem["shrc"], l + 1)
                sp.dma_start(O["new_shift_prompt"][l, 0].rearrange("(r c) -> r c", c=P), shr[0:14, :]).then_inc(sem["out"], 16)
                sp.dma_start(O["new_shift_sample"][l].rearrange("b (r c) -> (b r) c", c=P), shr[14:126, :]).then_inc(sem["out"], 16)
                sp.wait_ge(sem["Soc"], 9 * l + 9)
                for h2 in range(2):
                    for b in range(NB):
                        sp.dma_start(O["new_wkv_sample"][l, b].rearrange("(f h) i j -> h i f j", h=2)[h2],
                                     Sout[h2 * HD:(h2 + 1) * HD, b]).then_inc(sem["souts"], 16)
                    sp.dma_start(O["new_wkv_prompt"][l, 0].rearrange("(f h) i j -> h i f j", h=2)[h2],
                                 SoutP[h2 * HD:(h2 + 1) * HD]).then_inc(sem["souts"], 16)

                def cache(b, which):
                    s = sem[f"c{which}{b % 2}"]
                    dst, small = (cK, ckc) if which == "K" else (cV, cvc)
                    rows = I["cache_a_" + which.lower()][l, b].rearrange("r h d -> r (h d)")
                    old = rows[0:1536].rearrange("(n g r) c -> n g r c", n=6, r=16)
                    for n in range(6):
                        sp.dma_start(dst[b % 2][:, n, :], old[n, :, 0:8, :]).then_inc(s, 16)
                    sp.dma_start(dst[b % 2][:, 6:10, :], rows[1536:2048].rearrange("(p r) c -> p r c", p=P)).then_inc(s, 16)
                    sp.dma_start(small[b % 2][:], I["cache_c_" + which.lower()][l, b].rearrange("r h d -> r (h d)")).then_inc(s, 16)

                sp.wait_ge(sem["rw"], l + 1)
                sp.wait_ge(sem["souts"], 16 * 18 * (l + 1))
                for which in "KV":
                    cache(0, which)
                    cache(1, which)
                sp.wait_ge(sem["kvc"], 9 * (l + 1))
                sp.dma_start(snk[:], I["c_sink"][l].rearrange("k g -> (k g)").unsqueeze(1).unsqueeze(2).broadcast_to([16, TS, 1])).then_inc(sem["snk"], 16)
                for q in range(2):
                    rows = slice(q * P, (q + 1) * P)
                    sp.dma_start(O["new_a_k_prompt"][l, 0, rows].rearrange("t h d -> t (h d)"), tk[0][:, q, :]).then_inc(sem["out"], 16)
                    sp.dma_start(O["new_a_v_prompt"][l, 0, rows].rearrange("t h d -> t (h d)"), tk[1][:, q, :]).then_inc(sem["out"], 16)
                sp.dma_start(O["new_c_k_prompt"][l, 0].rearrange("t h d -> t (h d)"), tk[2][:, 1, 0:P]).then_inc(sem["out"], 16)
                sp.dma_start(O["new_c_v_prompt"][l, 0].rearrange("t h d -> t (h d)"), tk[2][:, 1, P:2 * P]).then_inc(sem["out"], 16)
                for name, src in (("new_a_k_sample", tk[0][0:NS, 2, :]), ("new_a_v_sample", tk[1][0:NS, 2, :]),
                                  ("new_c_k_sample", tk[2][0:NS, 2, 0:P]), ("new_c_v_sample", tk[2][0:NS, 2, P:2 * P])):
                    sp.dma_start(O[name][l].rearrange("b t h d -> (b t) (h d)"), src).then_inc(sem["out"], 16)

                def next_keys(b):
                    sp.wait_ge(sem["sc"], 13 * (NB * l + b - 1))
                    cache(b, "K")

                def next_values(b):
                    sp.wait_ge(sem["pv1"], NB * l + b - 1)
                    cache(b, "V")
                for b in (2, 3, 4, 5):
                    next_keys(b)
                for b in (2, 3):
                    next_values(b)
                for b in (6, 7):
                    next_keys(b)
                for b in (4, 5, 6, 7):
                    next_values(b)
                sp.wait_ge(sem["out"], 16 * 12 * (l + 1))
                sp.wait_ge(sem["sc"], 13 * NB * (l + 1))
                stream(l, "out")
                for kind, c in FFN:
                    stream(l, kind, c)
            for q in range(3):
                sp.wait_ge(sem["finc"], (5, 6, 6)[q])
                sp.wait_ge(sem["fina"], (5, 5, 6)[q])
                if q < 2:
                    sp.dma_start(O["y_prompt"][0, q * P:(q + 1) * P, :], yout[q][:]).then_inc(sem["fin"], 16)
                else:
                    sp.dma_start(O["y_sample"].rearrange("b t d -> (b t) d"), yout[2][0:NS, :]).then_inc(sem["fin"], 16)
            sp.wait_ge(sem["fin"], 48)
            sp.wait_ge(sem["out"], 16 * 12 * DEPTH)
            sp.wait_ge(sem["souts"], 16 * 18 * DEPTH)

        @block.gpsimd
        def _(pool):
            def low_parts(n):
                for g in (1, 2):
                    pool.wait_ge(sem["hh"], 4 * (4 * (n // 2) + n % 2 * 3) + g + 1)
                    x = slice(4 * g, 4 * g + 4)
                    pool.tensor_tensor(hl[:, x], ht[g][:], hh[:, x].bitcast(F32), ALU.subtract).then_inc(sem["hlp"], 1)

            for l in range(DEPTH):
                if l:
                    pool.wait_ge(sem["ev"], layer_first[l])
                for i in range(4):
                    pool.memset(lora[i][:], 0.0)
                pool.memset(S0in[:], 0.0).then_inc(sem["zero"], 1)
                low_parts(2 * l)
                pool.wait_ge(sem["shc"], l + 1)
                pool.memset(keep[:], 1.0).then_inc(sem["pool"], 1)
                pool.wait_ge(sem["pool"], 3 * l + 1)
                pool.memset(keep[:, 0:SEQ:HD], 0.0)
                pool.memset(keep[:, SEQ:TOK:TS], 0.0).then_inc(sem["keep"], 1)
                xv, mu = xm[:, 8:12], par[:, MU + 8:MU + 12].unsqueeze(2).broadcast_to([P, 4, TOK])
                pool.tensor_tensor(xv, xv, mu, ALU.mult).then_inc(sem["pool"], 1)
                pool.wait_ge(sem["pool"], 3 * l + 2)
                pool.tensor_tensor(xv, xv, pT[:, BR + 8:BR + 12], ALU.add).then_inc(sem["xs"], 1)
                pool.wait_ge(sem["cl"], l + 1)
                pool.tensor_tensor(dA[:], cl[:], lw[:], ALU.subtract).then_inc(sem["clr"], 1)
                pool.wait_ge(sem["xm"], l + 1)
                pool.wait_ge(sem["xs"], l + 1)
                pool.wait_ge(sem["xrs"], l + 1)
                pool.memset(S0P[:], 0.0)
                pool.memset(eA[:], 0.0)
                pool.memset(eB[:], 0.0)
                pool.memset(eR[:], 0.0).then_inc(sem["zero"], 1)
                pool.wait_ge(sem["expd"], l + 1)
                pool.tensor_copy(pc[:, :, 0:4], dR[:, :, HD - 1:SEQ:HD])
                pool.tensor_copy(pc[:, :, 4:12], dR[:, :, SEQ + TS - 1:TOK:TS]).then_inc(sem["pool"], 1)
                pool.wait_ge(sem["pool"], 3 * l + 3)
                pool.tensor_tensor(dR[:], dR[:], xm[:, 0:4], ALU.mult).then_inc(sem["drr"], 1)
                for tau in range(3):
                    nt = P if tau < 2 else NS
                    pool.wait_ge(sem["Gc"], 3 * l + tau + 1)
                    for hf in range(2):
                        m = C(f"lev{LEVELS[0]}", nt, nt).unsqueeze(1).broadcast_to([nt, 4, nt])
                        x, y = (z[0:nt, hf * 4 * nt:(hf + 1) * 4 * nt].rearrange("p (h t) -> p h t", h=4) for z in (MT, ET))
                        pool.tensor_tensor(y, x, m, ALU.mult).then_inc(sem["et0"], 1)
                pool.wait_ge(sem["G"], 15 * (l + 1))
                pool.memset(mkb[0][:], 0.0)
                pool.memset(mkb[1][:], 0.0).then_inc(sem["mz"], 1)
                pool.wait_ge(sem["Y"], 3 * (l + 1))
                for f in range(4):
                    if f >= 2:
                        pool.wait_ge(sem["Se"], 4 * l + f - 1)
                    for h2 in range(2):
                        cols = slice((2 * f + h2) * HD, (2 * f + h2 + 1) * HD)
                        a = pool.tensor_tensor(vx[f % 2][:, h2], vt[0:NS, cols].unsqueeze(1).broadcast_to([NS, NB, HD]),
                                               C("own", NS).unsqueeze(2).broadcast_to([NS, NB, HD]), ALU.mult)
                    a.then_inc(sem["vx"], 1)
                pool.wait_ge(sem["souts"], 16 * 18 * (l + 1))
                for i in range(2):
                    pool.memset(qdA[i][:], 0.0)
                    z = pool.memset(qdC[i][:], 0.0)
                z.then_inc(sem["qz"], 1)
                pool.wait_ge(sem["qz"], l + 1)
                pool.wait_ge(sem["rope"], 9 * (l + 1))
                for q in range(NB // 2):
                    if q >= 2:
                        pool.wait_ge(sem["bS"], 4 * l + q - 1)
                    o = SEQ + 2 * TS * q
                    for h2 in range(2):
                        rows = slice(h2 * HD, h2 * HD + HD)
                        for f in range(4):
                            c0 = (2 * f + h2) * TS
                            pool.tensor_copy(qdA[q % 2][rows, f, :, c0:c0 + TS], pT[rows, QA + f, o:o + 2 * TS].rearrange("p (b t) -> p b t", b=2))
                        for b2 in range(2):
                            a = pool.tensor_copy(qdC[q % 2][rows, b2, h2], pT[rows, QC:QC + 8, o + b2 * TS:o + b2 * TS + TS])
                    a.then_inc(sem["qbd"], 1)
                pool.wait_ge(sem["hh"], 16 * l + 8)
                pool.wait_ge(sem["pv1"], 8 * (l + 1))
                for g, t0 in ((2, QC), (3, QC + 4)):
                    pool.tensor_tensor(hl[:, 4 * g:4 * g + 4, 0:SEQ], pT[:, t0:t0 + 4, 0:SEQ], hh[:, 4 * g:4 * g + 4, 0:SEQ].bitcast(F32), ALU.subtract).then_inc(sem["hpp"], 1)
                low_parts(2 * l + 1)

        @block.scalar
        def _(act):
            want = Tally()

            def take(name, by=1):
                act.wait_ge(sem[name], want(sem[name], by))

            def split(n0, i, j, kts, nd):
                act.wait_ge(sem[f"w{j}"], 16 * nd * i + (landed[n0] + 16 * nd))
                if not (n0 == 0 and isinstance(i, int) and i == 0):
                    act.wait_ge(sem["mm"], 2 * i + (n0 + j - 1))
                act.activation(wh[j][:, 0:kts], raw[j][:, 0:kts], ACT.Copy).then_inc(sem["wh"], 1)

            def stream(l, kind, c=0, ready=False, ahead=None):
                _, _, _, n0, blocks, kts, nd = seg(l, kind, c)
                if not ready:
                    split(n0, 0, 0, kts, nd)

                def pair(i, last):
                    split(n0, i, 1, kts, nd)
                    if kind == "gu":
                        act.wait_ge(sem["mm"], 2 * i + (n0 + 1))
                        act.activation(ge[:], PS[:, 0, 0:TOK], ACT.Exp, scale=-1.0).then_inc(sem["gexp"], 1)
                    if not last:
                        split(n0, i + 1, 0, kts, nd)
                    elif ahead:
                        _, _, _, m0, _, k2, d2 = seg(*ahead)
                        split(m0, 0, 0, k2, d2)
                if blocks > 2:
                    with act.Fori(0, blocks // 2 - 1) as i:
                        pair(i, False)
                pair(blocks // 2 - 1, True)

            def squares():
                for g in range(4):
                    act.activation(sq[:, 4 * g:4 * g + 4], xT[:, 4 * g:4 * g + 4], ACT.Square).then_inc(sem["sq"], 1)

            def root(x):
                take("vr")
                act.activation(x[:], x[:], ACT.Sqrt).then_inc(sem["sd"], 1)

            def hi_parts():
                root(rsb)
                for g in range(4):
                    take("ht")
                    act.activation(hh[:, 4 * g:4 * g + 4], ht[g % 3][:], ACT.Copy).then_inc(sem["hh"], 1)

            for q in range(12):
                take("xtr")
                nt = P if q < 8 else NS
                tau, k0 = q // 4, q % 4 * 4
                act.activation(xT[:, k0:k0 + 4, tau * P:tau * P + nt],
                               PS[:, 2 + q % 4, 0:4 * nt].rearrange("p (k t) -> p k t", k=4), ACT.Copy).then_inc(sem["xtc"], 1)
            act.wait_ge(sem["xtc"], 12)
            for l in range(DEPTH):
                if l == 0:
                    squares()
                hi_parts()
                stream(l, "in", ahead=(l, "inq"))
                stream(l, "inq", ready=True, ahead=(l, "inkv"))
                stream(l, "inkv", ready=True)
                take("xl")
                act.activation(th12[:], xm[:, 12, :], ACT.Tanh).then_inc(sem["th"], 1)
                act.activation(sg13[:], xm[:, 13, :], ACT.Tanh, scale=0.5).then_inc(sem["th"], 1)
                take("xm")
                for f in range(4):
                    a = act.activation(dB[:, f], xm[:, 4 + f], ACT.Square, scale=par[:, KK + f:KK + f + 1])
                a.then_inc(sem["ksq"], 1)
                take("z")
                for f in range(4):
                    a = act.activation(e1[:, f], PS[:, f, 0:TOK], ACT.Tanh, scale=0.5, bias=npar[:, f:f + 1])
                a.then_inc(sem["zexp"], 1)
                take("aa")
                for f in range(4):
                    a = act.activation(e2[:, f], PS[:, 4 + f, 0:TOK], ACT.Tanh, scale=0.5, bias=npar[:, 4 + f:5 + f])
                a.then_inc(sem["aexp"], 1)
                act.wait_ge(sem["aexp"], l + 1)
                for f in range(4):
                    a = act.activation(dR[:, f], e2[:, f], ACT.Identity, scale=kap[:, f:f + 1], bias=kap[:, 4 + f:5 + f])
                a.then_inc(sem["kf"], 1)
                take("kss")
                act.activation(th12[:], PS[:, 4, 0:TOK], ACT.Sqrt).then_inc(sem["sd"], 1)
                take("g")
                act.activation(gg[:], PS[:, 0:4, 0:TOK], ACT.Copy).then_inc(sem["gc"], 1)
                take("clr")
                act.wait_ge(sem["cl"], l + 1)
                act.wait_ge(sem["rkp"], l + 1)
                act.activation(dR[:], cl[:], ACT.Exp, scale=DECAY / 2)
                act.activation(dK[:], cl[:], ACT.Exp, scale=-DECAY / 2)
                act.activation(dA[:], dA[:], ACT.Exp, scale=DECAY / 2).then_inc(sem["expd"], 1)
                for r in range(8):
                    take("st")
                    act.activation(S0T[:, r], PS[:, 4 + r % 4, :].rearrange("p (f i) -> p f i", f=4), ACT.Copy).then_inc(sem["stc"], 1)
                take("bon")
                for f in range(4):
                    a = act.activation(xm[:, 4 + f], xm[:, 4 + f], ACT.Identity, bias=par[:, LNB + f:LNB + f + 1])
                a.then_inc(sem["bl"], 1)
                for tau in range(3):
                    nt = P if tau < 2 else NS
                    for q, dst in enumerate((vt, at_, bt, kt_)):
                        take("tok")
                        act.activation(dst[0:nt, :], PS[0:nt, q, :], ACT.Copy).then_inc(sem["tokc"], 1)
                    act.wait_ge(sem["G"], 5 * (3 * l + tau) + 1)
                    act.activation(MT[0:nt, 0:8 * nt].rearrange("p (b h) -> p b h", b=2), PS[0:nt, 4:6, 0:4 * nt], ACT.Copy).then_inc(sem["Gc"], 1)
                    for size in LEVELS if tau < 2 else LEVELS[:2]:
                        for hf in range(2):
                            take("Z")
                            act.activation(ZZ[0:nt, hf * 4 * nt:(hf + 1) * 4 * nt], PS[0:nt, 6 + hf, 0:4 * nt], ACT.Copy).then_inc(sem["Zc"], 1)
                    take("TA")
                    act.activation(tat[:, 0:4 * nt], PS[:, 4, 0:4 * nt], ACT.Copy).then_inc(sem["TAc"], 1)
                take("U1", 4)
                act.activation(nvs[NS:2 * NS, :], PS[NS:2 * NS, 7, :], ACT.Copy).then_inc(sem["U1c"], 1)
                take("gnc")
                act.activation(dA[:], yy[:], ACT.Square).then_inc(sem["ysq"], 1)
                take("gv")
                act.activation(dB[:, 0], PS[:, 0, 0:TOK], ACT.Sqrt, scale=1.0 / HD, bias=C("gneps")).then_inc(sem["gsd"], 1)
                for r in range(9):
                    take("So")
                    for h2 in range(2):
                        rows, cols = slice(h2 * HD, h2 * HD + HD), slice(h2 * HD, h2 * HD + HD)
                        src = PS[rows, 4 + r % 4, :].rearrange("p (f j) -> p f j", f=4)[:, :, cols]
                        dst = Sout[rows, r] if r < 8 else SoutP[rows]
                        a = act.activation(dst, src, ACT.Copy)
                    a.then_inc(sem["Soc"], 1)
                for q in range(9):
                    take("kv")
                    n = 512 if q % 3 < 2 else 256
                    nt = P if q < 6 else NS
                    act.activation(tk[q % 3][0:nt, q // 3, :], PS[0:nt, 4 + q % 4, 0:n], ACT.Copy).then_inc(sem["kvc"], 1)
                for u in range(24 + 3):
                    if u < 24:
                        take("nmx")
                        for q in range(2):
                            cols = slice(0, P) if q == 0 else slice(P, 384)
                            a = act.activation(psm[u % 3][:, cols], psm[u % 3][:, cols], ACT.Exp,
                                               bias=nm[u % 3][:, q:q + 1], accum_out=sums[u % 3][:, q:q + 1])
                        if u >= 8:
                            h = (u - 8) // 2 + 8 * (u % 2)
                            a = act.activation(psk[u % 3][:], nm[u % 3][:], ACT.Exp, bias=sink[:, h:h + 1])
                        a.then_inc(sem["pex"], 1)
                    if 2 <= u < 26:
                        v = u - 2
                        take("PT")
                        if v >= 2:
                            act.wait_ge(sem["O"], 24 * l + v - 1)
                        act.activation(ppt[v % 2][:], PS[:, 2 + v % 2, 0:384], ACT.Copy).then_inc(sem["ptc"], 1)
                    if u >= 3:
                        v = u - 3
                        par2 = v % 2
                        tile = QA + v // 2 if v < 8 else QC + (v - 8) // 2
                        take("O")
                        rows = slice(par2 * HD, par2 * HD + HD)
                        act.activation(pT[rows, tile, 0:SEQ], PS[rows, 4 + par2, 0:SEQ], ACT.Copy).then_inc(sem["oc"], 1)
                def key_tiles(q):
                    for b in (2 * q, 2 * q + 1):
                        for m in range(13):
                            if b == 2 and m in (3, 6):
                                exps(0, m == 3)
                            n = QUADS[m // 4][1] * P if m < 12 else P
                            take("ktp")
                            if NB * l + b or m >= 3:
                                act.wait_ge(sem["sc"], 13 * (NB * l + b) + m - 2)
                            act.activation(ktr[(13 * (NB * l + b) + m) % 3][:, 0:n], PS[:, 4 + (13 * b + m) % 2, 0:n], ACT.Copy).then_inc(sem["ktc"], 1)

                def exps(q, first=None):
                    i = q % 2
                    if first in (None, True):
                        take("bnm")
                        act.activation(smA[i][:], smA[i][:], ACT.Exp, bias=snm[i][:, 0:1], accum_out=ssu[i][:, 0:1])
                    if first in (None, False):
                        for b2 in range(2):
                            act.activation(smC[i][:, b2], smC[i][:, b2], ACT.Exp, bias=snm[i][:, 1 + b2:2 + b2], accum_out=ssu[i][:, 1 + b2:2 + b2])
                        act.activation(ssk[i][:], snm[i][:, 1:3], ACT.Exp, bias=snk[:, 0:1]).then_inc(sem["bex"], 1)

                act.wait_ge(sem["snk"], 16 * (l + 1))
                key_tiles(0)
                for q in range(NB // 2):
                    if q < NB // 2 - 1:
                        key_tiles(q + 1)
                    if q == 0:
                        act.wait_ge(sem["out"], 16 * 12 * (l + 1))
                    for r in range(4):
                        take("pt2")
                        bank = PS[:, 6 + r % 2, :].rearrange("p (k c) -> p k c", k=4)
                        if r < 2:
                            a = act.activation(ptA[:, 4 * r:4 * r + 4], bank, ACT.Copy)
                        elif r == 2:
                            act.activation(ptA[:, 8:10], bank[:, 0:2], ACT.Copy)
                            a = act.activation(ptA[0:NS, 10], bank[0:NS, 2], ACT.Copy)
                        else:
                            bank = PS[:, 7, :].rearrange("p (b k c) -> p b k c", b=2, k=2)
                            act.activation(ptC[:, :, 0], bank[:, :, 0], ACT.Copy)
                            a = act.activation(ptC[0:NS, :, 1], bank[0:NS, :, 1], ACT.Copy)
                        a.then_inc(sem["ptd"], 1)
                    if q < NB // 2 - 1:
                        exps(q + 1)
                act.wait_ge(sem["sc"], 13 * NB * (l + 1))
                for g, t0 in enumerate((QA, BR, QC, QC + 4)):
                    act.activation(hh[:, 4 * g:4 * g + 4, 0:SEQ], pT[:, t0:t0 + 4, 0:SEQ], ACT.Copy).then_inc(sem["hh"], 1)
                act.wait_ge(sem["pv1"], 8 * (l + 1))
                _, _, _, n0, _, kts, nd = seg(l, "out")
                split(n0, 0, 0, kts, nd)
                act.wait_ge(sem["bo"], 4 * (l + 1))
                for g, t0 in enumerate((QA, BR, QC, QC + 4)):
                    act.activation(hh[:, 4 * g:4 * g + 4, SEQ:TOK], pT[:, t0:t0 + 4, SEQ:TOK], ACT.Copy).then_inc(sem["hh"], 1)
                stream(l, "out", ready=True, ahead=(l, *FFN[0]))
                hi_parts()
                for i, (kind, c) in enumerate(FFN):
                    stream(l, kind, c, ready=True, ahead=(l, *FFN[i + 1]) if i + 1 < len(FFN) else None)
            root(rsb)
            for q in range(1, 12, 2):
                take("fint", 2)
                g, tau = divmod(q, 3)
                nt = P if tau < 2 else NS
                act.activation(yout[tau][0:nt, g * 512:(g + 1) * 512], PS[0:nt, q % 4, :], ACT.Copy).then_inc(sem["fina"], 1)

        @block.vector
        def _(dve):
            want = Tally()

            def take(name, by=1):
                dve.wait_ge(sem[name], want(sem[name], by))

            def done(ins, name="dve"):
                ins.then_inc(sem[name], 1)
                dve.wait_ge(sem[name], want(sem[name]))

            tt, ts, stt = dve.tensor_tensor, dve.tensor_scalar, dve.scalar_tensor_tensor

            def split(n, j, kts):
                dve.wait_ge(sem["wh"], n + 1)
                tt(wl[j][:, 0:kts], raw[j][:, 0:kts], wh[j][:, 0:kts].bitcast(F32), ALU.subtract).then_inc(sem["wl"], 1)

            def stream(l, kind, c=0, ready=False, ahead=None):
                _, _, _, n0, blocks, kts, nd = seg(l, kind, c)
                tile0 = {"in": 0, "inq": QC, "inkv": KC}.get(kind, 0)
                if not ready:
                    split(n0, 0, kts)
                if kind == "out":
                    dve.wait_ge(sem["hpp"], 2 * (l + 1))
                if kind == "out" or (kind, c) == FFN[-1]:
                    done(dve.memset(ssum[:], 0.0))

                def drain(i, j):
                    if kind in ("in", "inq", "inkv"):
                        dve.wait_ge(sem["mm"], 2 * i + (n0 + j + 1))
                        dve.tensor_copy(pT[:, bass.ds(2 * i + (tile0 + j), 1), :].rearrange("p o t -> p (o t)"), PS[:, j, 0:TOK]).then_inc(sem["ev"], 1)
                    elif kind in ("out", "down"):
                        dve.wait_ge(sem["mm"], 2 * i + (n0 + j + 1))
                        x = xT[:, bass.ds(2 * i + j, 1), :].rearrange("p o t -> p (o t)")
                        tt(x, x, PS[:, j, 0:TOK], ALU.add).then_inc(sem["ev"], 1)
                        if kind == "out" or c == NCH - 1:
                            m = 2 * KT * l + (KT if kind == "down" else 0)
                            dve.wait_ge(sem["ev"], 2 * i + (n0 + j + 1))
                            tt(ga[:], x, x, ALU.mult).then_inc(sem["sqd"], 1)
                            dve.wait_ge(sem["sqd"], 2 * i + (m + j + 1))
                            tt(ssum[:], ssum[:], ga[:], ALU.add).then_inc(sem["ssd"], 1)
                            dve.wait_ge(sem["ssd"], 2 * i + (m + j + 1))
                    elif j == 0:
                        pairs = (l * NCH + c) * FC
                        dve.wait_ge(sem["gexp"], i + (pairs + 1))
                        ts(gt[:], ge[:], 1.0, None, ALU.add).then_inc(sem["act"], 1)
                        dve.wait_ge(sem["act"], 5 * (i + pairs) + 1)
                        dve.reciprocal(gt[:], gt[:]).then_inc(sem["act"], 1)
                        dve.wait_ge(sem["act"], 5 * (i + pairs) + 2)
                        tt(gt[:], gt[:], PS[:, 0, 0:TOK], ALU.mult).then_inc(sem["ev"], 1)
                    else:
                        pairs = (l * NCH + c) * FC
                        dve.wait_ge(sem["mm"], 2 * i + (n0 + 2))
                        dve.wait_ge(sem["ev"], 2 * i + (n0 + 1))
                        hi = ah[c % 2][:, bass.ds(i, 1), :].rearrange("p o t -> p (o t)")
                        lo = al[c % 2][:, bass.ds(i, 1), :].rearrange("p o t -> p (o t)")
                        tt(hi, gt[:], PS[:, 1, 0:TOK], ALU.mult).then_inc(sem["act"], 1)
                        tt(ga[:], gt[:], PS[:, 1, 0:TOK], ALU.mult).then_inc(sem["ev"], 1)
                        dve.wait_ge(sem["act"], 5 * (i + pairs) + 3)
                        dve.wait_ge(sem["ev"], 2 * i + (n0 + 2))
                        tt(lo, ga[:], hi.bitcast(F32), ALU.subtract).then_inc(sem["act"], 2)

                def pair(i, last):
                    split(2 * i + (n0 + 1), 1, kts)
                    drain(i, 0)
                    if not last:
                        split(2 * i + (n0 + 2), 0, kts)
                    elif ahead:
                        _, _, _, m0, _, k2, _ = seg(*ahead)
                        split(m0, 0, k2)
                    drain(i, 1)
                if blocks > 2:
                    with dve.Fori(0, blocks // 2 - 1) as i:
                        pair(i, False)
                pair(blocks // 2 - 1, True)
                dve.wait_ge(sem["ev"], n0 + blocks)

            def rms(first=False):
                if first:
                    for g in range(4):
                        take("sq")
                        x = sq[:, 4 * g:4 * g + 4].rearrange("p k t -> p t k")
                        done(dve.tensor_reduce(ht[0][:, g], x, AX_X, ALU.add), "ssum")
                take("nmm")
                done(ts(rsb[:], PS[:, 2, 0:TOK], 1.0 / D, 1e-6, ALU.mult, ALU.add), "vr")
                take("sd")
                done(dve.reciprocal(rsb[:], rsb[:]))

            def norm(g0, n):
                rms(n == 0)

                def scaled(g):
                    for k in range(4):
                        a = stt(ht[g % 3][:, k], xT[:, 4 * g + k], par[:, g0 + 4 * g + k:g0 + 4 * g + k + 1], rsb[:], ALU.mult, ALU.mult)
                    done(a, "ht")

                def low(g, by):
                    take("hh", by)
                    done(tt(hl[:, 4 * g:4 * g + 4], ht[g % 3][:], hh[:, 4 * g:4 * g + 4].bitcast(F32), ALU.subtract), "hl")
                scaled(0)
                scaled(1)
                low(0, 1)
                scaled(2)
                scaled(3)
                low(3, 3)

            def banks(b, nt):
                return PS[0:nt, b:b + 2, 0:4 * nt].rearrange("p b (h t) -> p b h t", h=4)

            def heads(x, nt):
                return x[0:nt, 0:8 * nt].rearrange("p (b h t) -> p b h t", b=2, h=4)

            def mask(name, nt):
                return C(name, nt, nt).unsqueeze(1).unsqueeze(1).broadcast_to([nt, 2, 4, nt])

            def halves():
                return [slice(0, HD), slice(HD, P)]

            zs = [0]

            def rotated(u):
                n = ROTATED[u].stop - ROTATED[u].start
                x, y = pT[:, ROTATED[u]], rt[:, 0:n]
                wide = lambda name: C(name).unsqueeze(1).broadcast_to([P, n, TOK])
                take("rot")
                tt(y, PS[:, 2:2 + n, 0:TOK] if u % 2 == 0 else PS[:, 5:5 + n, 0:TOK], wide("sin"), ALU.mult).then_inc(sem["rotc"], 1)
                done(tt(x, x, wide("cos"), ALU.mult), "rts")
                take("rotc")
                done(tt(x, x, y, ALU.add), "rope")

            def rwkv(l):
                pB = pT[:, BR:BR + 14]
                sam = lambda x: x[:, :, SEQ:TOK].rearrange("p k (b t) -> p k b t", b=NB)
                tt(xm[:, :, 1:SEQ], pB[:, :, 0:SEQ - 1], pB[:, :, 1:SEQ], ALU.subtract)
                ts(xm[:, :, 0:1], pB[:, :, 0:1], -1.0, None, ALU.mult)
                for b in range(NB):
                    o = SEQ + b * TS
                    tt(xm[:, :, o + 1:o + TS], pB[:, :, o:o + TS - 1], pB[:, :, o + 1:o + TS], ALU.subtract)
                tt(sam(xm[:])[:, :, :, 0], shf[:].rearrange("p b k -> p k b"), sam(pB)[:, :, :, 0], ALU.subtract)
                dve.tensor_copy(shc[:, 0, :], pB[:, :, SEQ - 1])
                done(dve.tensor_copy(shc[:, 1:9, :].rearrange("p b k -> p k b"), sam(pB)[:, :, :, TS - 1]), "shc")
                shifted = lambda k: stt(xm[:, k], xm[:, k], par[:, MU + k:MU + k + 1], pB[:, k], ALU.mult, ALU.add)
                for k in (12, 13, 4, 5, 6, 7):
                    a = shifted(k)
                    if k == 13:
                        a.then_inc(sem["xl"], 1)
                done(a, "xm")
                take("sht")
                done(dve.tensor_copy(shr[:], PS[0:126, 2, 0:P]), "shrc")
                take("th", 2)
                done(ts(sg13[:], sg13[:], 0.5, 0.5, ALU.mult, ALU.add), "sg")
                for k in range(4):
                    a = shifted(k)
                done(a, "xrs")
                xr, xk, xv = xm[:, 0:4], xm[:, 4:8], xm[:, 8:12]
                col = lambda r, f: par[:, r + f:r + f + 1]
                take("zexp")
                done(ts(lw[:], e1[:], 1.0, None, ALU.add))
                take("keep")
                for f in range(4):
                    a = dve.tensor_tensor_scan(cl[:, f], keep[:], lw[:, f], 0.0, ALU.mult, ALU.add)
                done(a, "cl")
                take("aexp")
                done(ts(aa[:], e2[:], 0.5, 0.5, ALU.mult, ALU.add))
                take("kf")
                done(tt(e2[:], dR[:], xk, ALU.mult))
                for f in range(4):
                    a = stt(e1[:, f], xr[:, f], col(RK_, f), e2[:, f], ALU.mult, ALU.mult)
                done(a, "rkp")
                take("sd")
                done(ts(th12[:], th12[:], 1e-12, None, ALU.max))
                done(dve.reciprocal(th12[:], th12[:]), "rn")
                take("rks")
                for f in range(4):
                    a = stt(kk[:, f], xk[:, f], col(KK, f), PS[:, 4 + f, 0:TOK], ALU.mult, ALU.mult)
                done(a)
                done(tt(dB[:], kk[:], aa[:], ALU.mult))
                take("expd")
                tt(dA[:], dA[:], kk[:], ALU.mult)
                done(tt(dB[:], dB[:], dK[:], ALU.mult))
                done(tt(dK[:], dK[:], e2[:], ALU.mult), "abkr")
                take("rk2")
                take("xs")
                done(tt(xk, PS[:, 0:4, 0:TOK], xv, ALU.mult), "bon")
                take("drr")
                dve.wait_ge(sem["zero"], 2 * l + 2)
                for tau in range(3):
                    c0, nt = tau * P, P if tau < 2 else NS
                    kind = "P" if tau < 2 else "S"
                    for x, y in ((dA, eA), (dB, eB), (dR, eR)):
                        for h2, rows in enumerate(halves()):
                            a = dve.tensor_copy(y[rows, :, h2, 0:nt], x[rows, :, c0:c0 + nt])
                    done(a, "exd")
                    take("G")
                    take("Gc")
                    done(tt(heads(WT, nt), heads(MT, nt), mask("negE1T", nt), ALU.mult))
                    done(tt(heads(WT, nt), heads(WT, nt), mask("ident", nt), ALU.add))
                    take("G")
                    done(tt(heads(TT, nt), banks(6, nt), mask("negE1", nt), ALU.mult))
                    done(tt(heads(TT, nt), heads(TT, nt), mask("ident", nt), ALU.add), "E1")
                    take("G")
                    tt(heads(NTm, nt), banks(0, nt), mask("strict" + kind, nt), ALU.mult).then_inc(sem["NT"], 1)
                    take("G")
                    tt(heads(RBm, nt), banks(2, nt), mask("incl" + kind, nt), ALU.mult).then_inc(sem["RB"], 1)
                    take("G")
                    done(tt(heads(RKm, nt), banks(4, nt), mask("incl" + kind, nt), ALU.mult))
                    levels = LEVELS if tau < 2 else LEVELS[:2]
                    quad = lambda x, hf: x[0:nt, hf * 4 * nt:(hf + 1) * 4 * nt].rearrange("p (h t) -> p h t", h=4)
                    qbank = lambda b, hf: PS[0:nt, b + hf, 0:4 * nt].rearrange("p (h t) -> p h t", h=4)

                    def corner(size, hf):
                        m = C(f"lev{size}", nt, nt).unsqueeze(1).broadcast_to([nt, 4, nt])
                        done(tt(quad(ET, hf), quad(MT, hf), m, ALU.mult), "et")
                    for i, size in enumerate(levels):
                        last = i == len(levels) - 1
                        if not last:
                            for hf in range(2):
                                zs[0] += 1
                                dve.wait_ge(sem["Z"], zs[0])
                                corner(levels[i + 1], hf)
                        else:
                            zs[0] += 2
                        for hf in range(2):
                            if not last:
                                take("TZ")
                                done(tt(quad(TT, hf), quad(TT, hf), qbank(0, hf), ALU.subtract), "TT")
                            take("WZ")
                            done(tt(quad(WT, hf), quad(WT, hf), qbank(2, hf), ALU.subtract), "TW")
                    take("NV")
                    done(dve.tensor_copy(nvs[0:nt, :], PS[0:nt, 5, :]), "NVc")
                    take("TNV")
                    done(dve.tensor_copy(tnv[0:nt, :], PS[0:nt, 6, :]), "tnv")
                    for c in range(2) if tau < 2 else range(1):
                        r = slice(c * HD, c * HD + HD)
                        if tau < 2:
                            take("U")
                        else:
                            dve.wait_ge(sem["TAc"], 3 * (l + 1))
                            take("mz")
                            for f in range(4):
                                if f >= 2:
                                    dve.wait_ge(sem["U1"], 4 * l + f - 1)
                                dve.tensor_copy(mkd[f % 2][0][:, :, 0:TS], tat[:, f * NS:(f + 1) * NS].rearrange("p (b t) -> p b t", b=NB))
                                done(dve.tensor_copy(mkd[f % 2][1][:, :, 0:TS], dR[:, f, SEQ:TOK].rearrange("p (b t) -> p b t", b=NB)), "mk")
                                if f:
                                    rotated(5 + f)
                            take("U1", 4)
                        done(stt(uu[r, :], PS[r, 7, :], -1.0, tnv[r, :], ALU.mult, ALU.subtract), "Uc")
                        if tau < 2:
                            if c:
                                rotated(3 * tau + 1)
                            rotated(3 * tau + 2 * c)
                            take("Sm")
                            ps = PS[:, 1, :].rearrange("p (f i) -> p f i", f=4)
                            done(tt(S0P[:], S0P[:], ps, ALU.add))
                            ch = 2 * tau + c
                            for f in range(4):
                                a = stt(S0P[:, f], S0P[:, f], pc[:, f, ch:ch + 1], C("headones"), ALU.mult, ALU.mult)
                            done(a, "SP")
                    take("Y")
                    if tau == 0:
                        dve.wait_ge(sem["out"], 16 * 12 * l + 32)
                    done(dve.tensor_copy(yy[:, :, c0:c0 + nt], PS[:, 0, 0:4 * nt].rearrange("p (f t) -> p f t", f=4)), "Yc")
                own = C("own", NS).unsqueeze(2).broadcast_to([NS, NB, HD])

                def expand(f):
                    for h2 in range(2):
                        cols = slice((2 * f + h2) * HD, (2 * f + h2 + 1) * HD)
                        a = tt(ux[f % 2][:, h2], uu[0:NS, cols].unsqueeze(1).broadcast_to([NS, NB, HD]), own, ALU.mult)
                    done(a, "ux")
                expand(0)
                take("gn")
                done(stt(yy[:], PS[:, 0:4, 0:TOK], -1.0 / HD, yy[:], ALU.mult, ALU.add), "gnc")
                expand(1)
                for f in range(4):
                    take("Se")
                    for h2, rows in enumerate(halves()):
                        tmp = stmp[rows, :].rearrange("p (b i) -> p b i", b=NB)
                        s0 = S0T[rows, :, f, h2 * HD:h2 * HD + HD]
                        done(tt(tmp, s0, PS[rows, 4 + f % 2, :].rearrange("p (b i) -> p b i", b=NB), ALU.add))
                        a = tt(s0, tmp, pc[rows, f, 4:12].unsqueeze(2).broadcast_to([HD, NB, HD]), ALU.mult)
                    done(a, "SF")
                    if f < 2:
                        expand(f + 2)
                take("gsd")
                done(dve.reciprocal(dB[:, 0], dB[:, 0]), "rn")
                take("grn")
                for f in range(4):
                    a = stt(yy[:, f], yy[:, f], col(LNW, f), PS[:, f, 0:TOK], ALU.mult, ALU.mult)
                done(a)
                take("bl")
                done(tt(yy[:], yy[:], xk, ALU.add))
                done(tt(pT[:, BR:BR + 4], yy[:], gg[:], ALU.mult), "rw")

            def attention(l):
                for u in range(24 + 1):
                    if u < 24:
                        take("S")
                        x = psm[u % 3]
                        if u >= 3:
                            dve.wait_ge(sem["PT"], 24 * l + u - 2)
                        done(stt(x[:], PS[:, u % 2, 0:384], SCALE, C("maskA" if u < 8 else "maskC"), ALU.mult, ALU.add), "sm")
                        dve.tensor_reduce(nm[u % 3][:, 0:1], x[:, 0:P], AX_X, ALU.max, negate=True)
                        done(dve.tensor_reduce(nm[u % 3][:, 1:2], x[:, P:384], AX_X, ALU.max, negate=True), "nmx")
                    if u >= 1:
                        v = u - 1
                        take("pex")
                        if v >= 8:
                            done(tt(sums[v % 3][:], sums[v % 3][:], psk[v % 3][:], ALU.add))
                        done(dve.reciprocal(sums[v % 3][:], sums[v % 3][:]))
                        y = psm[v % 3]
                        ts(y[:, 0:P], y[:, 0:P], sums[v % 3][:, 0:1], None, ALU.mult)
                        done(ts(y[:, P:384], y[:, P:384], sums[v % 3][:, 1:2], None, ALU.mult), "pn")
                dve.wait_ge(sem["PT"], 24 * (l + 1))
                dve.wait_ge(sem["O"], 24 * (l + 1))

                def scores(q):
                    x, y, i = smA[q % 2], smC[q % 2], q % 2
                    take("bS")
                    if q >= 2:
                        dve.wait_ge(sem["pt2"], 4 * (4 * l + q - 1))
                    for k in range(3):
                        n = 512 if k < 2 else 256
                        stt(x[:, 512 * k:512 * k + n], PS[:, k, 0:n], SCALE, C("oldA")[:, 512 * k:512 * k + n], ALU.mult, ALU.add)
                    stt(x[:, 1280:1344], PS[:, 2, 256:320], SCALE, C("newA")[:, 64 * q:64 * q + 64], ALU.mult, ALU.add)
                    ps = PS[:, 3, 0:384].rearrange("p (b k) -> p b k", b=2)
                    stt(y[:, :, 0:P], ps[:, :, 0:P], SCALE, C("oldC").unsqueeze(1).broadcast_to([P, 2, P]), ALU.mult, ALU.add)
                    done(stt(y[:, :, P:192], ps[:, :, P:192], SCALE, C("newC")[:, 128 * q:128 * q + 128].rearrange("p (b k) -> p b k", b=2), ALU.mult, ALU.add), "smb")
                    dve.tensor_reduce(snm[i][:, 0:1], x[:], AX_X, ALU.max, negate=True)
                    done(dve.tensor_reduce(snm[i][:, 1:3], y[:], AX_X, ALU.max, negate=True), "bnm")

                def weighted(q):
                    i = q % 2
                    take("bex")
                    done(tt(ssu[i][:, 1:3], ssu[i][:, 1:3], ssk[i][:], ALU.add))
                    done(dve.reciprocal(ssu[i][:], ssu[i][:]))
                    take("pv1", 2)
                    v3 = lambda z: z.rearrange("p (h d) -> p h d", h=8)
                    stt(v3(om[:]), v3(PS[:, 6, :]), ssu[i][:, 0:1], C("headof").unsqueeze(2).broadcast_to([P, 8, HD]), ALU.mult, ALU.mult)
                    for b2 in range(2):
                        a = stt(omC[:, b2], PS[:, 7, b2 * P:(b2 + 1) * P], ssu[i][:, 1 + b2:2 + b2], C("headones"), ALU.mult, ALU.mult)
                    done(a, "om")

                def outputs(q):
                    take("sel")
                    o = SEQ + 2 * TS * q
                    dve.tensor_copy(pT[:, QA:QA + 4, o:o + 2 * TS], PS[:, 7, 256:320].rearrange("p (f t) -> p f t", f=4))
                    for b2 in range(2):
                        a = dve.tensor_copy(pT[:, QC:QC + 8, o + b2 * TS:o + b2 * TS + TS],
                                            PS[:, 7, 320 + 64 * b2:384 + 64 * b2].rearrange("p (i t) -> p i t", i=8))
                    done(a, "bo")
                scores(0)
                for q in range(NB // 2):
                    if q:
                        outputs(q - 1)
                    if q < NB // 2 - 1:
                        scores(q + 1)
                    weighted(q)
                dve.wait_ge(sem["oc"], 24 * (l + 1))
                take("hh", 4)
                for g, t0 in enumerate((QA, BR)):
                    tt(hl[:, 4 * g:4 * g + 4, 0:SEQ], pT[:, t0:t0 + 4, 0:SEQ], hh[:, 4 * g:4 * g + 4, 0:SEQ].bitcast(F32), ALU.subtract)
                outputs(NB // 2 - 1)
                split(start_of(l, "out"), 0, KT)
                for g, t0 in enumerate((QA, BR, QC, QC + 4)):
                    take("hh")
                    done(tt(hl[:, 4 * g:4 * g + 4, SEQ:TOK], pT[:, t0:t0 + 4, SEQ:TOK], hh[:, 4 * g:4 * g + 4, SEQ:TOK].bitcast(F32), ALU.subtract), "mix")

            dve.wait_ge(sem["con2"], 16)
            for l in range(DEPTH):
                take("part")
                dve.tensor_copy(par[:], PS[:, 6, 0:N_PAR])
                done(dve.tensor_copy(shf[:].rearrange("p b k -> p (b k)"), PS[:, 7, 0:NB * 14]))
                ts(npar[:], par[:, W0:W0 + 8], 0.5, None, ALU.mult)
                ts(kap[:, 0:4], par[:, KA_:KA_ + 4], 0.5, None, ALU.mult)
                done(ts(kap[:, 4:8], par[:, KA_:KA_ + 4], -0.5, 1.0, ALU.mult, ALU.add), "parc")
                if l == 0:
                    dve.wait_ge(sem["xtc"], 12)
                norm(G_MIX, 2 * l)
                stream(l, "in", ahead=(l, "inq"))
                stream(l, "inq", ready=True, ahead=(l, "inkv"))
                stream(l, "inkv", ready=True)
                rwkv(l)
                attention(l)
                stream(l, "out", ready=True, ahead=(l, *FFN[0]))
                norm(G_FFN, 2 * l + 1)
                for i, (kind, c) in enumerate(FFN):
                    stream(l, kind, c, ready=True, ahead=(l, *FFN[i + 1]) if i + 1 < len(FFN) else None)
            rms()
            for g in range(4):
                for k in range(4 * g, 4 * g + 4):
                    a = stt(xT[:, k], xT[:, k], par[:, G_FIN + k:G_FIN + k + 1], rsb[:], ALU.mult, ALU.mult)
                done(a, "ht")
            for q in range(0, 12, 2):
                dve.wait_ge(sem["fint"], q + 1)
                g, tau = divmod(q, 3)
                nt = P if tau < 2 else NS
                dve.tensor_copy(yout[tau][0:nt, g * 512:(g + 1) * 512], PS[0:nt, q % 4, :]).then_inc(sem["finc"], 1)

        @block.tensor
        def _(pe):
            want = Tally()

            def take(name, by=1):
                pe.wait_ge(sem[name], want(sem[name], by))

            rots = [0]
            mm = lambda out, lhsT, rhs, start=True, stop=True: pe.matmul(out, lhsT, rhs, start=start, stop=stop, skip_group_check=True)
            tr = lambda out, x: pe.transpose(out, x, con[0:x.shape[0], at["ident"][0]:at["ident"][0] + x.shape[0]])

            def stream(l, kind, c=0, inputs=0):
                _, _, _, n0, blocks, kts, nd = seg(l, kind, c)
                xh, xl = (ah[c % 2], al[c % 2]) if kind == "down" else (hh, hl)

                def pair(i, first):
                    for j in range(2):
                        pe.wait_ge(sem["wl"], 2 * i + (n0 + j + 1))
                        if not (first and n0 == 0):
                            pe.wait_ge(sem["ev"], 2 * i + (n0 + j - 1))
                        for k in range(kts):
                            if first and j == 0 and k % 4 == 0 and kind in ("in", "gu") and c == 0:
                                g = k // 4
                                pe.wait_ge(sem["hl" if g in (0, 3) else "hlp"], inputs + (1, 1, 2, 2)[g])
                            mm(PS[:, j, 0:TOK], wh[j][:, k], xh[:, k], k == 0, False)
                            mm(PS[:, j, 0:TOK], wh[j][:, k], xl[:, k], False, False)
                            a = mm(PS[:, j, 0:TOK], wl[j][:, k], xh[:, k], False, k == kts - 1)
                        a.then_inc(sem["mm"], 1)
                pair(0, True)
                if blocks > 2:
                    with pe.Fori(1, blocks // 2) as i:
                        pair(i, False)

            def token_sums(n):
                if n == 0:
                    pe.wait_ge(sem["con2"], 16)
                    for g in range(4):
                        take("ssum")
                        a = mm(PS[:, 2, 0:TOK], C("ones"), ht[0][:, g], g == 0, g == 3)
                else:
                    pe.wait_ge(sem["ssd"], KT * n)
                    a = mm(PS[:, 2, 0:TOK], C("ones"), ssum[:])
                a.then_inc(sem["nmm"], 1)

            def bank2(b, h, nt):
                return PS[0:nt, b + h // 4, (h % 4) * nt:(h % 4 + 1) * nt]

            def head(x, h, nt):
                return x[0:nt, h * nt:(h + 1) * nt]

            def rotate(u):
                if u % 9 >= 2:
                    pe.wait_ge(sem["rotc"], rots[0] - 1)
                for i, tile in enumerate(range(ROTATED[u].start, ROTATED[u].stop)):
                    a = mm(PS[:, (2, 5)[u % 2] + i, 0:TOK], C("rot"), pT[:, tile])
                a.then_inc(sem["rot"], 1)
                rots[0] += 1

            def rwkv(l):
                take("shc")
                tr(PS[0:126, 2, 0:P], shc[:].rearrange("p b k -> p (b k)")).then_inc(sem["sht"], 1)
                pe.wait_ge(sem["lora"], 64 * (l + 1))
                take("shrc")
                take("sg")
                for f in range(4):
                    a = mm(PS[:, f, 0:TOK], lora[0][:, f * P:(f + 1) * P], th12[:])
                a.then_inc(sem["z"], 1)
                for f in range(4):
                    mm(PS[:, 4 + f, 0:TOK], lora[1][:, f * P:(f + 1) * P], xm[:, 12], True, False)
                    a = mm(PS[:, 4 + f, 0:TOK], lora[2][:, f * P:(f + 1) * P], xm[:, 13], False, True)
                a.then_inc(sem["aa"], 1)
                take("zexp")
                for f in range(4):
                    a = mm(PS[:, f, 0:TOK], lora[3][:, f * P:(f + 1) * P], sg13[:])
                a.then_inc(sem["g"], 1)

                def few_sums(x, b, name):
                    for f in range(4):
                        a = mm(PS[32 * f:32 * f + 32, b, 0:TOK], C("headones")[:, HD - 16:HD + 16], x[:, f])
                    a.then_inc(sem[name], 1)

                def spread(x, b0, name):
                    for f in range(4):
                        r = slice(32 * f, 32 * f + 32)
                        a = mm(PS[:, b0 + f, 0:TOK], C("spread")[r], x[r])
                    a.then_inc(sem[name], 1)

                def head_sums(x, b0, name):
                    for f in range(4):
                        a = mm(PS[:, b0 + f, 0:TOK], C("headones"), x[:, f])
                    a.then_inc(sem[name], 1)
                take("ksq")
                take("aexp")
                few_sums(dB, 4, "kss")
                take("rn")
                spread(th12, 4, "rks")
                take("rkp")
                take("gc")
                head_sums(e1, 0, "rk2")
                take("abkr")
                pe.wait_ge(sem["s0"], 16 * 16 * (l + 1))
                for r in range(8):
                    if r >= 4:
                        pe.wait_ge(sem["stc"], 8 * l + r - 3)
                    for f in range(4):
                        a = tr(PS[:, 4 + r % 4, f * P:(f + 1) * P], S0in[:, r, f])
                    a.then_inc(sem["st"], 1)
                take("bon")
                pe.wait_ge(sem["stc"], 8 * l + 8)
                for tau in range(3):
                    c0, nt = tau * P, P if tau < 2 else NS
                    cols = slice(c0, c0 + nt)
                    for q, x in enumerate((xm[:, 8:12], dA, dB, dK)):
                        for f in range(4):
                            a = tr(PS[0:nt, q, f * P:(f + 1) * P], x[:, f, cols])
                        a.then_inc(sem["tok"], 1)
                    take("exd")
                    def gram(b, x, y):
                        for f in range(4):
                            a = mm(PS[0:nt, b + f // 2, (f % 2) * 2 * nt:(f % 2 + 1) * 2 * nt], x[:, f, cols],
                                   y[:, f, :, 0:nt])
                        a.then_inc(sem["G"], 1)
                    gram(4, dB, eA)
                    gram(6, dA, eB)
                    take("tokc", 4)
                    gram(0, dK, eA)
                    gram(2, dB, eR)
                    take("Gc")
                    gram(4, dK, eR)
                    levels = LEVELS if tau < 2 else LEVELS[:2]
                    for i, size in enumerate(levels):
                        for hf in range(2):
                            if i:
                                take("et")
                                take("TT")
                            else:
                                take("et0")
                                if not hf:
                                    take("E1")
                            for h in range(4 * hf, 4 * hf + 4):
                                a = mm(bank2(6, h, nt), head(ET, h, nt), head(TT, h, nt))
                            a.then_inc(sem["Z"], 1)
                        for hf in range(2):
                            take("Zc")
                            if i:
                                take("TW")
                            if not i and not hf:
                                take("NT")
                                take("RB")
                            if size != levels[-1]:
                                for h in range(4 * hf, 4 * hf + 4):
                                    a = mm(bank2(0, h, nt), head(WT, h, nt), head(ZZ, h, nt))
                                a.then_inc(sem["TZ"], 1)
                            for h in range(4 * hf, 4 * hf + 4):
                                a = mm(bank2(2, h, nt), head(ZZ, h, nt), head(WT, h, nt))
                            a.then_inc(sem["WZ"], 1)
                    take("TW", 2)
                    for h in range(8):
                        r = slice(h % 2 * HD, h % 2 * HD + HD)
                        a = mm(PS[r, 4, (h // 2) * nt:(h // 2 + 1) * nt], at_[0:nt, h * HD:(h + 1) * HD], head(WT, h, nt))
                    a.then_inc(sem["TA"], 1)
                    for h in range(8):
                        a = mm(PS[0:nt, 5, h * HD:(h + 1) * HD], head(NTm, h, nt), vt[0:nt, h * HD:(h + 1) * HD])
                    a.then_inc(sem["NV"], 1)
                    take("NVc")
                    for h in range(8):
                        a = mm(PS[0:nt, 6, h * HD:(h + 1) * HD], head(WT, h, nt), nvs[0:nt, h * HD:(h + 1) * HD])
                    a.then_inc(sem["TNV"], 1)
                    take("TAc")
                    take("tnv")
                    ybank = lambda f, a0, a1: PS[:, 0, f * nt + a0:f * nt + a1]
                    if tau < 2:
                        for c in range(2):
                            r = slice(c * HD, c * HD + HD)
                            if tau or c:
                                take("SP")
                            for f in range(4):
                                a = mm(PS[r, 7, f * P:(f + 1) * P], tat[:, f * P + c * HD:f * P + c * HD + HD], S0P[:, f])
                            a.then_inc(sem["U"], 1)
                            for f in range(4):
                                mm(ybank(f, c * HD, c * HD + HD), S0P[:, f], dR[:, f, c0 + c * HD:c0 + c * HD + HD], c == 0 and f == 0, False)
                            rotate(3 * tau + 2 * c)
                            take("Uc")
                            for f in range(4):
                                fc = slice(f * P, (f + 1) * P)
                                mm(PS[:, 1, fc], bt[r, fc], uu[r, fc], True, False)
                                a = mm(PS[:, 1, fc], kt_[r, fc], vt[r, fc], False, True)
                            a.then_inc(sem["Sm"], 1)
                            if c == 0:
                                rotate(3 * tau + 1)
                        if tau == 1:
                            take("SP")
                    else:
                        for f in range(4):
                            take("mk")
                            for b in range(NB):
                                a = mm(PS[:, 7, f * P:(f + 1) * P], mk[f % 2][:, b], S0T[:, b, f], b == 0, b == NB - 1)
                            a.then_inc(sem["U1"], 1)
                            if f < 3:
                                rotate(6 + f)
                        take("U1c")
                        for f in range(4):
                            mm(ybank(f, 0, NS), nvs[NS:2 * NS, f * P:(f + 1) * P], ident[NS:2 * NS, NS:2 * NS], f == 0, False)
                        take("Uc")
                    for h in range(8):
                        out = PS[h % 2 * HD:h % 2 * HD + HD, 0, (h // 2) * nt:(h // 2 + 1) * nt]
                        mm(out, uu[0:nt, h * HD:(h + 1) * HD], head(RBm, h, nt), False, False)
                        a = mm(out, vt[0:nt, h * HD:(h + 1) * HD], head(RKm, h, nt), False, True)
                    a.then_inc(sem["Y"], 1)
                    take("Yc")
                head_sums(yy, 0, "gn")
                for f in range(4):
                    take("ux")
                    take("vx")
                    for h2 in range(2):
                        hc = slice((2 * f + h2) * HD, (2 * f + h2 + 1) * HD)
                        out = PS[h2 * HD:h2 * HD + HD, 4 + f % 2, :]
                        mm(out, bt[0:NS, hc], ux[f % 2][:, h2].rearrange("p b i -> p (b i)"), True, False)
                        a = mm(out, kt_[0:NS, hc], vx[f % 2][:, h2].rearrange("p b i -> p (b i)"), False, True)
                    a.then_inc(sem["Se"], 1)
                    if f == 1:
                        take("ysq")
                        few_sums(dA, 0, "gv")
                take("SF", 4)
                for r in range(9):
                    if r >= 4:
                        pe.wait_ge(sem["Soc"], 9 * l + r - 3)
                    for f in range(4):
                        a = tr(PS[:, 4 + r % 4, f * P:(f + 1) * P], S0T[:, r, f] if r < 8 else S0P[:, f])
                    a.then_inc(sem["So"], 1)
                    if r == 3:
                        take("rn")
                        spread(dB[:, 0], 0, "grn")

            def attention(l):
                take("rope", 9)
                pe.wait_ge(sem["Soc"], 9 * (l + 1))
                for q in range(9):
                    if q >= 4:
                        pe.wait_ge(sem["kvc"], 9 * l + q - 3)
                    t0, nt = q // 3 * P, P if q < 6 else NS
                    for i, tile in enumerate([range(KA, KA + 4), range(VA, VA + 4), (KC, VC)][q % 3]):
                        a = tr(PS[0:nt, 4 + q % 4, i * P:(i + 1) * P], pT[:, tile, t0:t0 + nt])
                    a.then_inc(sem["kv"], 1)
                pe.wait_ge(sem["kvc"], 9 * l + 9)
                take("rw")
                for u in range(24 + 3):
                    if u < 24:
                        qt, kt = (QA + u // 2, KA + u // 2) if u < 8 else (QC + (u - 8) // 2, KC)
                        rows = slice(u % 2 * HD, u % 2 * HD + HD)
                        if u >= 2:
                            pe.wait_ge(sem["sm"], 24 * l + u - 1)
                        mm(PS[:, u % 2, 0:P], pT[rows, qt, 0:P], pT[rows, kt, 0:P])
                        mm(PS[:, u % 2, P:384], pT[rows, qt, P:SEQ], pT[rows, kt, 0:SEQ]).then_inc(sem["S"], 1)
                    if 2 <= u < 26:
                        v = u - 2
                        if v >= 2:
                            pe.wait_ge(sem["ptc"], 24 * l + v - 1)
                        take("pn")
                        x = psm[v % 3]
                        for i in range(3):
                            a = tr(PS[:, 2 + v % 2, i * P:(i + 1) * P], x[:, i * P:(i + 1) * P])
                        a.then_inc(sem["PT"], 1)
                    if u >= 3:
                        v = u - 3
                        r = slice(v % 2 * HD, v % 2 * HD + HD)
                        vals = tk[1][:, :, (v * HD):(v + 1) * HD] if v < 8 else tk[2][:, :, P + v % 2 * HD:P + (v % 2 + 1) * HD]
                        pe.wait_ge(sem["ptc"], 24 * l + v + 1)
                        if v >= 2:
                            pe.wait_ge(sem["oc"], 24 * l + v - 1)
                        mm(PS[r, 4 + v % 2, 0:SEQ], vals[:, 0, :], ppt[v % 2][:, 0:SEQ], True, False)
                        mm(PS[r, 4 + v % 2, P:SEQ], vals[:, 1, :], ppt[v % 2][:, SEQ:384], False, True).then_inc(sem["O"], 1)
                pe.wait_ge(sem["oc"], 24 * (l + 1))

                def keys(q):
                    take("qbd")
                    if q:
                        pe.wait_ge(sem["smb"], 4 * l + q)
                    steps = [(b, m) for b in (2 * q, 2 * q + 1) for m in range(13)]

                    def turn(b, m):
                        g, b2 = 13 * (NB * l + b) + m, b % 2
                        if m == 0:
                            pe.wait_ge(sem[f"cK{b2}"], 16 * CACHE_DMAS * (NB // 2 * l + q + 1))
                        bank = PS[:, 4 + g % 2, :]
                        if m >= 2 or b:
                            pe.wait_ge(sem["ktc"], g - 1)
                        if m < 12:
                            f, (k0, n) = m % 4, QUADS[m // 4]
                            for k in range(n):
                                a = tr(bank[:, k * P:(k + 1) * P], cK[b2][:, k0 + k, f * P:(f + 1) * P])
                        else:
                            a = tr(bank[:, 0:P], ckc[b2][:])
                        a.then_inc(sem["ktp"], 1)

                    def score(b, m):
                        g, b2 = 13 * (NB * l + b) + m, b % 2
                        pe.wait_ge(sem["ktc"], g + 1)
                        if m < 12:
                            f, n = m % 4, QUADS[m // 4][1] * P
                            a = mm(PS[b2 * 64:b2 * 64 + 64, m // 4, 0:n], qdA[q % 2][:, f, b2], ktr[g % 3][:, 0:n], f == 0, f == 3)
                        else:
                            a = mm(PS[:, 3, b2 * 192:b2 * 192 + P], qdC[q % 2][:, b2].rearrange("p k i t -> p (k i t)"), ktr[g % 3][:, 0:P])
                        a.then_inc(sem["sc"], 1)
                    turn(*steps[0])
                    turn(*steps[1])
                    for i, step in enumerate(steps):
                        if i + 2 < len(steps):
                            turn(*steps[i + 2])
                        if i == len(steps) // 2 and q >= 2:
                            select(q - 2)
                        score(*step)
                    for f in range(4):
                        mm(PS[:, 2, 256:320], qdA[q % 2][:, f].rearrange("p b c -> p (b c)"), pT[:, KA + f, SEQ:TOK], f == 0, f == 3)
                    for b2 in range(2):
                        a = mm(PS[:, 3, b2 * 192 + P:b2 * 192 + 192], qdC[q % 2][:, b2].rearrange("p k i t -> p (k i t)"), pT[:, KC, SEQ:TOK])
                    a.then_inc(sem["bS"], 1)

                def values(q):
                    pe.wait_ge(sem["bex"], 4 * l + q + 1)
                    x, y = smA[q % 2], smC[q % 2]
                    for r in range(4):
                        if r >= 2:
                            pe.wait_ge(sem["ptd"], 4 * (4 * l + q) + r - 1)
                        elif r == 1 and q:
                            pe.wait_ge(sem["bo"], 4 * l + q)
                        bank = PS[:, 6 + r % 2, :].rearrange("p (k c) -> p k c", k=4)
                        if r < 3:
                            for k in range(4 * r, min(4 * r + 4, 11)):
                                n = P if k < 10 else NS
                                a = tr(bank[0:n, k % 4], x[:, k * P:k * P + n])
                        else:
                            for b2 in range(2):
                                tr(bank[:, 2 * b2], y[:, b2, 0:P])
                                a = tr(bank[0:NS, 2 * b2 + 1], y[:, b2, P:192])
                        a.then_inc(sem["pt2"], 1)
                    pe.wait_ge(sem["ptd"], 4 * (4 * l + q) + 4)
                    mm(PS[:, 6, :], ptA[0:NS, 10], tk[1][0:NS, 2, :], True, False)
                    for b2 in range(2):
                        pe.wait_ge(sem[f"cV{b2}"], 16 * CACHE_DMAS * (NB // 2 * l + q + 1))
                        mm(PS[:, 7, b2 * P:(b2 + 1) * P], ptC[:, b2, 0], cvc[b2][:], True, False)
                        mm(PS[:, 7, b2 * P:(b2 + 1) * P], ptC[0:NS, b2, 1], tk[2][0:NS, 2, P:2 * P], False, True)
                        for k in range(10):
                            a = mm(PS[b2 * 64:b2 * 64 + 64, 6, :], ptA[:, k, b2 * 64:b2 * 64 + 64], cV[b2][:, k, :], False, k == 9)
                        a.then_inc(sem["pv1"], 1)

                def select(q):
                    take("om")
                    for f in range(4):
                        mm(PS[:, 7, 256 + 16 * f:272 + 16 * f], om[:, f * P:(f + 1) * P], C("selA"))
                    for b2 in range(2):
                        a = mm(PS[:, 7, 320 + 64 * b2:384 + 64 * b2], omC[:, b2], C("selC"))
                    a.then_inc(sem["sel"], 1)
                keys(0)
                for q in range(NB // 2):
                    if q < NB // 2 - 1:
                        keys(q + 1)
                    elif q:
                        select(q - 1)
                    values(q)
                select(NB // 2 - 1)

            pe.wait_ge(sem["con"], 16)
            pe.wait_ge(sem["x"], 48)
            for q in range(12):
                tau, k0 = q // 4, q % 4 * 4
                nt = P if tau < 2 else NS
                if q >= 4:
                    pe.wait_ge(sem["xtc"], q - 3)
                for k in range(4):
                    a = tr(PS[:, 2 + q % 4, k * nt:(k + 1) * nt], xin[0:nt, tau, (k0 + k) * P:(k0 + k + 1) * P])
                a.then_inc(sem["xtr"], 1)
            pe.wait_ge(sem["xtc"], 12)
            for l in range(DEPTH):
                pe.wait_ge(sem["par"], 16 * 13 * (l + 1))
                tr(PS[:, 6, 0:N_PAR], prow[:])
                tr(PS[:, 7, 0:NB * 14], srow[:]).then_inc(sem["part"], 1)
                token_sums(2 * l)
                stream(l, "in", inputs=4 * l)
                stream(l, "inq")
                stream(l, "inkv")
                pe.wait_ge(sem["ev"], start_of(l, "out"))
                rwkv(l)
                attention(l)
                pe.wait_ge(sem["mix"], 4 * l + 4)
                pe.wait_ge(sem["hpp"], 2 * (l + 1))
                stream(l, "out")
                token_sums(2 * l + 1)
                for i, (kind, c) in enumerate(FFN):
                    if kind == "down":
                        pe.wait_ge(sem["act"], 5 * FC * (l * NCH + c + 1))
                    stream(l, kind, c, inputs=0 if i else 4 * l + 2)
            token_sums(2 * DEPTH)
            for q in range(12):
                g, tau = divmod(q, 3)
                nt = P if tau < 2 else NS
                pe.wait_ge(sem["ht"], 8 * DEPTH + g + 1)
                if q >= 4:
                    pe.wait_ge(sem["fina" if q % 2 else "finc"], q // 2 - 1)
                for k in range(4):
                    a = tr(PS[0:nt, q % 4, k * P:(k + 1) * P], xT[:, 4 * g + k, tau * P:tau * P + nt])
                a.then_inc(sem["fint"], 1)


_OUTS = [
    ("y_prompt", (1, SEQ, D)), ("y_sample", (NB, TS, D)),
    ("new_a_k_prompt", (DEPTH, 1, SEQ, 8, HD)), ("new_a_v_prompt", (DEPTH, 1, SEQ, 8, HD)),
    ("new_c_k_prompt", (DEPTH, 1, P, 2, HD)), ("new_c_v_prompt", (DEPTH, 1, P, 2, HD)),
    ("new_wkv_prompt", (DEPTH, 1, 8, HD, HD)), ("new_shift_prompt", (DEPTH, 1, B_COLS)),
    ("new_a_k_sample", (DEPTH, NB, TS, 8, HD)), ("new_a_v_sample", (DEPTH, NB, TS, 8, HD)),
    ("new_c_k_sample", (DEPTH, NB, TS, 2, HD)), ("new_c_v_sample", (DEPTH, NB, TS, 2, HD)),
    ("new_wkv_sample", (DEPTH, NB, 8, HD, HD)), ("new_shift_sample", (DEPTH, NB, B_COLS)),
]


def kernel(**inputs):
    import concourse.bacc as bacc
    from concourse.bass_utils import run_bass_kernel_spmd

    nc = bacc.Bacc("TRN2", target_bir_lowering=False, num_devices=1)
    con, at = constants()
    arrays = {"in_con": con}
    handles = {"con": nc.dram_tensor("in_con", con.shape, F32, kind="ExternalInput").ap()}
    for name, a in inputs.items():
        a = np.ascontiguousarray(a)
        arrays[f"in_{name}"] = a
        handles[name] = nc.dram_tensor(f"in_{name}", a.shape, mybir.dt.from_np(a.dtype), kind="ExternalInput").ap()
    outs = {n: nc.dram_tensor(f"out_{n}", s, F32, kind="ExternalOutput").ap() for n, s in _OUTS}
    build(nc, handles, outs, at)
    r = run_bass_kernel_spmd(nc, [arrays], core_ids=[0])
    return tuple(r.results[0][f"out_{n}"] for n, _ in _OUTS)
```
